# Optimizing a Trainium2 kernel written in Bass

```python
import math
import jax
import jax.numpy as jnp
from jax import lax
import numpy as np

D_MODEL = 1024
BATCH = 1
SEQ = 256
DEPTH = 4
DEC_BATCH = 8
DEC_SEQ = 1
PAST_LEN = 1024
PAGE_SIZE = 128

N_MIXERS = 3
N_A = (DEPTH + 2) // 3
N_B = (DEPTH + 1) // 3
N_C = DEPTH // 3
EPS = 1e-6
F32 = jnp.float32

M_DINNER = 2 * D_MODEL
M_HEADDIM = 64
M_HEADS = M_DINNER // M_HEADDIM
M_GROUPS = 4
M_DSTATE = 128
M_CONV = 4
M_GN = M_GROUPS * M_DSTATE
M_CONV_DIM = M_DINNER + 2 * M_GN
M_PROJ = M_DINNER + M_CONV_DIM + M_HEADS
M_CHUNK = 128

N_HEADS = 16
HEAD_DIM = D_MODEL // N_HEADS
KV_HEADS = 4
HPG = N_HEADS // KV_HEADS
KV_DIM = KV_HEADS * HEAD_DIM
CMP_BLOCK = 32
CMP_STRIDE = 16
SEL_BLOCK = 64
SEL_TOPK = 16
WINDOW = 512
SEL_QBLK = 32
WIN_QBLK = 128
NSA_PROJ = N_HEADS * HEAD_DIM + 6 * KV_DIM + 3 * N_HEADS
SCALE = HEAD_DIM ** -0.5
REL_BUCKETS = 32
REL_MAX_DIST = 128

H_DK = 128
H_HEADS = D_MODEL // H_DK
H_DV = D_MODEL // H_HEADS
H_CHUNK = 32

MOE_GROUPS = 4
MOE_EPG = 4
MOE_EXPERTS = MOE_GROUPS * MOE_EPG
MOE_TOPK = 2
MOE_FF = 512

kernel_name = 'hybrid_ssd_nsa_hgrn2_hmoe_step'

def rmsnorm(x, g):
    xf = x.astype(F32)
    y = xf * lax.rsqrt(jnp.mean(xf * xf, axis=-1, keepdims=True) + EPS)
    return (y * g.astype(F32)).astype(x.dtype)

def causal_dwconv(u, buf, w, b):
    L = u.shape[1]
    ext = jnp.concatenate([buf.astype(u.dtype), u], axis=1)
    out = b + sum(ext[:, k:k + L] * w[k] for k in range(M_CONV))
    return out, ext[:, L:]

def ssd_scan(x, dt, a, bm, cm, h0):
    bsz, L = x.shape[0], x.shape[1]
    q = M_CHUNK if L % M_CHUNK == 0 else L
    nc = L // q
    hpg = M_HEADS // M_GROUPS
    xdt = (x * dt[..., None]).reshape(bsz, nc, q, M_GROUPS, hpg, M_HEADDIM)
    acum = jnp.cumsum((dt * a).reshape(bsz, nc, q, M_GROUPS, hpg), axis=2)
    bc = bm.reshape(bsz, nc, q, M_GROUPS, M_DSTATE)
    cc = cm.reshape(bsz, nc, q, M_GROUPS, M_DSTATE)
    tri = jnp.tril(jnp.ones((q, q), bool))[:, :, None, None]
    seg = acum[:, :, :, None] - acum[:, :, None]
    decay = jnp.exp(jnp.where(tri, seg, -jnp.inf))
    cb = jnp.einsum('bclgn,bcsgn->bclsg', cc, bc)
    y_diag = jnp.einsum('bclsg,bclsgh,bcsghp->bclghp', cb, decay, xdt)
    decay_end = jnp.exp(acum[:, :, -1:] - acum)
    states = jnp.einsum('bcsgn,bcsgh,bcsghp->bcghpn', bc, decay_end, xdt)
    chunk_decay = jnp.exp(acum[:, :, -1])

    def step(h, inp):
        cd, st = inp
        return cd[..., None, None] * h + st, h

    h_last, h_prev = lax.scan(step, h0.reshape(bsz, M_GROUPS, hpg, M_HEADDIM, M_DSTATE),
                              (chunk_decay.swapaxes(0, 1), states.swapaxes(0, 1)))
    y_off = jnp.einsum('bclgn,bclgh,bcghpn->bclghp', cc, jnp.exp(acum), h_prev.swapaxes(0, 1))
    y = (y_diag + y_off).reshape(bsz, L, M_HEADS, M_HEADDIM)
    return y, h_last.reshape(bsz, M_HEADS, M_HEADDIM, M_DSTATE)

def mamba_mixer(u, conv_buf, h0, w_in, conv_w, conv_b, dt_bias, a_log, d_skip, norm_g, w_out):
    bsz, L, _ = u.shape
    proj = u @ w_in
    z = proj[..., :M_DINNER]
    xbc = proj[..., M_DINNER:M_DINNER + M_CONV_DIM]
    dt_raw = proj[..., M_DINNER + M_CONV_DIM:]
    xbc, new_buf = causal_dwconv(xbc, conv_buf, conv_w, conv_b)
    xbc = jax.nn.silu(xbc)
    xs = xbc[..., :M_DINNER].reshape(bsz, L, M_HEADS, M_HEADDIM).astype(F32)
    bm = xbc[..., M_DINNER:M_DINNER + M_GN].reshape(bsz, L, M_GROUPS, M_DSTATE).astype(F32)
    cm = xbc[..., M_DINNER + M_GN:].reshape(bsz, L, M_GROUPS, M_DSTATE).astype(F32)
    dt = jax.nn.softplus(dt_raw.astype(F32) + dt_bias.astype(F32))
    a = -jnp.exp(a_log.astype(F32))
    y, h = ssd_scan(xs, dt, a, bm, cm, h0.astype(F32))
    y = y + xs * d_skip.astype(F32)[:, None]
    y = y.reshape(bsz, L, M_DINNER).astype(u.dtype)
    y = rmsnorm(y * jax.nn.silu(z), norm_g)
    return y @ w_out, new_buf, h.astype(h0.dtype)

def rel_bucket(dist):
    exact = REL_BUCKETS // 2
    d = jnp.maximum(dist, 0)
    ratio = jnp.log(jnp.maximum(d, 1).astype(F32) / exact) / math.log(REL_MAX_DIST / exact)
    large = jnp.minimum(exact + (ratio * (REL_BUCKETS - exact)).astype(jnp.int32), REL_BUCKETS - 1)
    return jnp.where(d < exact, d, large)

def head_bias(rel_table, dist):
    b = rel_table[rel_bucket(dist)].astype(F32)
    return jnp.moveaxis(b, -1, 0).reshape(KV_HEADS, HPG, dist.shape[0], dist.shape[1])

def masked_softmax(s, valid):
    s = jnp.where(valid, s, -1e30)
    e = jnp.where(valid, jnp.exp(s - jnp.max(s, axis=-1, keepdims=True)), 0.0)
    return e / jnp.maximum(jnp.sum(e, axis=-1, keepdims=True), 1e-30)

def group_attend(qg, qpos, k, v, kpos, valid, rel_table):
    s = jnp.einsum('bqghd,bkgd->bghqk', qg, k).astype(F32) * SCALE
    s = s + head_bias(rel_table, qpos[:, None] - kpos[None, :])
    p = masked_softmax(s, valid)
    o = jnp.einsum('bghqk,bkgd->bqghd', p.astype(v.dtype), v)
    return o, p

def compress(rows, pe, w1, w2):
    bsz, T = rows.shape[0], rows.shape[1]
    nc = (T - CMP_BLOCK) // CMP_STRIDE + 1
    idx = jnp.arange(nc)[:, None] * CMP_STRIDE + jnp.arange(CMP_BLOCK)[None, :]
    blk = rows[:, idx] + pe[:, None, :]
    blk = jnp.moveaxis(blk, 2, 3).reshape(bsz, nc, KV_HEADS, CMP_BLOCK * HEAD_DIM)
    return jax.nn.silu(blk @ w1) @ w2

def select_blocks(p_cmp, qpos, n_sel):
    nc = p_cmp.shape[-1]
    cstart = jnp.arange(nc) * CMP_STRIDE
    sstart = jnp.arange(n_sel) * SEL_BLOCK
    overlap = ((cstart[:, None] < sstart[None, :] + SEL_BLOCK) &
               (cstart[:, None] + CMP_BLOCK > sstart[None, :])).astype(F32)
    imp = jnp.einsum('bghqc,cs->bgqs', p_cmp, overlap)
    qblk = qpos // SEL_BLOCK
    j = jnp.arange(n_sel)
    forced = (j[None, :] == qblk[:, None]) | (j[None, :] == 0)
    score = jnp.where(forced, 1e9, jnp.where(j[None, :] <= qblk[:, None], imp, -1e30))
    _, idx = lax.top_k(score, min(SEL_TOPK, n_sel))
    return idx

def sel_attend(qg, qpos, idx, kblk, vblk, rel_table):
    bsz, lq = qg.shape[0], qg.shape[1]
    bi = jnp.arange(bsz)[:, None, None, None]
    gi = jnp.arange(KV_HEADS)[None, :, None, None]
    kg = kblk[bi, gi, idx]
    vg = vblk[bi, gi, idx]
    s = jnp.einsum('bqghd,bgqkrd->bghqkr', qg, kg).astype(F32) * SCALE
    kpos = idx[..., None] * SEL_BLOCK + jnp.arange(SEL_BLOCK)
    dist = qpos[:, None, None] - kpos
    g5 = jnp.arange(KV_HEADS)[None, :, None, None, None]
    bias = rel_table.reshape(REL_BUCKETS, KV_HEADS, HPG)[rel_bucket(dist), g5].astype(F32)
    s = s + jnp.moveaxis(bias, -1, 2)
    nk = idx.shape[-1]
    valid = (dist >= 0)[:, :, None].reshape(bsz, KV_HEADS, 1, lq, nk * SEL_BLOCK)
    p = masked_softmax(s.reshape(bsz, KV_HEADS, HPG, lq, nk * SEL_BLOCK), valid)
    p = p.reshape(bsz, KV_HEADS, HPG, lq, nk, SEL_BLOCK)
    return jnp.einsum('bghqkr,bgqkrd->bqghd', p.astype(vg.dtype), vg)

def nsa_mixer(u, pos0, kv_cmp_past, kv_sel_past, kv_win_past, n_keep,
              w_in, q_g, k_g, cmp_pe, cmp_w1, cmp_w2, w_out, rel_table):
    bsz, L, _ = u.shape
    sizes = [N_HEADS * HEAD_DIM] + [KV_DIM] * 6 + [3 * N_HEADS]
    q, kc, vc, ks, vs, kw, vw, gl = jnp.split(u @ w_in, np.cumsum(sizes)[:-1].tolist(), axis=-1)
    q = rmsnorm(q.reshape(bsz, L, KV_HEADS, HPG, HEAD_DIM), q_g)

    def kv(t):
        return t.reshape(bsz, L, KV_HEADS, HEAD_DIM)

    new_cmp = jnp.stack([kv(kc), kv(vc)], axis=2)
    new_sel = jnp.stack([rmsnorm(kv(ks), k_g[1]), kv(vs)], axis=2)
    new_win = jnp.stack([rmsnorm(kv(kw), k_g[2]), kv(vw)], axis=2)
    qpos = pos0 + jnp.arange(L)

    crows = jnp.concatenate([kv_cmp_past.astype(u.dtype), new_cmp], axis=1)
    kcmp = rmsnorm(compress(crows[:, :, 0], cmp_pe[0], cmp_w1[0], cmp_w2[0]), k_g[0])
    vcmp = compress(crows[:, :, 1], cmp_pe[1], cmp_w1[1], cmp_w2[1])
    ends = jnp.arange(kcmp.shape[1]) * CMP_STRIDE + CMP_BLOCK - 1
    o_cmp, p_cmp = group_attend(q, qpos, kcmp, vcmp, ends, qpos[:, None] >= ends[None, :], rel_table)

    srows = jnp.concatenate([kv_sel_past.astype(u.dtype), new_sel], axis=1)
    T = srows.shape[1]
    n_sel = -(-T // SEL_BLOCK)
    srows = jnp.pad(srows, ((0, 0), (0, n_sel * SEL_BLOCK - T), (0, 0), (0, 0), (0, 0)))
    blocks = srows.reshape(bsz, n_sel, SEL_BLOCK, 2, KV_HEADS, HEAD_DIM).transpose(3, 0, 4, 1, 2, 5)
    idx = select_blocks(p_cmp, qpos, n_sel)
    qb = SEL_QBLK if L % SEL_QBLK == 0 else L
    nqb = L // qb

    def sel_block(args):
        qgi, qposi, idxi = args
        return sel_attend(qgi, qposi, idxi, blocks[0], blocks[1], rel_table)

    o_sel = lax.map(sel_block, (q.reshape(bsz, nqb, qb, KV_HEADS, HPG, HEAD_DIM).swapaxes(0, 1),
                                qpos.reshape(nqb, qb),
                                idx.reshape(bsz, KV_HEADS, nqb, qb, -1).transpose(2, 0, 1, 3, 4)))
    o_sel = o_sel.swapaxes(0, 1).reshape(bsz, L, KV_HEADS, HPG, HEAD_DIM)

    p_win = kv_win_past.shape[1]
    wrows = jnp.concatenate([kv_win_past.astype(u.dtype), new_win], axis=1)
    wpad = jnp.pad(wrows, ((0, 0), (WINDOW, 0), (0, 0), (0, 0), (0, 0)))
    n_all = WINDOW + p_win + L
    kpos_all = pos0 - p_win - WINDOW + jnp.arange(n_all)
    kvalid_all = jnp.arange(n_all) >= WINDOW
    wq = WIN_QBLK if L % WIN_QBLK == 0 else L

    def win_block(i):
        start = p_win + i * wq
        qgi = lax.dynamic_slice_in_dim(q, i * wq, wq, axis=1)
        kvi = lax.dynamic_slice_in_dim(wpad, start, WINDOW + wq, axis=1)
        kposi = lax.dynamic_slice_in_dim(kpos_all, start, WINDOW + wq)
        kvalidi = lax.dynamic_slice_in_dim(kvalid_all, start, WINDOW + wq)
        qposi = pos0 + i * wq + jnp.arange(wq)
        dist = qposi[:, None] - kposi[None, :]
        valid = kvalidi[None, :] & (dist >= 0) & (dist <= WINDOW)
        o, _ = group_attend(qgi, qposi, kvi[:, :, 0], kvi[:, :, 1], kposi, valid, rel_table)
        return o

    o_win = lax.map(win_block, jnp.arange(L // wq)).swapaxes(0, 1).reshape(bsz, L, KV_HEADS, HPG, HEAD_DIM)

    g = jax.nn.sigmoid(gl.astype(F32)).reshape(bsz, L, KV_HEADS, HPG, 3)
    o = g[..., 0:1] * o_cmp + g[..., 1:2] * o_sel + g[..., 2:3] * o_win
    y = o.astype(u.dtype).reshape(bsz, L, N_HEADS * HEAD_DIM) @ w_out
    return y, new_cmp, new_sel, wrows[:, -n_keep:]

def gla_chunked(q, k, v, logf, s0):
    bsz, L = q.shape[0], q.shape[1]
    nc = -(-L // H_CHUNK)
    pad = nc * H_CHUNK - L

    def prep(t):
        t = jnp.pad(t, ((0, 0), (0, pad), (0, 0), (0, 0)))
        return t.reshape(bsz, nc, H_CHUNK, H_HEADS, t.shape[-1])

    q, k, v, logf = prep(q), prep(k), prep(v), prep(logf)
    acum = jnp.cumsum(logf, axis=2)
    alast = acum[:, :, -1:]
    qe = q * jnp.exp(acum)
    ke = k * jnp.exp(-acum)
    kd = k * jnp.exp(alast - acum)
    tri = jnp.tril(jnp.ones((H_CHUNK, H_CHUNK), bool))
    att = jnp.where(tri, jnp.einsum('bcthk,bcshk->bchts', qe, ke), 0.0)
    o_intra = jnp.einsum('bchts,bcshv->bcthv', att, v)
    upd = jnp.einsum('bcshk,bcshv->bchkv', kd, v)

    def step(s, inp):
        dec, up = inp
        return dec[..., None] * s + up, s

    s_last, s_prev = lax.scan(step, s0, (jnp.exp(alast[:, :, 0]).swapaxes(0, 1), upd.swapaxes(0, 1)))
    o_inter = jnp.einsum('bcthk,bchkv->bcthv', qe, s_prev.swapaxes(0, 1))
    o = (o_intra + o_inter).reshape(bsz, nc * H_CHUNK, H_HEADS, H_DV)[:, :L]
    return o, s_last

def hgrn2_mixer(u, s0, lb, w_in, norm_g, w_out):
    bsz, L, _ = u.shape
    q, fr, iv, gate = jnp.split(u @ w_in, 4, axis=-1)
    q = jax.nn.silu(q).reshape(bsz, L, H_HEADS, H_DK).astype(F32)
    forget = lb + (1.0 - lb) * jax.nn.sigmoid(fr.astype(F32))
    logf = jnp.log(forget).reshape(bsz, L, H_HEADS, H_DK)
    k = (1.0 - forget).reshape(bsz, L, H_HEADS, H_DK)
    v = iv.reshape(bsz, L, H_HEADS, H_DV).astype(F32)
    o, s = gla_chunked(q, k, v, logf, s0.astype(F32))
    o = rmsnorm(o.astype(u.dtype), norm_g) * jax.nn.silu(gate.reshape(bsz, L, H_HEADS, H_DV))
    return o.reshape(bsz, L, D_MODEL) @ w_out, s.astype(s0.dtype)

def hier_moe(u, w_rg, b_rg, w_re, b_re, w1, w3, w2):
    shp = u.shape
    x = u.reshape(-1, D_MODEL)
    pg = jax.nn.softmax((x @ w_rg).astype(F32) + b_rg.astype(F32), axis=-1)
    pg_top, g_idx = lax.top_k(pg, 1)
    le = ((x @ w_re).astype(F32) + b_re.astype(F32)).reshape(-1, MOE_GROUPS, MOE_EPG)
    le_g = jnp.einsum('tge,tg->te', le, jax.nn.one_hot(g_idx[:, 0], MOE_GROUPS, dtype=F32))
    top_l, e_idx = lax.top_k(le_g, MOE_TOPK)
    wts = pg_top * jax.nn.softmax(top_l, axis=-1)
    eid = g_idx * MOE_EPG + e_idx
    combine = jnp.einsum('tk,tke->te', wts, jax.nn.one_hot(eid, MOE_EXPERTS, dtype=F32))
    h = jax.nn.silu(jnp.einsum('td,edf->tef', x, w1)) * jnp.einsum('td,edf->tef', x, w3)
    y = jnp.einsum('tef,efd->td', h * combine[:, :, None].astype(h.dtype), w2)
    return y.reshape(shp)

def gather_pages(cache, page_table):
    pages = cache[page_table]
    b, n, p = pages.shape[0], pages.shape[1], pages.shape[2]
    return pages.reshape(b, n * p, *pages.shape[3:])

def setup_inputs(seed: int = 0) -> dict:
    key = jax.random.key(seed)
    keys = iter(jax.random.split(key, 48))

    def nrm(shape, scale):
        return scale * jax.random.normal(next(keys), shape, F32)

    n_pages = PAST_LEN // PAGE_SIZE
    n_pool = (DEC_BATCH * n_pages * 5) // 4
    win_buf = min(WINDOW, PAST_LEN)
    page_table = jax.random.permutation(next(keys), n_pool)[:DEC_BATCH * n_pages]
    page_table = page_table.reshape(DEC_BATCH, n_pages).astype(jnp.int32)
    dt0 = jnp.exp(jax.random.uniform(next(keys), (N_A, M_HEADS), F32, math.log(1e-3), math.log(1e-1)))
    a_log = jnp.log(jax.random.uniform(next(keys), (N_A, M_HEADS), F32, 1.0, 16.0))
    return {
        'x_prompt': nrm((BATCH, SEQ, D_MODEL), 1.0),
        'x_sample': nrm((DEC_BATCH, DEC_SEQ, D_MODEL), 1.0),
        'state_ssm': nrm((N_A, DEC_BATCH, M_HEADS, M_HEADDIM, M_DSTATE), 0.3),
        'state_conv': nrm((N_A, DEC_BATCH, M_CONV - 1, M_CONV_DIM), 1.0),
        'cache_kv_cmp': nrm((N_B, n_pool, PAGE_SIZE, 2, KV_HEADS, HEAD_DIM), 1.0),
        'cache_kv_sel': nrm((N_B, n_pool, PAGE_SIZE, 2, KV_HEADS, HEAD_DIM), 1.0),
        'cache_kv_win': nrm((N_B, DEC_BATCH, win_buf, 2, KV_HEADS, HEAD_DIM), 1.0),
        'state_hgrn': nrm((N_C, DEC_BATCH, H_HEADS, H_DK, H_DV), 0.3),
        'page_table': page_table,
        'norm_g': 1.0 + nrm((DEPTH, 2, D_MODEL), 0.02),
        'rel_table': nrm((REL_BUCKETS, N_HEADS), 0.3),
        'm_w_in': nrm((N_A, D_MODEL, M_PROJ), D_MODEL ** -0.5),
        'm_conv_w': nrm((N_A, M_CONV, M_CONV_DIM), M_CONV ** -0.5),
        'm_conv_b': nrm((N_A, M_CONV_DIM), 0.02),
        'm_dt_bias': dt0 + jnp.log(-jnp.expm1(-dt0)),
        'm_a_log': a_log,
        'm_d': 1.0 + nrm((N_A, M_HEADS), 0.1),
        'm_norm_g': 1.0 + nrm((N_A, M_DINNER), 0.02),
        'm_w_out': nrm((N_A, M_DINNER, D_MODEL), M_DINNER ** -0.5),
        'n_w_in': nrm((N_B, D_MODEL, NSA_PROJ), D_MODEL ** -0.5),
        'n_q_g': 1.0 + nrm((N_B, HEAD_DIM), 0.02),
        'n_k_g': 1.0 + nrm((N_B, 3, HEAD_DIM), 0.02),
        'n_cmp_pe': nrm((N_B, 2, CMP_BLOCK, HEAD_DIM), 0.1),
        'n_cmp_w1': nrm((N_B, 2, CMP_BLOCK * HEAD_DIM, HEAD_DIM), (CMP_BLOCK * HEAD_DIM) ** -0.5),
        'n_cmp_w2': nrm((N_B, 2, HEAD_DIM, HEAD_DIM), HEAD_DIM ** -0.5),
        'n_w_out': nrm((N_B, N_HEADS * HEAD_DIM, D_MODEL), (N_HEADS * HEAD_DIM) ** -0.5),
        'h_w_in': nrm((N_C, D_MODEL, 4 * D_MODEL), D_MODEL ** -0.5),
        'h_lb': nrm((DEPTH, H_HEADS * H_DK), 0.1),
        'h_norm_g': 1.0 + nrm((N_C, H_DV), 0.02),
        'h_w_out': nrm((N_C, D_MODEL, D_MODEL), D_MODEL ** -0.5),
        'moe_w_rg': nrm((DEPTH, D_MODEL, MOE_GROUPS), D_MODEL ** -0.5),
        'moe_b_rg': nrm((DEPTH, MOE_GROUPS), 0.01),
        'moe_w_re': nrm((DEPTH, D_MODEL, MOE_EXPERTS), D_MODEL ** -0.5),
        'moe_b_re': nrm((DEPTH, MOE_EXPERTS), 0.01),
        'moe_w1': nrm((DEPTH, MOE_EXPERTS, D_MODEL, MOE_FF), D_MODEL ** -0.5),
        'moe_w3': nrm((DEPTH, MOE_EXPERTS, D_MODEL, MOE_FF), D_MODEL ** -0.5),
        'moe_w2': nrm((DEPTH, MOE_EXPERTS, MOE_FF, D_MODEL), MOE_FF ** -0.5),
    }

def reference(x_prompt, x_sample, state_ssm, state_conv, cache_kv_cmp, cache_kv_sel, cache_kv_win,
              state_hgrn, page_table, norm_g, rel_table,
              m_w_in, m_conv_w, m_conv_b, m_dt_bias, m_a_log, m_d, m_norm_g, m_w_out,
              n_w_in, n_q_g, n_k_g, n_cmp_pe, n_cmp_w1, n_cmp_w2, n_w_out,
              h_w_in, h_lb, h_norm_g, h_w_out,
              moe_w_rg, moe_b_rg, moe_w_re, moe_b_re, moe_w1, moe_w3, moe_w2):
    bp, lp = x_prompt.shape[0], x_prompt.shape[1]
    past_len = page_table.shape[1] * cache_kv_cmp.shape[2]
    dt = x_prompt.dtype
    lbs = jax.nn.softmax(h_lb.astype(F32), axis=0)
    lbs = jnp.cumsum(lbs, axis=0) - lbs[0]
    xp, xs = x_prompt, x_sample
    ssm_p, conv_p, cmp_p, sel_p, win_p, hg_p = [], [], [], [], [], []
    ssm_s, conv_s, cmp_s, sel_s, win_s, hg_s = [], [], [], [], [], []
    for i in range(DEPTH):
        kind, j = i % N_MIXERS, i // N_MIXERS
        hp = rmsnorm(xp, norm_g[i, 0])
        hs = rmsnorm(xs, norm_g[i, 0])
        if kind == 0:
            w = (m_w_in[j], m_conv_w[j], m_conv_b[j], m_dt_bias[j], m_a_log[j], m_d[j], m_norm_g[j], m_w_out[j])
            yp, cbuf, hh = mamba_mixer(hp, jnp.zeros((bp, M_CONV - 1, M_CONV_DIM), dt),
                                       jnp.zeros((bp, M_HEADS, M_HEADDIM, M_DSTATE), dt), *w)
            ssm_p.append(hh)
            conv_p.append(cbuf)
            ys, cbuf, hh = mamba_mixer(hs, state_conv[j], state_ssm[j], *w)
            ssm_s.append(hh)
            conv_s.append(cbuf)
        elif kind == 1:
            w = (n_w_in[j], n_q_g[j], n_k_g[j], n_cmp_pe[j], n_cmp_w1[j], n_cmp_w2[j], n_w_out[j], rel_table)
            empty = jnp.zeros((bp, 0, 2, KV_HEADS, HEAD_DIM), dt)
            yp, rc, rs, wb = nsa_mixer(hp, 0, empty, empty, empty, min(WINDOW, lp), *w)
            cmp_p.append(rc)
            sel_p.append(rs)
            win_p.append(wb)
            ys, rc, rs, wb = nsa_mixer(hs, past_len, gather_pages(cache_kv_cmp[j], page_table),
                                       gather_pages(cache_kv_sel[j], page_table), cache_kv_win[j],
                                       cache_kv_win.shape[2], *w)
            cmp_s.append(rc)
            sel_s.append(rs)
            win_s.append(wb)
        else:
            w = (lbs[i], h_w_in[j], h_norm_g[j], h_w_out[j])
            yp, st = hgrn2_mixer(hp, jnp.zeros((bp, H_HEADS, H_DK, H_DV), dt), *w)
            hg_p.append(st)
            ys, st = hgrn2_mixer(hs, state_hgrn[j], *w)
            hg_s.append(st)
        xp = xp + yp
        xs = xs + ys
        mw = (moe_w_rg[i], moe_b_rg[i], moe_w_re[i], moe_b_re[i], moe_w1[i], moe_w3[i], moe_w2[i])
        xp = xp + hier_moe(rmsnorm(xp, norm_g[i, 1]), *mw)
        xs = xs + hier_moe(rmsnorm(xs, norm_g[i, 1]), *mw)
    return (xp, xs,
            jnp.stack(ssm_p), jnp.stack(conv_p), jnp.stack(cmp_p), jnp.stack(sel_p), jnp.stack(win_p), jnp.stack(hg_p),
            jnp.stack(ssm_s), jnp.stack(conv_s), jnp.stack(cmp_s), jnp.stack(sel_s), jnp.stack(win_s), jnp.stack(hg_s))


_drawn_inputs = setup_inputs


def setup_inputs(seed=0):
    import zlib

    import numpy as np

    out = dict(_drawn_inputs(seed))
    spreads = {}
    factors = {'n_q_g': 8.0, 'n_k_g': 3.654, 'h_norm_g': 3.649, 'moe_b_re': 3.214}
    for name, (base, spread) in spreads.items():
        noise = np.random.default_rng([zlib.crc32(name.encode()), seed]).standard_normal(out[name].shape)
        drawn = base * np.exp(spread * noise) if base else spread * noise
        out[name] = jnp.asarray(drawn.astype(out[name].dtype))
    for name, factor in factors.items():
        out[name] = (out[name] * factor).astype(out[name].dtype)
    return out
```

```python
from contextlib import ExitStack, contextmanager

import numpy as np
import concourse.bass as bass
from concourse import mybir

ALU = mybir.AluOpType
ACT = mybir.ActivationFunctionType
AX = mybir.AxisListType
F32 = mybir.dt.float32
I32 = mybir.dt.int32
U32 = mybir.dt.uint32

D = 1024
LP = 256
NB = 8
T = LP + NB
KT = D // 128
EPS = 1e-6
NEG = -1e30
DI = 2048
CI = DI // 128
NCH = 24
MH = 32
NG = 4
HD = 64
PAST = 1024
NPAGE = PAST // 128
NCMP = 63
NCMPP = 15
NSEL = 17
NSTRIP = 512
HH = 8
HC = 32
NHC = LP // HC
NE = 16
FF = 512
SLOTS = 6
SLOT = 2048


def constants():
    c = {}
    i = np.arange(128)
    c["ident"] = np.eye(128)
    c["ones"] = np.ones((128, 128))
    c["ones64"] = (i[:, None] // 64 == i[None, :] // 64) * 1.0
    c["ssd_mask"] = np.where(i[None, :] >= i[:, None], 0.0, NEG)
    c["att_mask"] = ((i[None, :] >= i[:, None]) & (i[None, :] // HC == i[:, None] // HC)) * 1.0
    b, hd = i // 16, i % 16
    grp = (hd // 8) * 2 + hd % 2
    c["same_group"] = ((b[:, None] == b[None, :]) & (grp[:, None] == grp[None, :])) * 1.0
    c["of_seq"] = (b[:, None] == np.arange(8)[None, :]) * 1.0
    ov = np.zeros((128, NSEL))
    for k in range(NCMP):
        for j in range(NSEL):
            ov[k, j] = 16 * k < 64 * j + 64 and 16 * k + 32 > 64 * j
    ov[64:] = ov[:64]
    c["overlap"] = ov
    c["block_no"] = np.tile(np.arange(1, NSEL + 1.0), (128, 1))
    c["forced"] = np.tile(np.where((np.arange(NSEL) == 0) | (np.arange(NSEL) == NSEL - 1), 1e9, 0.0), (128, 1))
    q = np.arange(256).reshape(2, 128)[:, ::-1].T
    ends = np.arange(16) * 16 + 31
    v = (q[:, :, None] >= ends[None, None, :]) & (np.arange(16) < NCMPP)
    c["cmp_valid"] = v.reshape(128, 32) * 1.0
    c["four_down"] = np.tile([4.0, 3.0, 2.0, 1.0], (128, 1))
    c["scan_keep"] = np.tile((np.arange(LP) % HC != 0) * 1.0, (128, 1))
    off, at = {}, 0
    for k, a in c.items():
        off[k] = (at, a.shape[1])
        at += a.shape[1]
    return np.concatenate([np.asarray(a, np.float32) for a in c.values()], axis=1), off


def bucket(dist):
    d = np.maximum(dist, 0)
    ratio = np.log(np.maximum(d, 1).astype(np.float32) / 16) / np.float32(np.log(8.0))
    large = np.minimum(16 + (ratio * 16).astype(np.int32), 31)
    return np.where(d < 16, d, large)


def bucket_onehots():
    dist = 255 - np.arange(NSTRIP)
    a = (bucket(dist)[None, :] == np.arange(32)[:, None]) & (dist >= 0)[None, :]
    b = bucket(PAST - np.arange(PAST + 1))[None, :] == np.arange(32)[:, None]
    return np.concatenate([a, b], axis=1).astype(np.float32)


PCOLS, _at = {}, 0
for _n, _w in [("norm_g", 64), ("conv_w", 2 * NCH * 4), ("conv_b", 2 * NCH), ("m_norm_g", 2 * CI), ("m_d", 2 * CI),
               ("a_log", 2), ("dt_bias", 2), ("q_g", 1), ("k_g", 3), ("h_lb", 32), ("h_norm_g", 1),
               ("pe", 32), ("moe_b", 80)]:
    PCOLS[_n] = (_at, _w)
    _at += _w
NPAR = _at


class Count:

    def __init__(self, sem, step=1):
        self.sem, self.step, self.n, self.start = sem, step, 0, 0
        self.turn = 0

    def one(self):
        self.n += self.step
        return self.sem, self.step

    def now(self):
        return self.sem, self.turn + self.n

    def at(self, k):
        return self.sem, self.start + k * self.step

    @contextmanager
    def each(self, i, per, trips):
        first = self.n
        self.turn = i * (per * self.step)
        yield
        assert self.n == first + per * self.step, (self.n, first, per)
        self.turn = 0
        self.n = first + per * self.step * trips


class Core:

    def __init__(self, nc, ctx):
        self.nc, self.ctx, self.counts, self.blocks = nc, ctx, {}, 0
        self.bank = [ctx.enter_context(nc.psum_tensor(f"bank{i}", [128, 512], F32)) for i in range(8)]

    def sb(self, name, shape, dt=F32, ctx=None):
        return (ctx or self.ctx).enter_context(self.nc.sbuf_tensor(name, shape, dt))

    def count(self, name, step=1):
        if name not in self.counts:
            self.counts[name] = Count(self.ctx.enter_context(self.nc.semaphore(name)), step)
        return self.counts[name]

    @contextmanager
    def block(self):
        for c in self.counts.values():
            c.start = c.n
        with self.nc.Block(no_gpsimd_drain=True) as b:
            yield b


class Weights:

    def __init__(self, core):
        self.core = core
        self.ring = core.sb("ring", [128, SLOTS, SLOT])
        self.full = [core.count(f"slot_full{s}", 16) for s in range(SLOTS)]
        self.free = [core.count(f"slot_free{s}") for s in range(SLOTS)]
        self.plan, self.sent, self.used = [], 0, 0

    def add(self, w, kt, cols):
        self.plan.append((w, kt, cols))

    def view(self, s, kt, cols):
        return self.ring[:, s, 0:kt * cols].rearrange("p (k c) -> p k c", k=kt)

    def send(self, sp, upto):
        while self.sent < min(upto, len(self.plan)):
            s = self.sent % SLOTS
            w, kt, cols = self.plan[self.sent]
            if self.sent >= SLOTS:
                sp.wait_ge(self.free[s].sem, self.sent // SLOTS)
            sp.dma_start(self.view(s, kt, cols), w.rearrange("(k p) c -> p k c", p=128)).then_inc(*self.full[s].one())
            self.sent += 1


def build(nc, I, O):
    with ExitStack() as ctx:
        core = Core(nc, ctx)
        sb, count, bank = core.sb, core.count, core.bank

        cst_np, coff = constants()
        consts = sb("consts", [128, cst_np.shape[1]])
        params = sb("params", [128, NPAR])
        xT = sb("xT", [128, KT, T])
        uT = sb("uT", [128, KT, T])
        w_dt = sb("w_dt", [128, 2, KT, MH])
        w_gl = sb("w_gl", [128, KT, 48])
        w_rt = sb("w_rt", [128, 4, KT, 20])
        eps = sb("eps", [128, 3])
        lb = sb("lb", [128, 16])
        W = Weights(core)

        def cst(name):
            a, n = coff[name]
            return consts[:, a:a + n]

        def par(name, k=0, n=1):
            a = PCOLS[name][0] + k
            return params[:, a:a + n]

        ident, ones = cst("ident"), cst("ones")
        scr = {}

        def scratch(name, shape):
            if name not in scr:
                scr[name] = nc.dram_tensor(name, shape, F32, kind="Internal").ap()
            return scr[name]

        def plan_proj(w, k, n):
            kt = k // 128
            per = SLOT // kt
            for c in range(0, n, per):
                W.add(w[:, c:c + min(per, n - c)], kt, min(per, n - c))

        def plan_moe(layer):
            for e in range(NE):
                for h in range(2):
                    W.add(I["moe_w1"][layer, e][:, 256 * h:256 * h + 256], KT, 256)
                    W.add(I["moe_w3"][layer, e][:, 256 * h:256 * h + 256], KT, 256)
                for h in range(2):
                    W.add(I["moe_w2"][layer, e][:, 512 * h:512 * h + 512], FF // 128, 512)

        for layer in range(4):
            j = layer // 3
            if layer % 3 == 0:
                plan_proj(I["m_w_in"][j], D, 5120)
                plan_proj(I["m_w_out"][j], DI, D)
            elif layer == 1:
                plan_proj(I["n_w_in"], D, 2560)
                plan_proj(I["n_w_out"], D, D)
            else:
                plan_proj(I["h_w_in"], D, 4096)
                plan_proj(I["h_w_out"], D, D)
            plan_moe(layer)

        pe_done, act_done, dve_done = count("pe_done"), count("act_done"), count("dve_done")
        pool_done = count("pool_done")
        in_loaded = count("in_loaded", 16)
        out_sent = count("out_sent", 16)
        misc = count("misc_dma", 16)

        def linker(eng, c):
            def link(ins):
                ins.then_inc(*c.one())
                eng.wait_ge(*c.now())
                return ins
            return link

        with core.block() as block:
            @block.sync
            def _(sp):
                for dst, src in [(consts, I["consts"]), (params, I["params"]), (xT, I["xT"]), (w_dt, I["w_dt"]),
                                 (w_gl, I["w_gl"]), (w_rt, I["w_rt"])]:
                    sp.dma_start(dst[:], src).then_inc(*in_loaded.one())
                W.send(sp, SLOTS)
                sp.wait_ge(*in_loaded.now())

            @block.vector
            def _(dve):
                link = linker(dve, dve_done)
                link(nc.vector.memset(eps[:, 0:1], EPS))
                link(nc.vector.memset(eps[:, 1:2], 64 * EPS))
                link(nc.vector.memset(eps[:, 2:3], 1.0))
        with core.block() as block:
            lbm, lbe = sb("lbm", [128, 8]), sb("lbe", [128, 32])

            @block.vector
            def _(dve):
                link = linker(dve, dve_done)
                lbv = par("h_lb", 0, 32)
                link(nc.vector.tensor_reduce(lbm[:], lbv.rearrange("p (l c) -> p c l", l=4), AX.X, ALU.max))
                for l in range(4):
                    link(nc.vector.tensor_tensor(lbe[:, 8 * l:8 * l + 8], lbv[:, 8 * l:8 * l + 8], lbm[:], ALU.subtract))
                dve.wait_ge(*act_done.at(1))
                link(nc.vector.tensor_reduce(lbm[:], lbe[:].rearrange("p (l c) -> p c l", l=4), AX.X, ALU.add))
                link(nc.vector.reciprocal(lbm[:], lbm[:]))
                link(nc.vector.tensor_tensor(lb[:, 0:8], lbe[:, 8:16], lbe[:, 16:24], ALU.add))
                link(nc.vector.tensor_tensor(lb[:, 0:8], lb[:, 0:8], lbm[:], ALU.mult))
                link(nc.vector.tensor_scalar(lb[:, 8:16], lb[:, 0:8], -1.0, 1.0, ALU.mult, ALU.add))

            @block.scalar
            def _(act):
                act.wait_ge(*dve_done.at(5))
                nc.scalar.activation(lbe[:], lbe[:], ACT.Exp).then_inc(*act_done.one())

        def norm_all(src, chunks, gain, dst, name):
            with ExitStack() as st:
                sq = sb(name + "_sq", [128, 4, T], ctx=st)
                rs = sb(name + "_rs", [128, T], ctx=st)
                parts = chunks // 2
                with core.block() as block:
                    @block.scalar
                    def _(act):
                        for c in range(parts):
                            if c >= 2:
                                act.wait_ge(*pe_done.at(c - 1))
                            nc.scalar.activation(sq[:, 2 * (c % 2):2 * (c % 2) + 2], src[:, 2 * c:2 * c + 2], ACT.Square).then_inc(*act_done.one())
                        act.wait_ge(*pe_done.at(parts))
                        nc.scalar.activation(rs[:], bank[0][:, 0:T], ACT.Sqrt, bias=eps[:, 0:1], scale=1.0 / (128 * chunks)).then_inc(*act_done.one())

                    @block.tensor
                    def _(pe):
                        for c in range(parts):
                            pe.wait_ge(*act_done.at(c + 1))
                            for k in range(2):
                                mm = nc.tensor.matmul(bank[0][:, 0:T], ones, sq[:, 2 * (c % 2) + k], start=(c + k == 0),
                                                      stop=(c == parts - 1 and k == 1))
                            mm.then_inc(*pe_done.one())

                    @block.vector
                    def _(dve):
                        link = linker(dve, dve_done)
                        dve.wait_ge(*act_done.at(parts + 1))
                        link(nc.vector.reciprocal(rs[:], rs[:]))
                        for c in range(chunks):
                            nc.vector.scalar_tensor_tensor(out=dst[:, c], in0=src[:, c], scalar=gain(c), in1=rs[:],
                                                           op0=ALU.mult, op1=ALU.mult).then_inc(*dve_done.one())

        def norm_each(jobs, ones_m, name):
            with ExitStack() as st:
                n = len(jobs)
                sq = sb(name + "_sq", [128, 2, T], ctx=st)
                rs = sb(name + "_rs", [128, 2, T], ctx=st)
                with core.block() as block:
                    @block.scalar
                    def _(act):
                        for k in range(n + 1):
                            if k < n:
                                if k >= 2:
                                    act.wait_ge(*pe_done.at(k - 1))
                                nc.scalar.activation(sq[:, k % 2], jobs[k][0], ACT.Square).then_inc(*act_done.one())
                            if k >= 1:
                                act.wait_ge(*pe_done.at(k))
                                if k >= 3:
                                    act.wait_ge(*dve_done.at(2 * (k - 2)))
                                nc.scalar.activation(rs[:, (k - 1) % 2], bank[(k - 1) % 2][:, 0:T], ACT.Sqrt,
                                                     bias=jobs[k - 1][4], scale=jobs[k - 1][3]).then_inc(*act_done.one())

                    def root_at(k):
                        return 2 * k + 3 if k < n - 1 else 2 * n

                    def square_at(k):
                        return 1 if k == 0 else 2 * k

                    @block.tensor
                    def _(pe):
                        for k in range(n):
                            pe.wait_ge(*act_done.at(square_at(k)))
                            if k >= 2:
                                pe.wait_ge(*act_done.at(root_at(k - 2)))
                            nc.tensor.matmul(bank[k % 2][:, 0:T], ones_m, sq[:, k % 2], start=True, stop=True).then_inc(*pe_done.one())

                    @block.vector
                    def _(dve):
                        for k in range(n):
                            dve.wait_ge(*act_done.at(root_at(k)))
                            nc.vector.reciprocal(rs[:, k % 2], rs[:, k % 2]).then_inc(*dve_done.one())
                            dve.wait_ge(*dve_done.now())
                            nc.vector.scalar_tensor_tensor(out=jobs[k][1], in0=jobs[k][0], scalar=jobs[k][2], in1=rs[:, k % 2],
                                                           op0=ALU.mult, op1=ALU.mult).then_inc(*dve_done.one())


        def project(actT, kt, n_cols, act_step, dve_step, extra=None):
            per = SLOT // kt
            n_tiles = n_cols // 128
            first = W.used
            slots = n_cols // per
            total = n_tiles + (1 if extra else 0)
            took_a, took_v = count("tile_taken_act"), count("tile_taken_dve")
            filled = count("tile_filled")
            with core.block() as block:
                @block.sync
                def _(sp):
                    W.send(sp, first + slots + SLOTS)

                @block.tensor
                def _(pe):
                    for t in range(total):
                        s = (first + t * 128 // per) % SLOTS
                        if t < n_tiles and t * 128 % per == 0:
                            pe.wait_ge(W.full[s].sem, 16 * ((first + t * 128 // per) // SLOTS + 1))
                        if t >= 4:
                            pe.wait_ge(*took_a.at(t - 3))
                            pe.wait_ge(*took_v.at(t - 3))
                        for k in range(kt):
                            if t < n_tiles:
                                c = t * 128 % per
                                lhs, m = W.view(s, kt, per)[:, k, c:c + 128], 128
                            else:
                                lhs, m = extra[0][:, k], extra[1]
                            mm = nc.tensor.matmul(bank[t % 4][0:m, 0:T], lhs, actT[:, k], start=(k == 0), stop=(k == kt - 1))
                        mm.then_inc(*filled.one())

                @block.scalar
                def _(act):
                    for t in range(total):
                        act.wait_ge(*filled.at(t + 1))
                        if t < n_tiles and (t + 1) * 128 % per == 0:
                            act.sem_inc(*W.free[(first + t * 128 // per) % SLOTS].one())
                        ins = act_step(act, t, bank[t % 4])
                        if ins is None:
                            act.sem_inc(*took_a.one())
                        else:
                            ins.then_inc(*took_a.one())

                @block.vector
                def _(dve):
                    for t in range(total):
                        dve.wait_ge(*took_a.at(t + 1))
                        ins = dve_step(dve, t, bank[t % 4])
                        if ins is None:
                            dve.sem_inc(*took_v.one())
                        else:
                            ins.then_inc(*took_v.one())
            W.used += slots

        def add_residual(dve, t, ps):
            return nc.vector.tensor_tensor(xT[:, t], xT[:, t], ps[:, 0:T], ALU.add)

        nothing = lambda eng, t, ps: None

        env = dict(nc=nc, core=core, I=I, O=O, W=W, cst=cst, par=par, xT=xT, uT=uT, eps=eps, lb=lb, w_dt=w_dt, w_gl=w_gl,
                   w_rt=w_rt, scratch=scratch, linker=linker, norm_all=norm_all, norm_each=norm_each, project=project,
                   add_residual=add_residual, nothing=nothing, ident=ident, ones=ones)
        for layer in range(4):
            norm_all(xT, KT, lambda c: par("norm_g", (layer * 2) * 8 + c), uT, f"na{layer}")
            if layer % 3 == 0:
                ssd_layer(env, layer // 3)
            elif layer == 1:
                nsa_layer(env)
            else:
                hgrn_layer(env)
            norm_all(xT, KT, lambda c: par("norm_g", (layer * 2 + 1) * 8 + c), uT, f"nm{layer}")
            moe(env, layer)
        with core.block() as block:
            @block.sync
            def _(sp):
                sp.dma_start(O["yT"], xT[:]).then_inc(*out_sent.one())
                sp.wait_ge(*out_sent.now())


def ssd_layer(env, j):
    (nc, core, I, O, W, cst, par, xT, uT, eps, scratch, linker, ident, ones) = (
        env[k] for k in ("nc", "core", "I", "O", "W", "cst", "par", "xT", "uT", "eps", "scratch", "linker", "ident", "ones"))
    count, bank = core.count, core.bank
    pe_done, act_done, dve_done, pool_done = (count(n) for n in ("pe_done", "act_done", "dve_done", "pool_done"))
    misc, out_sent = count("misc_dma", 16), count("out_sent", 16)
    state_in, state_out = [count(f"state_in{b}", 16) for b in range(3)], [count(f"state_out{b}", 16) for b in range(3)]
    group_in, pool_sent = [count(f"group_in{b}", 16) for b in range(2)], count("pool_sent", 16)
    n = f"s{j}_"
    with ExitStack() as layer:
        def sb(name, shape, dt=F32, ctx=layer):
            return core.sb(n + name, shape, dt, ctx)

        xbc = sb("xbc", [128, NCH, T])
        zT = sb("zT", [128, CI, T])
        tail = sb("tail", [128, NCH, 11])
        with ExitStack() as st:
            conv0 = sb("conv0", [128, NCH, 3, NB])
            dtr = sb("dtr", [32, T])
            with core.block() as block:
                @block.gpsimd
                def _(pool):
                    pool.dma_start(conv0[:], I["conv0"][j]).then_inc(*misc.one())
                    pool.wait_ge(*misc.now())

            def act_step(act, t, ps):
                if t < CI:
                    return nc.scalar.activation(zT[:, t], ps[:, 0:T], ACT.Silu)
                if t < CI + NCH:
                    return nc.scalar.copy(tail[:, t - CI], ps[:, 253:T])
                return nc.scalar.copy(dtr[:], ps[0:32, 0:T])

            def dve_step(dve, t, ps):
                if t < CI or t == CI + NCH:
                    return None
                link = linker(dve, dve_done)
                c = t - CI
                o = xbc[:, c]

                def w(k):
                    return par("conv_w", (j * NCH + c) * 4 + k)
                link(nc.vector.tensor_scalar(o, ps[:, 0:T], w(3), par("conv_b", j * NCH + c), ALU.mult, ALU.add))
                for k in (2, 1, 0):
                    s = 3 - k
                    nc.vector.scalar_tensor_tensor(out=o[:, LP:T], in0=conv0[:, c, k], scalar=w(k), in1=o[:, LP:T],
                                                   op0=ALU.mult, op1=ALU.add).then_inc(*dve_done.one())
                    ins = nc.vector.scalar_tensor_tensor(out=o[:, s:LP], in0=ps[:, 0:LP - s], scalar=w(k), in1=o[:, s:LP],
                                                         op0=ALU.mult, op1=ALU.add)
                    if k:
                        link(ins)
                return ins

            env["project"](uT, KT, 5120, act_step, dve_step, extra=(env["w_dt"][:, j], MH))

            dtT = sb("dtT", [32, T])
            daT = sb("daT", [32, T])
            acT = sb("acT", [32, LP])
            stack = sb("stack", [96, LP])
            s1, s2 = sb("s1", [32, T]), sb("s2", [32, T])
            ea1 = sb("ea1", [32, 128])
            acol = sb("acol", [32, 2])
            one_row = sb("one_row", [32, 128])
            d_ac, d_e1, d_dec = scratch("scr_ac", [32, LP]), scratch("scr_e1", [32, 128]), scratch("scr_dec", [2, 32, NB])
            with core.block() as block:
                @block.vector
                def _(dve):
                    link = linker(dve, dve_done)
                    link(nc.vector.memset(one_row[:], 1.0))
                    link(nc.vector.tensor_scalar(dtr[:], dtr[:], par("dt_bias", j)[0:32], None, ALU.add))
                    link(nc.vector.scalar_tensor_tensor(out=s1[:], in0=dtr[:], scalar=-1.0, in1=dtr[:], op0=ALU.mult, op1=ALU.max))
                    dve.wait_ge(*act_done.at(3))
                    link(nc.vector.scalar_tensor_tensor(out=dtT[:], in0=dtr[:], scalar=0.0, in1=s2[:], op0=ALU.max, op1=ALU.add))
                    link(nc.vector.tensor_scalar(acol[:, 1:2], acol[:, 0:1], -1.0, None, ALU.mult))
                    link(nc.vector.tensor_scalar(daT[:], dtT[:], acol[:, 1:2], None, ALU.mult))
                    for c in range(2):
                        link(nc.vector.tensor_tensor_scan(acT[:, 128 * c:128 * c + 128], one_row[:], daT[:, 128 * c:128 * c + 128],
                                                          0.0, ALU.mult, ALU.add))
                    link(nc.vector.tensor_copy(stack[0:32, :], dtT[:, 0:LP]))
                    link(nc.vector.tensor_scalar(stack[64:96, :], acT[:], -1.0, None, ALU.mult))
                    dve.wait_ge(*act_done.at(6))
                    link(nc.vector.tensor_tensor(stack[32:64, :], s1[:, 0:LP], dtT[:, 0:LP], ALU.mult))

                @block.scalar
                def _(act):
                    nc.scalar.activation(acol[:, 0:1], par("a_log", j)[0:32], ACT.Exp).then_inc(*act_done.one())
                    act.wait_ge(*dve_done.at(3))
                    nc.scalar.activation(s2[:], s1[:], ACT.Exp, scale=-1.0).then_inc(*act_done.one())
                    act.wait_ge(*act_done.now())
                    nc.scalar.activation(s2[:], s2[:], ACT.Ln, bias=eps[0:32, 2:3]).then_inc(*act_done.one())
                    nc.scalar.activation(xbc[:, :], xbc[:, :], ACT.Silu).then_inc(*act_done.one())
                    act.wait_ge(*dve_done.at(8))
                    for c in range(2):
                        nc.scalar.activation(s1[:, 128 * c:128 * c + 128], acT[:, 128 * c:128 * c + 128], ACT.Exp, scale=-1.0,
                                             bias=acT[:, 128 * c + 127:128 * c + 128]).then_inc(*act_done.one())
                    nc.scalar.activation(ea1[:], acT[:, 128:LP], ACT.Exp).then_inc(*act_done.one())
                    nc.scalar.activation(daT[:, LP:T], daT[:, LP:T], ACT.Exp).then_inc(*act_done.one())

                @block.gpsimd
                def _(pool):
                    pool.dma_start(O["conv_tail"][j], tail[:]).then_inc(*pool_sent.one())
                    pool.dma_start(O["conv_keep"][j], conv0[:, :, 1:3]).then_inc(*pool_sent.one())
                    pool.wait_ge(*dve_done.at(8))
                    pool.dma_start(d_ac, acT[:]).then_inc(*misc.one())
                    pool.dma_start(d_dec[0], dtT[:, LP:T]).then_inc(*misc.one())
                    pool.wait_ge(*act_done.at(8))
                    pool.dma_start(d_e1, ea1[:]).then_inc(*misc.one())
                    pool.dma_start(d_dec[1], daT[:, LP:T]).then_inc(*misc.one())
                    pool.wait_ge(*misc.now())
                    pool.wait_ge(*pool_sent.now())

        with ExitStack() as st:
            acb = sb("acb", [128, MH, 128], ctx=st)
            e1b = sb("e1b", [128, CI, 128], ctx=st)
            nat = sb("nat", [128, 96], ctx=st)
            xdt = sb("xdt", [128, DI], ctx=st)
            xdd = sb("xdd", [128, DI], ctx=st)
            bn = sb("bn", [128, 512], ctx=st)
            s0 = sb("s0", [128, DI], ctx=st)
            cdb = sb("cdb", [128, MH], ctx=st)
            yt = sb("yt", [128, 512], ctx=st)
            for c in range(2):
                lo = 128 * c
                tl = slice(lo, lo + 128)
                with core.block() as block:
                    @block.gpsimd
                    def _(pool):
                        pool.dma_start(acb[:], d_ac[:, tl].rearrange("(o h) l -> o h l", o=1).to_broadcast([128, MH, 128])).then_inc(*misc.one())
                        if c == 1:
                            for h in range(2):
                                pool.dma_start(e1b[64 * h:64 * h + 64], d_e1.rearrange("(o c h) l -> h o c l", h=2, o=1)[h].to_broadcast([64, CI, 128])).then_inc(*misc.one())
                        pool.wait_ge(*misc.now())

                    @block.tensor
                    def _(pe):
                        nc.tensor.transpose(bank[0][:, 0:96], stack[:, tl], ident[0:96, 0:96]).then_inc(*pe_done.one())
                        for g in range(NG):
                            mm = nc.tensor.transpose(bank[1][:, 128 * g:128 * g + 128], xbc[:, CI + g, tl], ident)
                        mm.then_inc(*pe_done.one())
                        for g in range(NG):
                            mm = nc.tensor.matmul(bank[2][:, 128 * g:128 * g + 128], xbc[:, CI + g, tl], xbc[:, CI + NG + g, tl], start=True, stop=True)
                        mm.then_inc(*pe_done.one())
                        for q in range(4):
                            for i in range(4):
                                mm = nc.tensor.transpose(bank[3 + q][:, 128 * i:128 * i + 128], xbc[:, 4 * q + i, tl], ident)
                            mm.then_inc(*pe_done.one())

                    @block.vector
                    def _(dve):
                        dve.wait_ge(*pe_done.at(1))
                        nc.vector.tensor_copy(nat[:], bank[0][:, 0:96]).then_inc(*dve_done.one())
                        dve.wait_ge(*pe_done.at(2))
                        nc.vector.tensor_copy(bn[:], bank[1][:]).then_inc(*dve_done.one())
                        dve.wait_ge(*dve_done.at(1))
                        for q in range(4):
                            dve.wait_ge(*pe_done.at(4 + q))
                            src = bank[3 + q][:].rearrange("p (h d) -> p h d", h=8)
                            for out, r in ((xdt, 0), (xdd, 32)):
                                nc.vector.tensor_tensor(out[:, 512 * q:512 * q + 512].rearrange("p (h d) -> p h d", h=8), src,
                                                        nat[:, r + 8 * q:r + 8 * q + 8].rearrange("p (h o) -> p h o", o=1).to_broadcast([128, 8, 64]),
                                                        ALU.mult).then_inc(*dve_done.one())
                        dve.wait_ge(*misc.now())
                        dve.wait_ge(*act_done.at(1))
                        for g in range(NG):
                            nc.vector.tensor_tensor(acb[:, 8 * g:8 * g + 8], acb[:, 8 * g:8 * g + 8],
                                                    cst("ssd_mask").rearrange("p (o l) -> p o l", o=1).to_broadcast([128, 8, 128]),
                                                    ALU.add).then_inc(*dve_done.one())
                        for g in range(NG):
                            dve.wait_ge(*act_done.at(1 + 8 * (g + 1)))
                            nc.vector.tensor_tensor(acb[:, 8 * g:8 * g + 8], acb[:, 8 * g:8 * g + 8],
                                                    bank[2][:, 128 * g:128 * g + 128].rearrange("p (o l) -> p o l", o=1).to_broadcast([128, 8, 128]),
                                                    ALU.mult).then_inc(*dve_done.one())

                    @block.scalar
                    def _(act):
                        act.wait_ge(*misc.now())
                        nc.scalar.activation(cdb[:], acb[:, :, 127:128].rearrange("p h o -> p (h o)"), ACT.Exp).then_inc(*act_done.one())
                        for g in range(NG):
                            act.wait_ge(*dve_done.at(11 + g))
                            for h in range(8 * g, 8 * g + 8):
                                nc.scalar.activation(acb[:, h], acb[:, h], ACT.Exp, bias=nat[:, 64 + h:65 + h]).then_inc(*act_done.one())

                with core.block() as block:
                    @block.tensor
                    def _(pe):
                        for q in range(4):
                            for i in range(4):
                                for h in range(2):
                                    hd = 2 * (4 * q + i) + h
                                    mm = nc.tensor.matmul(bank[q % 2][64 * h:64 * h + 64, 128 * i:128 * i + 128], xdt[:, 64 * hd:64 * hd + 64],
                                                          acb[:, hd], start=True, stop=True)
                            mm.then_inc(*pe_done.one())
                            if c == 1:
                                for i in range(4):
                                    k = 4 * q + i
                                    mm = nc.tensor.matmul(bank[2 + q % 2][:, 128 * i:128 * i + 128], s0[:, 128 * k:128 * k + 128],
                                                          xbc[:, CI + NG + q, tl], start=True, stop=True)
                                mm.then_inc(*pe_done.one())
                            nc.tensor.matmul(bank[4 + q][:], bn[:, 128 * q:128 * q + 128], xdd[:, 512 * q:512 * q + 512], start=True,
                                             stop=True).then_inc(*pe_done.one())
                            if q in (1, 2):
                                pe.wait_ge(*dve_done.at((5 + c) * q))

                    @block.vector
                    def _(dve):
                        link = linker(dve, dve_done)
                        per = 2 + c
                        for q in range(4):
                            dve.wait_ge(*pe_done.at(per * q + 1))
                            for i in range(4):
                                k = 4 * q + i
                                nc.vector.scalar_tensor_tensor(out=xbc[:, k, tl], in0=xbc[:, k, tl], scalar=par("m_d", j * CI + k),
                                                               in1=bank[q % 2][:, 128 * i:128 * i + 128], op0=ALU.mult,
                                                               op1=ALU.add).then_inc(*dve_done.one())
                            if c == 1:
                                dve.wait_ge(*pe_done.at(per * q + 2))
                                link(nc.vector.tensor_tensor(yt[:].rearrange("p (k l) -> p k l", k=4), bank[2 + q % 2][:].rearrange("p (k l) -> p k l", k=4),
                                                             e1b[:, 4 * q:4 * q + 4], ALU.mult))
                                link(nc.vector.tensor_tensor(xbc[:, 4 * q:4 * q + 4, tl], xbc[:, 4 * q:4 * q + 4, tl],
                                                             yt[:].rearrange("p (k l) -> p k l", k=4), ALU.add))
                            else:
                                dve.wait_ge(*pe_done.at(per * q + 2))
                                link(nc.vector.tensor_copy(s0[:, 512 * q:512 * q + 512], bank[4 + q][:]))
                        if c == 1:
                            for q in range(4):
                                sl = s0[:, 512 * q:512 * q + 512]
                                dve.wait_ge(*pe_done.at(12))
                                link(nc.vector.tensor_tensor(sl.rearrange("p (h d) -> p h d", h=8), sl.rearrange("p (h d) -> p h d", h=8),
                                                             cdb[:, 8 * q:8 * q + 8].rearrange("p (h o) -> p h o", o=1).to_broadcast([128, 8, 64]), ALU.mult))
                                link(nc.vector.tensor_tensor(sl, sl, bank[4 + q][:], ALU.add))
            with core.block() as block:
                @block.sync
                def _(sp):
                    sp.dma_start(O["ssm_p"][j], s0[:]).then_inc(*out_sent.one())
                    sp.wait_ge(*out_sent.now())

        with ExitStack() as st:
            dtb = sb("dtb", [128, CI, NB], ctx=st)
            dab = sb("dab", [128, CI, NB], ctx=st)
            bcr = sb("bcr", [64, 128], ctx=st)
            bcp = sb("bcp", [128, 64], ctx=st)
            bg, cg = sb("bg", [128, 2, NB, 128], ctx=st), sb("cg", [128, 2, NB, 128], ctx=st)
            hbuf = sb("hbuf", [128, 3, 2, NB, 128], ctx=st)
            tmp = sb("tmp", [128, 2, NB, 128], ctx=st)
            ys = sb("ys", [128, CI, NB], ctx=st)
            d_bc = scratch("scr_bc", [64, 128])
            with core.block() as block:
                @block.tensor
                def _(pe):
                    pe.wait_ge(*dve_done.at(1))
                    nc.tensor.transpose(bank[0][0:64, 0:128], bcp[:], ident).then_inc(*pe_done.one())

                @block.vector
                def _(dve):
                    nc.vector.tensor_copy(bcp[:].rearrange("p (k b) -> p k b", k=8), xbc[:, CI:NCH, LP:T]).then_inc(*dve_done.one())
                    dve.wait_ge(*pe_done.at(1))
                    nc.vector.tensor_copy(bcr[:], bank[0][0:64, 0:128]).then_inc(*dve_done.one())
                    dve.wait_ge(*misc.at(4))
                    nc.vector.tensor_tensor(dtb[:], dtb[:], xbc[:, 0:CI, LP:T], ALU.mult).then_inc(*dve_done.one())

                @block.gpsimd
                def _(pool):
                    for k, t in ((0, dtb), (1, dab)):
                        for h in range(2):
                            pool.dma_start(t[64 * h:64 * h + 64], d_dec[k].rearrange("(o c h) b -> h o c b", h=2, o=1)[h].to_broadcast([64, CI, NB])).then_inc(*misc.one())
                    pool.wait_ge(*dve_done.at(2))
                    pool.dma_start(d_bc, bcr[:]).then_inc(*pool_sent.one())
                    pool.wait_ge(*misc.now())
                    pool.wait_ge(*pool_sent.now())

            def bcast(t, g):
                return t[:, 2 * g:2 * g + 2].rearrange("p k (b o) -> p k b o", o=1).to_broadcast([128, 2, NB, 128])
            with core.block() as block:
                @block.gpsimd
                def _(pool):
                    for g in range(NG):
                        if g >= 2:
                            pool.wait_ge(*dve_done.at(14 * (g - 1)))
                        for t, r in ((bg, 0), (cg, 32)):
                            pool.dma_start(t[:, g % 2].rearrange("p b n -> p (b n)"), d_bc[r + 8 * g:r + 8 * g + 8].rearrange("(o b) n -> o (b n)", o=1)
                                           .to_broadcast([128, NB * 128])).then_inc(*group_in[g % 2].one())

                @block.scalar
                def _(act):
                    for k in range(8):
                        if k >= 3:
                            act.wait_ge(*state_out[k % 3].at(k // 3))
                            act.wait_ge(*dve_done.at(7 * (k - 3) + 6))
                        act.dma_start(hbuf[:, k % 3], I["ssm0"][j, :, 2 * k:2 * k + 2]).then_inc(*state_in[k % 3].one())

                @block.sync
                def _(sp):
                    for k in range(8):
                        sp.wait_ge(*dve_done.at(7 * k + 4))
                        sp.dma_start(O["ssm_s"][j, :, 2 * k:2 * k + 2], hbuf[:, k % 3]).then_inc(*state_out[k % 3].one())
                    for b in range(3):
                        sp.wait_ge(*state_out[b].now())

                @block.vector
                def _(dve):
                    link = linker(dve, dve_done)
                    for k in range(8):
                        g = k // 2
                        h = hbuf[:, k % 3]
                        dve.wait_ge(*state_in[k % 3].at(k // 3 + 1))
                        dve.wait_ge(*group_in[g % 2].at(2 * (g // 2 + 1)))
                        link(nc.vector.tensor_tensor(h, h, bcast(dab, k), ALU.mult))
                        for q in range(2):
                            link(nc.vector.tensor_tensor(tmp[:, q], dtb[:, 2 * k + q].rearrange("p (b o) -> p b o", o=1).to_broadcast([128, NB, 128]),
                                                         bg[:, g % 2], ALU.mult))
                        link(nc.vector.tensor_tensor(h, h, tmp[:], ALU.add))
                        for q in range(2):
                            link(nc.vector.tensor_tensor(tmp[:, q], h[:, q], cg[:, g % 2], ALU.mult))
                        link(nc.vector.tensor_reduce(ys[:, 2 * k:2 * k + 2], tmp[:], AX.X, ALU.add))
            with core.block() as block:
                @block.vector
                def _(dve):
                    link = linker(dve, dve_done)
                    for k in range(CI):
                        nc.vector.scalar_tensor_tensor(out=xbc[:, k, LP:T], in0=xbc[:, k, LP:T], scalar=par("m_d", j * CI + k), in1=ys[:, k],
                                                       op0=ALU.mult, op1=ALU.add).then_inc(*dve_done.one())
                    dve.wait_ge(*dve_done.now())
                    link(nc.vector.tensor_tensor(zT[:], zT[:], xbc[:, 0:CI], ALU.mult))
        env["norm_all"](zT, CI, lambda c: par("m_norm_g", j * CI + c), zT, n + "n")
        env["project"](zT, CI, D, env["nothing"], env["add_residual"])


def moe(env, layer):
    (nc, core, I, W, cst, par, xT, uT, scratch, linker, ident) = (
        env[k] for k in ("nc", "core", "I", "W", "cst", "par", "xT", "uT", "scratch", "linker", "ident"))
    count, bank = core.count, core.bank
    pe_done, act_done, dve_done = (count(n) for n in ("pe_done", "act_done", "dve_done"))
    misc = count("misc_dma", 16)
    n = f"e{layer}_"
    TT = 3
    tok0 = (0, 128, T - 128)
    with ExitStack() as st:
        def sb(name, shape):
            return core.sb(n + name, shape, F32, st)

        lg = sb("lg", [128, TT, 20])
        m4 = sb("m4", [128, TT, 4])
        ex = sb("ex", [128, TT, 4])
        v = sb("v", [128, TT, 8])
        le, k1, k2 = sb("le", [128, TT, 4]), sb("k1", [128, TT, 4]), sb("k2", [128, TT, 4])
        leg = sb("leg", [128, TT, 16])
        comb = sb("comb", [128, TT, 16])
        combT = sb("combT", [16, T])
        combb = sb("combb", [128, NE, T])
        d_comb = scratch("scr_comb", [16, T])

        def one(c):
            return v[:, :, c:c + 1]

        def four(c):
            return v[:, :, c:c + 1].to_broadcast([128, TT, 4])
        down = cst("four_down").rearrange("p (o e) -> p o e", o=1).to_broadcast([128, TT, 4])
        mark = {}
        with core.block() as block:
            @block.vector
            def _(dve):
                link = linker(dve, dve_done)
                TTn = nc.vector.tensor_tensor

                def first_of(mask):
                    link(TTn(mask, mask, down, ALU.mult))
                    link(nc.vector.tensor_reduce(one(7), mask, AX.X, ALU.max))
                    link(TTn(mask, mask, four(7), ALU.is_equal))
                dve.wait_ge(*pe_done.at(1))
                link(TTn(lg[:], bank[0][:, 0:96].rearrange("p (t c) -> p t c", t=TT)[:, :, 0:20],
                         par("moe_b", 20 * layer, 20).rearrange("p (o c) -> p o c", o=1).to_broadcast([128, TT, 20]), ALU.add))
                link(nc.vector.tensor_reduce(one(0), lg[:, :, 0:4], AX.X, ALU.max))
                link(TTn(ex[:], lg[:, :, 0:4], four(0), ALU.subtract))
                mark["group exponents"] = dve_done.now()
                link(TTn(m4[:], lg[:, :, 0:4], four(0), ALU.is_equal))
                first_of(m4[:])
                for t in range(TT):
                    link(TTn(leg[:, t].rearrange("p (g e) -> p g e", g=4), lg[:, t, 4:20].rearrange("p (g e) -> p g e", g=4),
                             m4[:, t].rearrange("p (g o) -> p g o", o=1).to_broadcast([128, 4, 4]), ALU.mult))
                link(nc.vector.tensor_reduce(le[:], leg[:].rearrange("p t (g e) -> p t e g", g=4), AX.X, ALU.add))
                link(nc.vector.tensor_reduce(one(1), le[:], AX.X, ALU.max))
                link(TTn(k1[:], le[:], four(1), ALU.is_equal))
                first_of(k1[:])
                link(nc.vector.scalar_tensor_tensor(out=le[:], in0=k1[:], scalar=NEG, in1=le[:], op0=ALU.mult, op1=ALU.add))
                link(nc.vector.tensor_reduce(one(2), le[:], AX.X, ALU.max))
                link(TTn(k2[:], le[:], four(2), ALU.is_equal))
                link(TTn(one(4), one(2), one(1), ALU.subtract))
                mark["second's exponent"] = dve_done.now()
                first_of(k2[:])
                dve.wait_ge(*act_done.at(2))
                link(nc.vector.tensor_reduce(one(3), ex[:], AX.X, ALU.add))
                link(nc.vector.scalar_tensor_tensor(out=one(3), in0=one(4), scalar=1.0, in1=one(3), op0=ALU.add, op1=ALU.mult))
                link(nc.vector.reciprocal(one(3), one(3)))
                link(TTn(k2[:], k2[:], four(4), ALU.mult))
                link(TTn(k1[:], k1[:], k2[:], ALU.add))
                link(TTn(k1[:], k1[:], four(3), ALU.mult))
                for t in range(TT):
                    link(TTn(comb[:, t].rearrange("p (g e) -> p g e", g=4), m4[:, t].rearrange("p (g o) -> p g o", o=1).to_broadcast([128, 4, 4]),
                             k1[:, t].rearrange("p (o e) -> p o e", o=1).to_broadcast([128, 4, 4]), ALU.mult))
                mark["combine"] = dve_done.now()
                dve.wait_ge(*pe_done.at(2))
                link(nc.vector.tensor_copy(combT[:, 0:256], bank[1][0:16, 0:256]))
                link(nc.vector.tensor_copy(combT[:, 256:T], bank[1][0:16, 376:384]))
                mark["combine turned"] = dve_done.now()

            @block.tensor
            def _(pe):
                for t in range(TT):
                    for k in range(KT):
                        mm = nc.tensor.matmul(bank[0][:, 32 * t:32 * t + 20], uT[:, k, tok0[t]:tok0[t] + 128], env["w_rt"][:, layer, k],
                                              start=(k == 0), stop=(k == KT - 1))
                mm.then_inc(*pe_done.one())
                pe.wait_ge(*mark["combine"])
                for t in range(TT):
                    mm = nc.tensor.transpose(bank[1][0:16, 128 * t:128 * t + 128], comb[:, t], ident)
                mm.then_inc(*pe_done.one())

            @block.scalar
            def _(act):
                act.wait_ge(*mark["group exponents"])
                nc.scalar.activation(ex[:], ex[:], ACT.Exp).then_inc(*act_done.one())
                act.wait_ge(*mark["second's exponent"])
                nc.scalar.activation(one(4), one(4), ACT.Exp).then_inc(*act_done.one())

            @block.gpsimd
            def _(pool):
                pool.wait_ge(*mark["combine turned"])
                pool.dma_start(d_comb, combT[:]).then_inc(*misc.one())
                pool.wait_ge(*misc.now())
                pool.dma_start(combb[:], d_comb.rearrange("(o e) t -> o e t", o=1).to_broadcast([128, NE, T])).then_inc(*misc.one())
                pool.wait_ge(*misc.now())

        hs = sb("hs", [128, 4, T])
        sl = sb("sl", [128, 2, T])
        h_filled, h_used, silu_done = count("h_filled"), count("h_used"), count("silu_done")
        weighted = count("weighted")
        y_filled, y_used = count("y_filled"), count("y_used")
        first = W.used
        slot = [(first + k) % SLOTS for k in range(6)]
        fills = [(first + k) // SLOTS for k in range(6)]
        with core.block() as block:
            @block.sync
            def _(sp):
                assert W.sent == first + 6, (W.sent, first)
                with sp.Fori(0, NE - 1) as e:
                    for k in range(6):
                        s = slot[k]
                        sp.wait_ge(W.free[s].sem, e + (fills[k] + 1))
                        if k < 4:
                            w = I[("moe_w1", "moe_w3")[k % 2]][layer, bass.ds(e + 1, 1), :, 256 * (k // 2):256 * (k // 2) + 256]
                            view = W.view(s, KT, 256)
                        else:
                            w = I["moe_w2"][layer, bass.ds(e + 1, 1), :, 512 * (k - 4):512 * (k - 4) + 512]
                            view = W.view(s, FF // 128, 512)
                        sp.dma_start(view, w.rearrange("e (k p) c -> p (e k) c", p=128)).then_inc(W.full[s].sem, 16)
                W.sent = first + 6 * NE
                W.send(sp, first + 6 * NE + SLOTS)

            @block.tensor
            def _(pe):
                with pe.Fori(0, NE) as e, h_filled.each(e, 4, NE), y_filled.each(e, 8, NE):
                    for f in range(4):
                        sa, sb_ = slot[2 * (f // 2)], slot[2 * (f // 2) + 1]
                        if f % 2 == 0:
                            pe.wait_ge(W.full[sa].sem, e * 16 + 16 * (fills[2 * (f // 2)] + 1))
                            pe.wait_ge(W.full[sb_].sem, e * 16 + 16 * (fills[2 * (f // 2) + 1] + 1))
                        pe.wait_ge(h_used.sem, e * 4 + (h_used.start + f + 1))
                        for s, b in ((sa, 0), (sb_, 2)):
                            w = W.view(s, KT, 256)
                            for k in range(KT):
                                mm = nc.tensor.matmul(bank[b + f % 2][:, 0:T], w[:, k, 128 * (f % 2):128 * (f % 2) + 128], uT[:, k],
                                                      start=(k == 0), stop=(k == KT - 1))
                        mm.then_inc(*h_filled.one())
                    pe.wait_ge(h_used.sem, e * 4 + (h_used.start + 2 + 4))
                    for c in range(8):
                        s = slot[4 + c // 4]
                        if c % 4 == 0:
                            pe.wait_ge(W.full[s].sem, e * 16 + 16 * (fills[4 + c // 4] + 1))
                        pe.wait_ge(y_used.sem, e * 8 + (y_used.start + c + 1))
                        w = W.view(s, 4, 512)
                        for f in range(4):
                            mm = nc.tensor.matmul(bank[4 + c % 4][:, 0:T], w[:, f, 128 * (c % 4):128 * (c % 4) + 128], hs[:, f], start=(f == 0),
                                                  stop=(f == 3))
                        mm.then_inc(*y_filled.one())

            @block.scalar
            def _(act):
                with act.Fori(0, NE) as e, silu_done.each(e, 4, NE):
                    for f in range(4):
                        act.wait_ge(h_filled.sem, e * 4 + (h_filled.start + f + 1))
                        if f % 2:
                            for s in slot[f - 1:f + 1]:
                                act.sem_inc(W.free[s].sem, 1)
                        act.wait_ge(weighted.sem, e * 4 + (weighted.start + f + 1))
                        nc.scalar.activation(sl[:, f % 2], bank[f % 2][:, 0:T], ACT.Silu).then_inc(*silu_done.one())

            @block.vector
            def _(dve):
                for _ in range(2):
                    dve.sem_inc(*h_used.one())
                    dve.sem_inc(*weighted.one())
                for _ in range(4):
                    dve.sem_inc(*y_used.one())
                with dve.Fori(0, NE) as e, weighted.each(e, 4, NE), h_used.each(e, 4, NE), y_used.each(e, 8, NE):
                    cb = combb[:, bass.ds(e, 1)].rearrange("p e t -> p (e t)")
                    for f in range(4):
                        dve.wait_ge(silu_done.sem, e * 4 + (silu_done.start + f + 1))
                        nc.vector.tensor_tensor(hs[:, f], sl[:, f % 2], cb, ALU.mult).then_inc(*weighted.one())
                        dve.wait_ge(*weighted.now())
                        nc.vector.tensor_tensor(hs[:, f], hs[:, f], bank[2 + f % 2][:, 0:T], ALU.mult).then_inc(*h_used.one())
                    for c in range(8):
                        dve.wait_ge(y_filled.sem, e * 8 + (y_filled.start + c + 1))
                        if c % 4 == 3:
                            dve.sem_inc(W.free[slot[4 + c // 4]].sem, 1)
                        nc.vector.tensor_tensor(xT[:, c], xT[:, c], bank[4 + c % 4][:, 0:T], ALU.add).then_inc(*y_used.one())
        W.used += 6 * NE


def nsa_layer(env):
    (nc, core, I, O, W, cst, par, xT, uT, eps, scratch, linker, ident, ones) = (
        env[k] for k in ("nc", "core", "I", "O", "W", "cst", "par", "xT", "uT", "eps", "scratch", "linker", "ident", "ones"))
    count, bank = core.count, core.bank
    pe_done, act_done, dve_done, pool_done = (count(n) for n in ("pe_done", "act_done", "dve_done", "pool_done"))
    misc, out_sent, in_loaded, pool_sent = count("misc_dma", 16), count("out_sent", 16), count("in_loaded", 16), count("pool_sent", 16)
    ones64 = cst("ones64")
    V = nc.vector
    with ExitStack() as layer:
        def sb(name, shape, dt=F32, ctx=layer):
            return core.sb("n_" + name, shape, dt, ctx)

        qT = sb("qT", [128, 8, T])
        kvT = sb("kvT", [128, 12, T])
        glT = sb("glT", [48, T])
        cw2 = sb("cw2", [64, 2, 64])
        rel = sb("rel", [32, 8, 16])
        onehots = sb("onehots", [32, NSTRIP + PAST + 1])
        pages = sb("pages", [1, 64], I32)
        pebias = sb("pebias", [64, 2])
        cw1 = sb("cw1", [128, 2, 8, 2, 64])
        d_strip, d_gl = scratch("scr_strip", [16, NSTRIP]), scratch("scr_gl", [48, NB])
        with core.block() as block:
            @block.gpsimd
            def _(pool):
                for dst, src in ((cw2[:], I["cmp_w2"]), (cw1[:], I["cmp_w1"]), (onehots[:], I["onehots"]), (pages[:], I["pages"]),
                                 (rel[:], I["rel"].rearrange("r (o h) -> r o h", o=1).to_broadcast([32, 8, 16]))):
                    pool.dma_start(dst, src).then_inc(*misc.one())
                pool.wait_ge(*misc.now())

        def act_step(act, t, ps):
            if t < 8:
                return nc.scalar.copy(qT[:, t], ps[:, 0:T])
            if t < 20:
                return nc.scalar.copy(kvT[:, t - 8], ps[:, 0:T])
            return nc.scalar.activation(glT[:], ps[0:48, 0:T], ACT.Sigmoid)

        env["project"](uT, KT, 2560, act_step, lambda eng, t, ps: None, extra=(env["w_gl"], 48))
        jobs = [(qT[:, c], qT[:, c], par("q_g"), 1.0, eps[:, 1:2]) for c in range(8)]
        jobs += [(kvT[:, c], kvT[:, c], par("k_g", b), 1 / 64, eps[:, 0:1]) for c, b in ((4, 1), (5, 1), (8, 2), (9, 2))]
        env["norm_each"](jobs, ones64, "nq")

        with ExitStack() as st:
            kcs = sb("kcs", [128, 2, 512], ctx=st)
            vcs = sb("vcs", [128, 4, 256], ctx=st)
            vnew = sb("vnew", [8, 2, 2, 128], ctx=st)
            dbias = sb("dbias", [128, PAST + 1], ctx=st)
            gdec = sb("gdec", [128, 3], ctx=st)
            page = sb("page", [128, 2, NPAGE, 512], ctx=st)
            page_in = [count(f"page_in{b}", 16) for b in range(2)]
            with ExitStack() as st2:
                hid = sb("hid", [64, 2, 4, NB, 64], ctx=st2)
                half0 = sb("half0", [64, 2, 4, 64], ctx=st2)
                hidden = count("hidden_done")
                def load_pages(sp, cache, cols, before):
                    for b in range(NB):
                        if b >= 2:
                            sp.wait_ge(*before(b - 1))
                        with sp.Fori(0, NPAGE) as k:
                            v = sp.value_load(pages[0:1, bass.ds(k + NPAGE * b, 1)], min_val=0, max_val=cache.shape[0] - 1)
                            sp.dma_start(page[:, b % 2, bass.ds(k, 1), cols], cache[bass.ds(v, 1), :, cols].rearrange("n p c -> p n c")) \
                                .then_inc(page_in[b % 2].sem, 16)
                        page_in[b % 2].n += 16 * NPAGE

                with core.block() as block:
                    @block.sync
                    def _(sp):
                        sp.dma_start(O["kvT"], kvT[:]).then_inc(*out_sent.one())
                        sp.dma_start(O["win_old"], I["win_rows"][:, 1:512]).then_inc(*out_sent.one())
                        load_pages(sp, I["cache_cmp"], slice(0, 512), lambda b: pe_done.at(2 + 2 * b))

                    @block.tensor
                    def _(pe):
                        for kv in range(2):
                            for h in range(2):
                                for r in range(8):
                                    mm = nc.tensor.matmul(bank[4][0:64, kv:kv + 1], cw1[:, kv, r, h], par("pe", 16 * kv + 8 * h + r),
                                                          start=(h + r == 0), stop=(h == 1 and r == 7))
                        mm.then_inc(*pe_done.one())
                        for br in range(2):
                            for p in range(2):
                                k = 2 * br + p
                                mm = nc.tensor.transpose(bank[5][0:8, 128 * k:128 * k + 128], kvT[:, 6 + 4 * br + p, LP:T], ident)
                        for k in range(2):
                            nc.tensor.matmul(bank[6 + k][:], rel[:].rearrange("r b h -> r (b h)"), onehots[:, NSTRIP + 512 * k:NSTRIP + 512 * k + 512],
                                             start=True, stop=True)
                        mm = nc.tensor.matmul(bank[4][:, 8:9], rel[:].rearrange("r b h -> r (b h)"), onehots[:, NSTRIP + PAST:NSTRIP + PAST + 1],
                                              start=True, stop=True)
                        mm.then_inc(*pe_done.one())
                        for b in range(NB):
                            pe.wait_ge(page_in[b % 2].sem, page_in[b % 2].start + 16 * NPAGE * (b // 2 + 1))
                            for kv in range(2):
                                if b >= 2:
                                    pe.wait_ge(*hidden.at(2 * (b - 2) + kv + 1))
                                x = page[:, b % 2].rearrange("p n (v r g c) -> p v r g n c", v=2, r=8, g=4)[:, kv]
                                for r in range(8):
                                    mm = nc.tensor.matmul(bank[2 * (b % 2) + kv][:, 0:256], cw1[:, kv, r].rearrange("p h e -> p (h e)"), x[:, r],
                                                          start=(r == 0), stop=(r == 7))
                                mm.then_inc(*pe_done.one())

                    @block.scalar
                    def _(act):
                        act.wait_ge(*dve_done.at(1))
                        for b in range(NB):
                            for kv in range(2):
                                k = 2 * b + kv
                                act.wait_ge(*pe_done.at(3 + k))
                                if k >= 2:
                                    act.wait_ge(*hidden.at(k - 1))
                                nc.scalar.copy(half0[:, kv], bank[2 * (b % 2) + kv][0:64, 0:256].rearrange("p (g c) -> p g c", g=4)).then_inc(*act_done.one())
                                act.wait_ge(*hidden.at(k + 1))
                                h = hid[:, kv, :, b, 0:NCMP]
                                nc.scalar.activation(h, h, ACT.Silu, bias=pebias[:, kv:kv + 1]).then_inc(*act_done.one())

                    @block.vector
                    def _(dve):
                        dve.wait_ge(*pe_done.at(2))
                        V.tensor_copy(pebias[:], bank[4][0:64, 0:2]).then_inc(*dve_done.one())
                        V.memset(hid[:, :, :, :, NCMP:64], 0.0).then_inc(*dve_done.one())
                        V.tensor_copy(vnew[:], bank[5][0:8].rearrange("p (a b c) -> p a b c", a=2, b=2)).then_inc(*dve_done.one())
                        for k in range(2):
                            V.tensor_copy(dbias[:, 512 * k:512 * k + 512], bank[6 + k][:]).then_inc(*dve_done.one())
                        V.tensor_copy(dbias[:, PAST:PAST + 1], bank[4][:, 8:9]).then_inc(*dve_done.one())
                        for b in range(NB):
                            for kv in range(2):
                                k = 2 * b + kv
                                dve.wait_ge(*act_done.at(2 * k + 1))
                                V.tensor_tensor(hid[:, kv, :, b, 0:NCMP], half0[:, kv, :, 0:NCMP],
                                                bank[2 * (b % 2) + kv][64:128, 0:256].rearrange("p (g c) -> p g c", g=4)[:, :, 1:64],
                                                ALU.add).then_inc(*hidden.one())

                    @block.gpsimd
                    def _(pool):
                        pool.dma_start(d_gl, glT[:, LP:T]).then_inc(*pool_sent.one())
                        pool.wait_ge(*pool_sent.now())
                        for b in range(NB):
                            src = bass.AP(d_gl.tensor, b, [[NB, 16], [16 * NB, 3]])
                            pool.dma_start(gdec[16 * b:16 * b + 16, :], src, allow_slow_non_contiguous=True).then_inc(*misc.one())
                        pool.wait_ge(*misc.now())

                with ExitStack() as st3:
                    kc = sb("kc", [64, 4, 512], ctx=st3)
                    sq = sb("sq", [64, 4, 512], ctx=st3)
                    rs = sb("rs", [64, 4, 512], ctx=st3)
                    with core.block() as block:
                        @block.tensor
                        def _(pe):
                            for g in range(4):
                                nc.tensor.matmul(bank[g][0:64, :], cw2[:, 0], hid[:, 0, g].rearrange("p b c -> p (b c)"), start=True,
                                                 stop=True).then_inc(*pe_done.one())
                            for q in range(4):
                                for g in range(4):
                                    mm = nc.tensor.matmul(bank[4 + q][:, 64 * g:64 * g + 64], hid[:, 1, g, 2 * q:2 * q + 2].rearrange("p b c -> p (b c)"),
                                                          cw2[:, 1], start=True, stop=True)
                                mm.then_inc(*pe_done.one())
                            for g in range(4):
                                pe.wait_ge(*act_done.at(2 * g + 2))
                                nc.tensor.matmul(bank[g][0:64, :], ones64[0:64, 0:64], sq[:, g], start=True, stop=True).then_inc(*pe_done.one())

                        @block.scalar
                        def _(act):
                            for g in range(4):
                                act.wait_ge(*pe_done.at(g + 1))
                                nc.scalar.copy(kc[:, g], bank[g][0:64, :]).then_inc(*act_done.one())
                                nc.scalar.activation(sq[:, g], bank[g][0:64, :], ACT.Square).then_inc(*act_done.one())
                            for g in range(4):
                                act.wait_ge(*pe_done.at(9 + g))
                                nc.scalar.activation(rs[:, g], bank[g][0:64, :], ACT.Sqrt, bias=eps[0:64, 0:1], scale=1 / 64).then_inc(*act_done.one())

                        @block.vector
                        def _(dve):
                            for q in range(4):
                                dve.wait_ge(*pe_done.at(5 + q))
                                V.tensor_copy(vcs[:, q], bank[4 + q][:, 0:256]).then_inc(*dve_done.one())
                            for g in range(4):
                                dve.wait_ge(*act_done.at(9 + g))
                                V.reciprocal(rs[:, g], rs[:, g]).then_inc(*dve_done.one())
                                dve.wait_ge(*dve_done.now())
                                V.scalar_tensor_tensor(out=kcs[64 * (g % 2):64 * (g % 2) + 64, g // 2], in0=kc[:, g], scalar=par("k_g", 0)[0:64],
                                                       in1=rs[:, g], op0=ALU.mult, op1=ALU.mult).then_inc(*dve_done.one())

            qblk = sb("qblk", [128, 2, NB, 128], ctx=st)
            pc = sb("pc", [128, 2, 64], ctx=st)
            pcg = sb("pcg", [128, 2, 64], ctx=st)
            pcT = sb("pcT", [128, 2, 128], ctx=st)
            imp = sb("imp", [128, 6, NSEL], ctx=st)
            st_ = sb("stat", [128, 16], ctx=st)
            ss = sb("ss", [128, PAST + 1], ctx=st)
            sw = sb("sw", [128, 513], ctx=st)
            pT = sb("pT", [128, 12, 128], ctx=st)
            dg = sb("dg", [128, 2, 128], ctx=st)
            pn = sb("pn", [8, 2, 128], ctx=st)
            kbuf = page[:].rearrange("p b n (h c) -> p b h n c", h=2)

            def stream(sp, half, before):
                cols = slice(256 * half, 256 * half + 256)
                for u in range(2 * NB):
                    b = u % NB
                    if u >= 2:
                        sp.wait_ge(*before(u - 2))
                    if u < NB:
                        with sp.Fori(0, NPAGE) as k:
                            v = sp.value_load(pages[0:1, bass.ds(k + NPAGE * b, 1)], min_val=0, max_val=I["cache_sel"].shape[0] - 1)
                            sp.dma_start(page[:, u % 2, bass.ds(k, 1), cols], I["cache_sel"][bass.ds(v, 1), :, cols].rearrange("n p c -> p n c")) \
                                .then_inc(page_in[u % 2].sem, 16)
                        page_in[u % 2].n += 16 * NPAGE
                    else:
                        sp.dma_start(page[:, u % 2, 0:4, cols], I["cache_win"][b, :, :, cols]).then_inc(*page_in[u % 2].one())

            def streamed(u):
                c = page_in[u % 2]
                return c.sem, c.start + 16 * (NPAGE * min(u // 2 + 1, 4) + max(u // 2 - 3, 0))

            mark = {}
            with core.block() as block:
                @block.sync
                def _(sp):
                    stream(sp, 0, lambda u: pe_done.at(u + 1))

                @block.vector
                def _(dve):
                    link = linker(dve, dve_done)
                    link(V.memset(qblk[:], 0.0))
                    flat = qblk[:].rearrange("p a b c -> p a (b c)")
                    for p in range(2):
                        for h in range(4):
                            for g2 in range(2):
                                o = 8 * p + 2 * h + g2
                                ins = V.tensor_copy(flat[64 * g2:64 * g2 + 64, p, o:o + 144 * 7 + 1:144], qT[64 * g2:64 * g2 + 64, 4 * p + h, LP:T])
                                ins.then_inc(*dve_done.one())
                    mark["qblk"] = dve_done.now()

                @block.tensor
                def _(pe):
                    pe.wait_ge(*mark["qblk"])
                    for u in range(2 * NB):
                        b = u % NB
                        pe.wait_ge(*streamed(u))
                        for p in range(2):
                            st0, sp0 = (b == 0 and p == 0), (b == NB - 1 and p == 1)
                            k = page[:, u % 2].rearrange("p n (h a r) -> p h a n r", h=2, a=2)[:, 0, p]
                            kw = dict(start=st0, stop=sp0, skip_group_check=True)
                            if u < NB:
                                for i in range(2):
                                    nc.tensor.matmul(bank[i][:], qblk[:, p, b], k[:, 4 * i:4 * i + 4], **kw)
                                mm = nc.tensor.matmul(bank[3][:, 0:1], qblk[:, p, b], kvT[:, 4 + p, LP + b:LP + b + 1], **kw)
                            else:
                                nc.tensor.matmul(bank[2][:], qblk[:, p, b], page[:, u % 2, 0:4, 128 * p:128 * p + 128], **kw)
                                mm = nc.tensor.matmul(bank[4][:, 0:1], qblk[:, p, b], kvT[:, 8 + p, LP + b:LP + b + 1], **kw)
                        mm.then_inc(*pe_done.one())
                    for b in range(NB):
                        for p in range(2):
                            mm = nc.tensor.matmul(bank[5][:, 0:64], qblk[:, p, b], kcs[:, p, 64 * b:64 * b + 64], start=(b + p == 0),
                                                  stop=(b == NB - 1 and p == 1), skip_group_check=True)
                    mm.then_inc(*pe_done.one())

            with core.block() as block:
                @block.vector
                def _(dve):
                    link = linker(dve, dve_done)
                    c63 = pc[:, 0, 0:NCMP]
                    link(V.memset(pc[:], 0.0))
                    link(V.tensor_tensor(c63, bank[5][:, 0:NCMP], dbias[:, 31:31 + 16 * 62 + 1:16], ALU.add))
                    link(V.tensor_reduce(st_[:, 0:1], c63, AX.X, ALU.max))
                    link(V.tensor_scalar(st_[:, 0:1], st_[:, 0:1], -1.0, None, ALU.mult))
                    mark["cmp max"] = dve_done.now()
                    for k in range(2):
                        V.tensor_tensor(ss[:, 512 * k:512 * k + 512], bank[k][:], dbias[:, 512 * k:512 * k + 512], ALU.add).then_inc(*dve_done.one())
                    V.tensor_tensor(ss[:, PAST:PAST + 1], bank[3][:, 0:1], dbias[:, PAST:PAST + 1], ALU.add).then_inc(*dve_done.one())
                    V.tensor_tensor(sw[:, 0:512], bank[2][:], dbias[:, 512:PAST], ALU.add).then_inc(*dve_done.one())
                    link(V.tensor_tensor(sw[:, 512:513], bank[4][:, 0:1], dbias[:, PAST:PAST + 1], ALU.add))
                    link(V.tensor_reduce(st_[:, 2:3], sw[:], AX.X, ALU.max))
                    link(V.tensor_scalar(st_[:, 2:3], st_[:, 2:3], -1.0, None, ALU.mult))
                    mark["win max"] = dve_done.now()
                    dve.wait_ge(*act_done.at(1))
                    link(V.reciprocal(st_[:, 4:5], st_[:, 3:4]))
                    link(V.tensor_scalar(c63, c63, st_[:, 4:5], None, ALU.mult))
                    link(V.tensor_copy(pc[:, 1], pc[:, 0]))
                    link(V.tensor_scalar(pcg[:], pc[:], gdec[:, 0:1], None, ALU.mult))
                    mark["pc"] = dve_done.now()
                    dve.wait_ge(*pe_done.at(1))
                    link(V.tensor_copy(pcT[:, 0], bank[5][:, 0:128]))
                    link(V.memset(pcT[:, 1], 0.0))
                    for k in range(2):
                        o = pcT[64 * k:64 * k + 64, 1].rearrange("p (b s h) -> p s b h", s=2, h=16)[:, k]
                        link(V.tensor_copy(o, bank[5][64 * k:64 * k + 64, 128:256].rearrange("p (b s h) -> p s b h", s=2, h=16)[:, k]))
                    mark["pcT"] = dve_done.now()
                    dve.wait_ge(*pe_done.at(2))
                    link(V.tensor_copy(imp[:, 0], bank[6][:, 0:NSEL]))
                    mark["imp of heads"] = dve_done.now()
                    dve.wait_ge(*pe_done.at(3))
                    link(V.tensor_tensor(imp[:, 1], bank[6][:, 32:32 + NSEL], cst("forced"), ALU.add))
                    link(V.tensor_reduce(st_[:, 5:6], imp[:, 1], AX.X, ALU.min))
                    link(V.tensor_scalar(imp[:, 2], imp[:, 1], st_[:, 5:6], None, ALU.is_equal))
                    link(V.tensor_tensor(imp[:, 2], imp[:, 2], cst("block_no"), ALU.mult))
                    link(V.tensor_reduce(st_[:, 6:7], imp[:, 2], AX.X, ALU.max))
                    link(V.tensor_scalar(imp[:, 3], cst("block_no"), st_[:, 6:7], NEG, ALU.is_equal, ALU.mult))
                    blocks = ss[:, 0:PAST].rearrange("p (j r) -> p j r", r=64)
                    link(V.tensor_tensor(blocks, blocks, imp[:, 3, 0:16].rearrange("p (j o) -> p j o", o=1).to_broadcast([128, 16, 64]), ALU.add))
                    link(V.tensor_reduce(st_[:, 1:2], ss[:], AX.X, ALU.max))
                    link(V.tensor_scalar(st_[:, 1:2], st_[:, 1:2], -1.0, None, ALU.mult))
                    mark["sel max"] = dve_done.now()
                    dve.wait_ge(*act_done.at(2))
                    link(V.reciprocal(st_[:, 8:9], st_[:, 7:8]))
                    link(V.tensor_scalar(sw[:], sw[:], st_[:, 8:9], gdec[:, 2:3], ALU.mult, ALU.mult))
                    link(V.tensor_scalar(dg[:, 1], ident, sw[:, 512:513], None, ALU.mult))
                    mark["win weights"] = dve_done.now()
                    dve.wait_ge(*act_done.at(3))
                    link(V.reciprocal(st_[:, 10:11], st_[:, 9:10]))
                    link(V.tensor_scalar(ss[:], ss[:], st_[:, 10:11], gdec[:, 1:2], ALU.mult, ALU.mult))
                    link(V.tensor_scalar(dg[:, 0], ident, ss[:, PAST:PAST + 1], None, ALU.mult))
                    mark["sel weights"] = dve_done.now()
                    for k, b in ((2, 2), (0, 0), (1, 1)):
                        dve.wait_ge(*pe_done.at(4 if k == 2 else 5))
                        link(V.tensor_copy(pT[:, 4 * k:4 * k + 4].rearrange("p a b -> p (a b)"), bank[b][:]))
                    link(V.tensor_copy(pn[:].rearrange("p a b -> p (a b)"), bank[3][0:8, 0:256]))

                @block.scalar
                def _(act):
                    act.wait_ge(*mark["cmp max"])
                    nc.scalar.activation(pc[:, 0, 0:NCMP], pc[:, 0, 0:NCMP], ACT.Exp, bias=st_[:, 0:1], accum_out=st_[:, 3:4]).then_inc(*act_done.one())
                    act.wait_ge(*mark["win max"])
                    nc.scalar.activation(sw[:], sw[:], ACT.Exp, bias=st_[:, 2:3], accum_out=st_[:, 7:8]).then_inc(*act_done.one())
                    act.wait_ge(*mark["sel max"])
                    nc.scalar.activation(ss[:], ss[:], ACT.Exp, bias=st_[:, 1:2], accum_out=st_[:, 9:10]).then_inc(*act_done.one())

                @block.tensor
                def _(pe):
                    pe.wait_ge(*mark["pc"])
                    nc.tensor.transpose(bank[5][:, 0:128], pc[:].rearrange("p a b -> p (a b)"), ident)
                    nc.tensor.transpose(bank[5][:, 128:256], pcg[:].rearrange("p a b -> p (a b)"), ident).then_inc(*pe_done.one())
                    pe.wait_ge(*mark["pcT"])
                    nc.tensor.matmul(bank[6][:, 0:NSEL], pcT[0:64, 0], cst("overlap")[0:64], start=True, stop=True).then_inc(*pe_done.one())
                    pe.wait_ge(*mark["imp of heads"])
                    nc.tensor.matmul(bank[6][:, 32:32 + NSEL], cst("same_group"), imp[:, 0], start=True, stop=True).then_inc(*pe_done.one())
                    pe.wait_ge(*mark["win weights"])
                    for k in range(4):
                        mm = nc.tensor.transpose(bank[2][:, 128 * k:128 * k + 128], sw[:, 128 * k:128 * k + 128], ident)
                    mm.then_inc(*pe_done.one())
                    pe.wait_ge(*mark["sel weights"])
                    for k in range(8):
                        nc.tensor.transpose(bank[k // 4][:, 128 * (k % 4):128 * (k % 4) + 128], ss[:, 128 * k:128 * k + 128], ident)
                    for k in range(2):
                        mm = nc.tensor.matmul(bank[3][0:8, 128 * k:128 * k + 128], cst("of_seq"), dg[:, k], start=True, stop=True)
                    mm.then_inc(*pe_done.one())

            with core.block() as block:
                @block.sync
                def _(sp):
                    stream(sp, 1, lambda u: pe_done.at(u + 1))

                @block.tensor
                def _(pe):
                    kw = dict(stop=False, skip_group_check=True)
                    for p in range(2):
                        for br in range(2):
                            nc.tensor.matmul(bank[6 + p][:, 0:128], vnew[:, br, p], pn[:, br], start=(br == 0), **kw)
                        for q in range(4):
                            nc.tensor.matmul(bank[6 + p][:, 32 * q:32 * q + 32], vcs[:, q, 128 * p:128 * p + 128], pcT[:, 1, 32 * q:32 * q + 32],
                                             start=False, **kw)
                    for u in range(2 * NB):
                        b = u % NB
                        pe.wait_ge(*streamed(u))
                        n, k0 = (8, 0) if u < NB else (4, 8)
                        for p in range(2):
                            for k in range(n):
                                mm = nc.tensor.matmul(bank[6 + p][:, 16 * b:16 * b + 16], page[:, u % 2, k, 256 + 128 * p:384 + 128 * p],
                                                      pT[:, k0 + k, 16 * b:16 * b + 16], start=False,
                                                      stop=(u == 2 * NB - 1 and k == n - 1), skip_group_check=True)
                        mm.then_inc(*pe_done.one())

                @block.vector
                def _(dve):
                    dve.wait_ge(*pe_done.at(2 * NB))
                    for p in range(2):
                        for g2 in range(2):
                            src = bank[6 + p][64 * g2:64 * g2 + 64, 0:128].rearrange("p (b a h g) -> p a g h b", a=2, h=4, g=2)[:, p, g2]
                            V.tensor_copy(uT[64 * g2:64 * g2 + 64, 4 * p:4 * p + 4, LP:T], src).then_inc(*dve_done.one())

        with ExitStack() as st:
            bias = sb("bias", [128, 2, 16, LP], ctx=st)
            qR = sb("qR", [128, 2, 8, 128], ctx=st)
            gR = sb("gR", [48, 2, 128], ctx=st)
            strip = sb("strip", [16, NSTRIP], ctx=st)
            vn = sb("vn", [128, 2, 2, 256], ctx=st)
            gate = sb("gate", [128, 2, 48], ctx=st)
            oacc = sb("oacc", [128, 2, D], ctx=st)
            hidp = sb("hidp", [64, 2, 4, 16], ctx=st)
            kcp = sb("kcp", [128, 2, 16], ctx=st)
            kk = sb("kk", [64, 3, 64], ctx=st)
            vblk = sb("vblk", [128, 4, 4, 64], ctx=st)
            with ExitStack() as st2:
                w1d = sb("w1d", [128, 2, 32, 64], ctx=st2)
                with core.block() as block:
                    @block.gpsimd
                    def _(pool):
                        pool.dma_start(w1d[:], I["cmp_w1d"]).then_inc(*misc.one())
                        pool.wait_ge(*misc.now())
                        pool.wait_ge(*dve_done.at(6))
                        pool.dma_start(d_strip, strip[:]).then_inc(*pool_sent.one())
                        pool.wait_ge(*pool_sent.now())
                        for t in range(2):
                            src = bass.AP(d_strip.tensor, 128 - 128 * t, [[1, 128], [NSTRIP, 16], [1, LP]])
                            pool.dma_start(bias[:, t], src).then_inc(*misc.one())
                        pool.wait_ge(*misc.now())

                    @block.tensor
                    def _(pe):
                        nc.tensor.matmul(bank[0][0:16, :], rel[:, 0], onehots[:, 0:NSTRIP], start=True, stop=True).then_inc(*pe_done.one())
                        for br in range(2):
                            for t in range(2):
                                for p in range(2):
                                    k = 2 * t + p
                                    mm = nc.tensor.transpose(bank[1 + br][:, 128 * k:128 * k + 128], kvT[:, 6 + 4 * br + p, 128 * t:128 * t + 128], ident)
                        pe.wait_ge(*dve_done.at(4))
                        for t in range(2):
                            mm = nc.tensor.transpose(bank[3][:, 48 * t:48 * t + 48], gR[:, t], ident[0:48, 0:48])
                        mm.then_inc(*pe_done.one())
                        pe.wait_ge(*misc.at(1))
                        for kv in range(2):
                            for g2 in range(2):
                                rows = slice(64 * g2, 64 * g2 + 64)
                                for r in range(32):
                                    mm = nc.tensor.matmul(bank[4 + 2 * kv + g2][0:64, 0:30], w1d[rows, kv, r],
                                                          kvT[rows, 2 * kv:2 * kv + 2, r:r + 16 * 14 + 1:16], start=(r == 0), stop=(r == 31))
                                mm.then_inc(*pe_done.one())
                        pe.wait_ge(*act_done.at(4))
                        nc.tensor.matmul(bank[0][0:64, 0:64], cw2[:, 0], hidp[:, 0].rearrange("p g c -> p (g c)"), start=True, stop=True) \
                            .then_inc(*pe_done.one())
                        for g in range(4):
                            mm = nc.tensor.matmul(bank[1][0:16, 64 * g:64 * g + 64], hidp[:, 1, g], cw2[:, 1], start=True, stop=True)
                        mm.then_inc(*pe_done.one())
                        pe.wait_ge(*act_done.at(6))
                        nc.tensor.matmul(bank[2][0:64, 0:64], ones64[0:64, 0:64], kk[:, 1], start=True, stop=True).then_inc(*pe_done.one())

                    @block.scalar
                    def _(act):
                        for kv in range(2):
                            for g2 in range(2):
                                act.wait_ge(*pe_done.at(3 + 2 * kv + g2))
                                act.wait_ge(*dve_done.at(10))
                                nc.scalar.activation(hidp[:, kv, g2:4:2, 0:NCMPP], bank[4 + 2 * kv + g2][0:64, 0:30].rearrange("p (a c) -> p a c", a=2),
                                                     ACT.Silu, bias=pebias[:, kv:kv + 1]).then_inc(*act_done.one())
                        act.wait_ge(*pe_done.at(7))
                        nc.scalar.copy(kk[:, 0], bank[0][0:64, 0:64]).then_inc(*act_done.one())
                        nc.scalar.activation(kk[:, 1], bank[0][0:64, 0:64], ACT.Square).then_inc(*act_done.one())
                        act.wait_ge(*pe_done.at(9))
                        nc.scalar.activation(kk[:, 2], bank[2][0:64, 0:64], ACT.Sqrt, bias=eps[0:64, 0:1], scale=1 / 64).then_inc(*act_done.one())

                    @block.vector
                    def _(dve):
                        link = linker(dve, dve_done)
                        for t in range(2):
                            back = slice(127, None, -1) if t == 0 else slice(255, 127, -1)
                            V.tensor_copy(qR[:, t], qT[:, :, back]).then_inc(*dve_done.one())
                            V.tensor_copy(gR[:, t], glT[:, back]).then_inc(*dve_done.one())
                        dve.wait_ge(*pe_done.at(1))
                        link(V.tensor_copy(strip[:, 0:LP], bank[0][0:16, 0:LP]))
                        link(V.memset(strip[:, LP:NSTRIP], NEG))
                        dve.wait_ge(*pe_done.at(2))
                        for br in range(2):
                            V.tensor_copy(vn[:, br].rearrange("p t c -> p (t c)"), bank[1 + br][:]).then_inc(*dve_done.one())
                        V.tensor_copy(gate[:].rearrange("p t c -> p (t c)"), bank[3][:, 0:96]).then_inc(*dve_done.one())
                        link(V.memset(hidp[:], 0.0))
                        link(V.memset(vblk[:], 0.0))
                        dve.wait_ge(*pe_done.at(8))
                        for g in range(4):
                            for h in range(4):
                                V.tensor_copy(vblk[32 * h:32 * h + 16, g, h], bank[1][0:16, 64 * g:64 * g + 64]).then_inc(*dve_done.one())
                        dve.wait_ge(*act_done.at(7))
                        link(V.reciprocal(kk[:, 2], kk[:, 2]))
                        for g in range(4):
                            V.scalar_tensor_tensor(out=kcp[64 * (g % 2):64 * (g % 2) + 64, g // 2], in0=kk[:, 0, 16 * g:16 * g + 16],
                                                   scalar=par("k_g", 0)[0:64], in1=kk[:, 2, 16 * g:16 * g + 16], op0=ALU.mult,
                                                   op1=ALU.mult).then_inc(*dve_done.one())

            with ExitStack() as st2:
                sc = sb("sc", [128, 2, 16, 16], ctx=st2)
                p32 = sb("p32", [128, 2, 4, 4, 32], ctx=st2)
                p32T = sb("p32T", [128, 2, 4, 128], ctx=st2)
                s1 = sb("s1", [128, 2, 16, 2], ctx=st2)
                mark = {}
                with core.block() as block:
                    @block.vector
                    def _(dve):
                        link = linker(dve, dve_done)
                        link(V.memset(sc[:], NEG))
                        link(V.memset(p32[:], 0.0))
                        dve.wait_ge(*pe_done.at(1))
                        for t in range(2):
                            for g2 in range(2):
                                link(V.tensor_tensor(sc[:, t, g2:16:2, 0:NCMPP], bank[7 * g2][:, 128 * t:128 * t + 128].rearrange("p (h c) -> p h c", h=8)[:, :, 0:NCMPP],
                                                     bias[:, t, g2:16:2, 31:LP:16], ALU.add))
                        link(V.tensor_reduce(s1[:, :, :, 0], sc[:], AX.X, ALU.max))
                        for t in range(2):
                            link(V.tensor_tensor(sc[:, t], sc[:, t], s1[:, t, :, 0:1].to_broadcast([128, 16, 16]), ALU.subtract))
                        mark["shifted"] = dve_done.now()
                        dve.wait_ge(*act_done.at(1))
                        for t in range(2):
                            link(V.tensor_tensor(sc[:, t], sc[:, t], cst("cmp_valid")[:, 16 * t:16 * t + 16].rearrange("p (o c) -> p o c", o=1)
                                                 .to_broadcast([128, 16, 16]), ALU.mult))
                        link(V.tensor_reduce(s1[:, :, :, 0], sc[:], AX.X, ALU.add))
                        link(V.tensor_scalar(s1[:, :, :, 0], s1[:, :, :, 0], 1e-30, None, ALU.max))
                        link(V.reciprocal(s1[:, :, :, 1], s1[:, :, :, 0]))
                        for t in range(2):
                            link(V.tensor_tensor(s1[:, t, :, 1], s1[:, t, :, 1], gate[:, t, 0:16], ALU.mult))
                            for g in range(4):
                                hd = slice(8 * (g // 2) + g % 2, 8 * (g // 2) + g % 2 + 7, 2)
                                link(V.tensor_tensor(p32[:, t, g, :, 0:16], sc[:, t, hd], s1[:, t, hd, 1:2].to_broadcast([128, 4, 16]), ALU.mult))
                        mark["weights"] = dve_done.now()
                        for t in range(2):
                            dve.wait_ge(*pe_done.at(2 + t))
                            link(V.tensor_copy(p32T[:, t].rearrange("p g q -> p (g q)"), bank[1 + t][:]))
                        mark["turned"] = dve_done.now()
                        for t in range(2):
                            for g in range(4):
                                dve.wait_ge(*pe_done.at(4 + 2 * t + g // 2))
                                V.tensor_copy(oacc[:, t].rearrange("p (a h b d) -> p a b h d", a=2, h=4, b=2)[:, g // 2, g % 2],
                                              bank[3 + 2 * t + g // 2][:, 256 * (g % 2):256 * (g % 2) + 256].rearrange("p (h d) -> p h d", h=4)) \
                                    .then_inc(*dve_done.one())

                    @block.scalar
                    def _(act):
                        act.wait_ge(*mark["shifted"])
                        nc.scalar.activation(sc[:], sc[:], ACT.Exp).then_inc(*act_done.one())

                    @block.tensor
                    def _(pe):
                        for t in range(2):
                            for hd in range(16):
                                p, h, g2 = hd // 8, hd % 8 // 2, hd % 2
                                rows = slice(64 * g2, 64 * g2 + 64)
                                o = 128 * t + 16 * (hd // 2)
                                mm = nc.tensor.matmul(bank[7 * g2][:, o:o + 16], qR[rows, t, 4 * p + h], kcp[rows, p], start=True, stop=True)
                        mm.then_inc(*pe_done.one())
                        pe.wait_ge(*mark["weights"])
                        for t in range(2):
                            for g in range(4):
                                mm = nc.tensor.transpose(bank[1 + t][:, 128 * g:128 * g + 128], p32[:, t, g].rearrange("p h c -> p (h c)"), ident)
                            mm.then_inc(*pe_done.one())
                        pe.wait_ge(*mark["turned"])
                        for t in range(2):
                            for g in range(4):
                                mm = nc.tensor.matmul(bank[3 + 2 * t + g // 2][:, 256 * (g % 2):256 * (g % 2) + 256], p32T[:, t, g],
                                                      vblk[:, g].rearrange("p h d -> p (h d)"), start=True, stop=True)
                                if g % 2:
                                    mm.then_inc(*pe_done.one())

            with ExitStack() as st2:
                s = sb("s", [128, 2, 4, LP], ctx=st2)
                pt = sb("pt", [128, 4, 2, 128], ctx=st2)
                stt = sb("stt", [128, 2, 3, 4], ctx=st2)
                ot = sb("ot", [128, 4, 64], ctx=st2)
                units = [(br, t, g) for br in range(2) for t in range(2) for g in range(4)]
                n = len(units)
                s_filled, s_ready, p_ready = count("s_filled"), count("s_ready"), count("p_ready")
                pt_filled, pt_copied, o_filled, o_added = count("pt_filled"), count("pt_copied"), count("o_filled"), count("o_added")
                with core.block() as block:
                    @block.tensor
                    def _(pe):
                        for u in range(n + 1):
                            if u < n:
                                br, t, g = units[u]
                                p, rows = g // 2, slice(64 * (g % 2), 64 * (g % 2) + 64)
                                if u >= 2:
                                    pe.wait_ge(*s_ready.at(u - 1))
                                for h in range(4):
                                    mm = nc.tensor.matmul(bank[2 * (u % 2) + h // 2][:, 256 * (h % 2):256 * (h % 2) + 256],
                                                          qR[rows, t, 4 * p + h], kvT[rows, 4 + 4 * br + p, 0:LP], start=True, stop=True)
                                mm.then_inc(*s_filled.one())
                            if u >= 1:
                                br, t, g = units[u - 1]
                                pe.wait_ge(*p_ready.at(u))
                                if u >= 2:
                                    pe.wait_ge(*pt_copied.at(u - 1))
                                for h in range(4):
                                    for k in range(t + 1):
                                        o = 256 * (h % 2) + 128 * k
                                        mm = nc.tensor.transpose(bank[4 + h // 2][:, o:o + 128], s[:, (u - 1) % 2, h, 128 * k:128 * k + 128], ident)
                                mm.then_inc(*pt_filled.one())
                                pe.wait_ge(*pt_copied.at(u))
                                if u >= 3:
                                    pe.wait_ge(*o_added.at(u - 2))
                                for h in range(4):
                                    for k in range(t + 1):
                                        mm = nc.tensor.matmul(bank[6 + (u - 1) % 2][:, 64 * h:64 * h + 64], pt[:, h, k], vn[:, br, k, 64 * g:64 * g + 64],
                                                              start=(k == 0), stop=(k == t))
                                mm.then_inc(*o_filled.one())

                    @block.scalar
                    def _(act):
                        for u in range(n + 1):
                            if u >= 1:
                                br, t, g = units[u - 1]
                                act.wait_ge(*pt_filled.at(u))
                                if u >= 2:
                                    act.wait_ge(*o_filled.at(u - 1))
                                for i in range(2):
                                    src = bank[4 + i][:].rearrange("p (h k q) -> p h k q", h=2, k=2)[:, :, 0:t + 1]
                                    ins = nc.scalar.copy(pt[:, 2 * i:2 * i + 2, 0:t + 1], src)
                                ins.then_inc(*pt_copied.one())
                            if u < n:
                                act.wait_ge(*s_ready.at(u + 1))
                                for h in range(4):
                                    ins = nc.scalar.activation(s[:, u % 2, h], s[:, u % 2, h], ACT.Exp, bias=stt[:, u % 2, 0, h:h + 1],
                                                               accum_out=stt[:, u % 2, 1, h:h + 1])
                                ins.then_inc(*p_ready.one())

                    @block.vector
                    def _(dve):
                        link = linker(dve, dve_done)
                        for u in range(n + 1):
                            if u < n:
                                br, t, g = units[u]
                                hd0 = 8 * (g // 2) + g % 2
                                dve.wait_ge(*s_filled.at(u + 1))
                                if u >= 2:
                                    dve.wait_ge(*pt_filled.at(u - 1))
                                for i in range(2):
                                    link(V.tensor_tensor(s[:, u % 2, 2 * i:2 * i + 2], bank[2 * (u % 2) + i][:].rearrange("p (h k) -> p h k", h=2),
                                                         bias[:, t, hd0 + 4 * i:hd0 + 4 * i + 3:2], ALU.add))
                                link(V.tensor_reduce(stt[:, u % 2, 0], s[:, u % 2], AX.X, ALU.max))
                                V.tensor_scalar(stt[:, u % 2, 0], stt[:, u % 2, 0], -1.0, None, ALU.mult).then_inc(*s_ready.one())
                            if u >= 1:
                                br, t, g = units[u - 1]
                                b = (u - 1) % 2
                                hd0 = 8 * (g // 2) + g % 2
                                dve.wait_ge(*p_ready.at(u))
                                link(V.reciprocal(stt[:, b, 2], stt[:, b, 1]))
                                link(V.tensor_tensor(stt[:, b, 2], stt[:, b, 2], gate[:, t, 16 + 16 * br + hd0:16 + 16 * br + hd0 + 7:2], ALU.mult))
                                dve.wait_ge(*o_filled.at(u))
                                link(V.tensor_tensor(ot[:], bank[6 + b][:, 0:256].rearrange("p (h d) -> p h d", h=4),
                                                     stt[:, b, 2].rearrange("p (h o) -> p h o", o=1).to_broadcast([128, 4, 64]), ALU.mult))
                                o = oacc[:, t].rearrange("p (a h b d) -> p a b h d", a=2, h=4, b=2)[:, g // 2, g % 2]
                                V.tensor_tensor(o, o, ot[:], ALU.add).then_inc(*o_added.one())
                                dve.wait_ge(*o_added.now())
            with core.block() as block:
                @block.sync
                def _(sp):
                    sp.wait_ge(*out_sent.now())

                @block.tensor
                def _(pe):
                    for t in range(2):
                        for c in range(8):
                            mm = nc.tensor.transpose(bank[2 * t + c // 4][:, 128 * (c % 4):128 * (c % 4) + 128], oacc[:, t, 128 * c:128 * c + 128], ident)
                            if c % 4 == 3:
                                mm.then_inc(*pe_done.one())

                @block.vector
                def _(dve):
                    for k in range(4):
                        dve.wait_ge(*pe_done.at(k + 1))
                        V.tensor_copy(uT[:, 4 * (k % 2):4 * (k % 2) + 4, 128 * (k // 2):128 * (k // 2) + 128],
                                      bank[k][:].rearrange("p (c q) -> p c q", c=4)[:, :, 127::-1]).then_inc(*dve_done.one())
        env["project"](uT, KT, D, env["nothing"], env["add_residual"])


def hgrn_layer(env):
    (nc, core, I, O, W, cst, par, xT, uT, eps, scratch, linker, ident, ones, lb) = (
        env[k] for k in ("nc", "core", "I", "O", "W", "cst", "par", "xT", "uT", "eps", "scratch", "linker", "ident", "ones", "lb"))
    count, bank = core.count, core.bank
    pe_done, act_done, dve_done = (count(n) for n in ("pe_done", "act_done", "dve_done"))
    misc, out_sent, pool_sent = count("misc_dma", 16), count("out_sent", 16), count("pool_sent", 16)
    state_in, state_out = [count(f"state_in{b}", 16) for b in range(3)], [count(f"state_out{b}", 16) for b in range(3)]
    V = nc.vector
    with ExitStack() as layer:
        def sb(name, shape, dt=F32, ctx=layer):
            return core.sb("h_" + name, shape, dt, ctx)

        qT, fT, vT, gT = (sb(n, [128, HH, T]) for n in ("qT", "fT", "vT", "gT"))
        oT = uT

        def act_step(act, t, ps):
            dst, f = ((qT, ACT.Silu), (fT, ACT.Sigmoid), (vT, ACT.Copy), (gT, ACT.Silu))[t // 8]
            return nc.scalar.activation(dst[:, t % 8], ps[:, 0:T], f)

        env["project"](uT, KT, 4096, act_step, lambda eng, t, ps: None)
        with core.block() as block:
            @block.vector
            def _(dve):
                for h in range(HH):
                    V.tensor_scalar(fT[:, h], fT[:, h], lb[:, 8 + h:9 + h], lb[:, h:h + 1], ALU.mult, ALU.add).then_inc(*dve_done.one())

        with ExitStack() as st:
            ke, kd = sb("ke", [128, HH, LP], ctx=st), sb("kd", [128, HH, LP], ctx=st)
            dec = sb("dec", [128, HH, NHC], ctx=st)
            vn, kdn = sb("vn", [128, 2, D], ctx=st), sb("kdn", [128, 2, D], ctx=st)
            with ExitStack() as st2:
                ac, ex = sb("ac", [128, HH, LP], ctx=st2), sb("ex", [128, HH, LP], ctx=st2)
                mark = {}

                def chunks(t):
                    return t[:].rearrange("p h (c t) -> p (h c) t", t=HC)
                with core.block() as block:
                    @block.vector
                    def _(dve):
                        link = linker(dve, dve_done)
                        dve.wait_ge(*act_done.at(1))
                        for h in range(HH):
                            V.tensor_tensor_scan(ac[:, h], cst("scan_keep"), ex[:, h], 0.0, ALU.mult, ALU.add).then_inc(*dve_done.one())
                        dve.wait_ge(*dve_done.now())
                        mark["ac"] = dve_done.now()
                        dve.wait_ge(*act_done.at(2))
                        q = qT[:, :, 0:LP]
                        link(V.tensor_tensor(q, q, ex[:], ALU.mult))
                        mark["qe"] = dve_done.now()
                        link(V.tensor_scalar(kd[:], fT[:, :, 0:LP], -1.0, 1.0, ALU.mult, ALU.add))
                        dve.wait_ge(*act_done.at(3))
                        link(V.tensor_tensor(ke[:], kd[:], ex[:], ALU.mult))
                        dve.wait_ge(*act_done.at(4))
                        a = chunks(ac)
                        link(V.tensor_tensor(a, a[:, :, HC - 1:HC].to_broadcast([128, HH * NHC, HC]), a, ALU.subtract))
                        mark["to end"] = dve_done.now()
                        dve.wait_ge(*act_done.at(5))
                        link(V.tensor_tensor(kd[:], kd[:], ex[:], ALU.mult))

                    @block.scalar
                    def _(act):
                        nc.scalar.activation(ex[:], fT[:, :, 0:LP], ACT.Ln).then_inc(*act_done.one())
                        act.wait_ge(*mark["ac"])
                        nc.scalar.activation(ex[:], ac[:], ACT.Exp).then_inc(*act_done.one())
                        act.wait_ge(*mark["qe"])
                        nc.scalar.activation(ex[:], ac[:], ACT.Exp, scale=-1.0).then_inc(*act_done.one())
                        nc.scalar.activation(dec[:], ac[:].rearrange("p h (c t) -> p h c t", t=HC)[:, :, :, HC - 1], ACT.Exp).then_inc(*act_done.one())
                        act.wait_ge(*mark["to end"])
                        nc.scalar.activation(ex[:], ac[:], ACT.Exp).then_inc(*act_done.one())
            att = sb("att", [128, 2, HH, 128], ctx=st)
            states = sb("states", [128, NHC + 1, HH, 128], ctx=st)
            mark = {}
            with core.block() as block:
                @block.tensor
                def _(pe):
                    for k, src in ((0, vT), (1, kd)):
                        for t in range(2):
                            for q in range(2):
                                for i in range(4):
                                    mm = nc.tensor.transpose(bank[4 * k + 2 * t + q][:, 128 * i:128 * i + 128], src[:, 4 * q + i, 128 * t:128 * t + 128], ident)
                                mm.then_inc(*pe_done.one())
                    for t in range(2):
                        for q in range(2):
                            pe.wait_ge(*act_done.at(2 * t + q + 1))
                            for i in range(4):
                                h = 4 * q + i
                                mm = nc.tensor.matmul(bank[2 * t + q][:, 128 * i:128 * i + 128], ke[:, h, 128 * t:128 * t + 128],
                                                      qT[:, h, 128 * t:128 * t + 128], start=True, stop=True)
                            mm.then_inc(*pe_done.one())

                @block.scalar
                def _(act):
                    for k in range(4):
                        act.wait_ge(*pe_done.at(k + 1))
                        nc.scalar.copy(vn[:, k // 2, 512 * (k % 2):512 * (k % 2) + 512], bank[k][:]).then_inc(*act_done.one())

                @block.vector
                def _(dve):
                    V.memset(att[:], 0.0).then_inc(*dve_done.one())
                    V.memset(states[:, 0], 0.0).then_inc(*dve_done.one())
                    for k in range(4):
                        dve.wait_ge(*pe_done.at(k + 5))
                        V.tensor_copy(kdn[:, k // 2, 512 * (k % 2):512 * (k % 2) + 512], bank[4 + k][:]).then_inc(*dve_done.one())
                    dve.wait_ge(*dve_done.now())
                    m = cst("att_mask").bitcast(U32).rearrange("p (o t) -> p o t", o=1).to_broadcast([128, 4, 128])
                    for k in range(4):
                        dve.wait_ge(*pe_done.at(k + 9))
                        V.copy_predicated(att[:, k // 2, 4 * (k % 2):4 * (k % 2) + 4], m, bank[k][:].rearrange("p (h t) -> p h t", h=4)) \
                            .then_inc(*dve_done.one())

            with core.block() as block:
                @block.tensor
                def _(pe):
                    for c in range(NHC):
                        rows, t, r = slice(32 * (c % 4), 32 * (c % 4) + 32), c // 4, c % 4
                        if c >= 4:
                            pe.wait_ge(*dve_done.at(3 * (c - 4) + 3))
                        for h in range(HH):
                            o = 128 * (h % 4)
                            mm = nc.tensor.matmul(bank[2 * r + h // 4][:, o:o + 128], kdn[rows, t, 128 * h:128 * h + 128],
                                                  vn[rows, t, 128 * h:128 * h + 128], start=True, stop=True, tile_position=(32 * r, 0))
                        mm.then_inc(*pe_done.one())

                @block.vector
                def _(dve):
                    link = linker(dve, dve_done)
                    for c in range(NHC):
                        new = states[:, c + 1]
                        link(V.tensor_tensor(new, states[:, c], dec[:, :, c:c + 1].to_broadcast([128, HH, 128]), ALU.mult))
                        dve.wait_ge(*pe_done.at(c + 1))
                        for q in range(2):
                            part = new[:, 4 * q:4 * q + 4]
                            V.tensor_tensor(part, part, bank[2 * (c % 4) + q][:].rearrange("p (h v) -> p h v", h=4), ALU.add).then_inc(*dve_done.one())
                        dve.wait_ge(*dve_done.now())
            with core.block() as block:
                @block.sync
                def _(sp):
                    sp.dma_start(O["hgrn_p"], states[:, NHC]).then_inc(*out_sent.one())
                    sp.wait_ge(*out_sent.now())

                @block.tensor
                def _(pe):
                    for h in range(HH):
                        o = LP * (h % 2)
                        for t in range(2):
                            mm = nc.tensor.matmul(bank[h // 2][:, o + 128 * t:o + 128 * t + 128], vn[:, t, 128 * h:128 * h + 128], att[:, t, h],
                                                  start=True, stop=False, skip_group_check=True)
                            for c in range(4 * t, 4 * t + 4):
                                mm = nc.tensor.matmul(bank[h // 2][:, o + HC * c:o + HC * c + HC], states[:, c, h], qT[:, h, HC * c:HC * c + HC],
                                                      start=False, stop=True, skip_group_check=True)
                        if h % 2:
                            mm.then_inc(*pe_done.one())

                @block.scalar
                def _(act):
                    for k in range(4):
                        act.wait_ge(*pe_done.at(k + 1))
                        nc.scalar.copy(oT[:, 2 * k:2 * k + 2, 0:LP], bank[k][:].rearrange("p (h t) -> p h t", h=2)).then_inc(*act_done.one())

        with ExitStack() as st:
            kS = sb("kS", [128, HH, NB], ctx=st)
            vnat = sb("vnat", [NB, D], ctx=st)
            vb = sb("vb", [128, NB, D], ctx=st)
            sbuf = sb("state", [128, 3, HH, 128], ctx=st)
            tmp = sb("tmp", [128, HH, 128], ctx=st)
            d_v = scratch("scr_v", [NB, D])
            with core.block() as block:
                @block.tensor
                def _(pe):
                    for h in range(HH):
                        mm = nc.tensor.transpose(bank[h // 4][0:NB, 128 * (h % 4):128 * (h % 4) + 128], vT[:, h, LP:T], ident)
                    mm.then_inc(*pe_done.one())

                @block.vector
                def _(dve):
                    V.tensor_scalar(kS[:], fT[:, :, LP:T], -1.0, 1.0, ALU.mult, ALU.add).then_inc(*dve_done.one())
                    dve.wait_ge(*pe_done.at(1))
                    for k in range(2):
                        V.tensor_copy(vnat[:, 512 * k:512 * k + 512], bank[k][0:NB, :]).then_inc(*dve_done.one())

                @block.gpsimd
                def _(pool):
                    pool.wait_ge(*dve_done.at(3))
                    pool.dma_start(d_v, vnat[:]).then_inc(*pool_sent.one())
                    pool.wait_ge(*pool_sent.now())
                    pool.dma_start(vb[:], d_v.rearrange("(o b) c -> o b c", o=1).to_broadcast([128, NB, D])).then_inc(*misc.one())
                    pool.wait_ge(*misc.now())
            with core.block() as block:
                @block.scalar
                def _(act):
                    for b in range(NB):
                        if b >= 3:
                            act.wait_ge(*state_out[b % 3].at(b // 3))
                            act.wait_ge(*pe_done.at(b - 2))
                        act.dma_start(sbuf[:, b % 3], I["hgrn0"][:, b]).then_inc(*state_in[b % 3].one())
                    act.wait_ge(*pe_done.at(NB))
                    nc.scalar.copy(oT[:, :, LP:T], bank[0][:, 0:64].rearrange("p (h b) -> p h b", h=HH)).then_inc(*act_done.one())

                @block.sync
                def _(sp):
                    for b in range(NB):
                        sp.wait_ge(*dve_done.at(3 * (b + 1)))
                        sp.dma_start(O["hgrn_s"][:, b], sbuf[:, b % 3]).then_inc(*state_out[b % 3].one())
                    for k in range(3):
                        sp.wait_ge(*state_out[k].now())

                @block.vector
                def _(dve):
                    link = linker(dve, dve_done)
                    for b in range(NB):
                        s = sbuf[:, b % 3]
                        dve.wait_ge(*state_in[b % 3].at(b // 3 + 1))
                        link(V.tensor_tensor(s, s, fT[:, :, LP + b:LP + b + 1].to_broadcast([128, HH, 128]), ALU.mult))
                        link(V.tensor_tensor(tmp[:], vb[:, b].rearrange("p (h v) -> p h v", h=HH), kS[:, :, b:b + 1].to_broadcast([128, HH, 128]), ALU.mult))
                        link(V.tensor_tensor(s, s, tmp[:], ALU.add))

                @block.tensor
                def _(pe):
                    for b in range(NB):
                        pe.wait_ge(*dve_done.at(3 * (b + 1)))
                        for h in range(HH):
                            mm = nc.tensor.matmul(bank[0][:, NB * h + b:NB * h + b + 1], sbuf[:, b % 3, h], qT[:, h, LP + b:LP + b + 1], start=True, stop=True)
                        mm.then_inc(*pe_done.one())
        env["norm_each"]([(oT[:, h], oT[:, h], par("h_norm_g"), 1 / 128, eps[:, 0:1]) for h in range(HH)], ones, "hn")
        with core.block() as block:
            @block.vector
            def _(dve):
                V.tensor_tensor(oT[:], oT[:], gT[:], ALU.mult).then_inc(*dve_done.one())
        env["project"](oT, KT, D, env["nothing"], env["add_residual"])


def pack_params(x):
    def cols(a):
        return a.reshape(-1, 128).T
    rep = lambda a: np.tile(a, 128 // a.shape[0])[:, None]
    pad = lambda a: np.concatenate([a, np.zeros((128 - a.shape[0],), a.dtype)])[:, None]
    cw = x["m_conv_w"].reshape(2, 4, NCH, 128).transpose(0, 2, 1, 3).reshape(-1, 128).T
    pe = x["n_cmp_pe"][0].reshape(2, 2, 8, 128).transpose(3, 0, 1, 2).reshape(128, 32)
    moe_b = np.concatenate([x["moe_b_rg"], x["moe_b_re"]], axis=1).reshape(1, 80)
    parts = [cols(x["norm_g"]), cw, cols(x["m_conv_b"]), cols(x["m_norm_g"]), cols(np.repeat(x["m_d"], 64, axis=1)),
             pad(x["m_a_log"][0]), pad(x["m_a_log"][1]), pad(x["m_dt_bias"][0]), pad(x["m_dt_bias"][1]), rep(x["n_q_g"][0]),
             rep(x["n_k_g"][0, 0]), rep(x["n_k_g"][0, 1]), rep(x["n_k_g"][0, 2]), cols(x["h_lb"]), x["h_norm_g"][0][:, None],
             pe, np.broadcast_to(moe_b, (128, 80))]
    return np.concatenate(parts, axis=1)


def lay_out(x):
    f = {}
    f["consts"] = constants()[0]
    f["onehots"] = bucket_onehots()
    f["params"] = pack_params(x)
    xx = np.concatenate([x["x_prompt"][0], x["x_sample"][:, 0]], axis=0)
    f["xT"] = xx.T.reshape(KT, 128, T).transpose(1, 0, 2)
    chunk = lambda w: w.reshape(w.shape[:-2] + (-1, 128, w.shape[-1]))
    f["m_w_in"] = x["m_w_in"]
    f["w_dt"] = chunk(x["m_w_in"][:, :, 5120:]).transpose(2, 0, 1, 3)
    f["m_w_out"] = x["m_w_out"]
    f["conv0"] = x["state_conv"].reshape(2, NB, 3, NCH, 128).transpose(0, 4, 3, 2, 1)
    f["ssm0"] = x["state_ssm"].reshape(2, NB, CI, 128, 128).transpose(0, 3, 2, 1, 4)
    def heads(w):
        return w.reshape(w.shape[:-1] + (2, 2, 4, 64)).swapaxes(-3, -2).reshape(w.shape)
    w = x["n_w_in"][0]
    f["n_w_in"] = np.concatenate([heads(w[:, :1024]), w[:, 1024:2560]], axis=1)
    gl = w[:, 2560:].reshape(D, 2, 2, 4, 3).transpose(0, 4, 1, 3, 2).reshape(D, 48)
    f["w_gl"] = chunk(gl).transpose(1, 0, 2)
    f["n_w_out"] = heads(x["n_w_out"][0].T).T
    f["rel"] = x["rel_table"].reshape(32, 2, 2, 4).swapaxes(-2, -1).reshape(32, 16)
    f["cmp_w1"] = x["n_cmp_w1"][0].reshape(2, 2, 8, 128, 64).transpose(3, 0, 2, 1, 4)
    f["cmp_w1d"] = np.tile(x["n_cmp_w1"][0].reshape(2, 32, 64, 64).transpose(2, 0, 1, 3), (2, 1, 1, 1))
    f["cmp_w2"] = x["n_cmp_w2"][0].transpose(1, 0, 2)
    n_pool = x["cache_kv_cmp"].shape[1]
    c = x["cache_kv_cmp"][0].reshape(n_pool, 8, 8, 2, 2, 4, 64)
    f["cache_cmp"] = c.transpose(0, 3, 6, 4, 2, 5, 1).reshape(n_pool, 128, 512)

    def kv_page(c):
        k = c[..., 0, :, :].reshape(c.shape[:-4] + (128, 2, 128))
        k = np.swapaxes(k, -3, -1)
        k = k.reshape(c.shape[:-4] + (128, 256))
        return np.concatenate([k, c[..., 1, :, :].reshape(c.shape[:-4] + (128, 256))], axis=-1)
    f["cache_sel"] = kv_page(x["cache_kv_sel"][0])
    win = x["cache_kv_win"][0]
    f["cache_win"] = kv_page(win.reshape(NB, 4, 128, 2, 4, 64)).transpose(0, 2, 1, 3)
    f["win_rows"] = win.reshape(NB, 512, 512)
    f["pages"] = x["page_table"].reshape(1, 64)
    f["h_w_in"], f["h_w_out"] = x["h_w_in"][0], x["h_w_out"][0]
    f["hgrn0"] = x["state_hgrn"][0].transpose(2, 0, 1, 3)
    f["w_rt"] = chunk(np.concatenate([x["moe_w_rg"], x["moe_w_re"]], axis=2)).transpose(2, 0, 1, 3)
    for k in ("moe_w1", "moe_w3", "moe_w2"):
        f[k] = x[k]
    return {k: np.ascontiguousarray(v) for k, v in f.items()}


OUTS = {"yT": (128, KT, T), "conv_tail": (2, 128, NCH, 11), "conv_keep": (2, 128, NCH, 2, NB), "ssm_p": (2, 128, DI),
        "ssm_s": (2, 128, CI, NB, 128), "kvT": (128, 12, T), "win_old": (NB, 511, 512), "hgrn_p": (128, HH, 128),
        "hgrn_s": (128, NB, HH, 128)}


def give_back(r):
    y = r["yT"].transpose(2, 1, 0).reshape(T, D)
    tail = r["conv_tail"].transpose(0, 3, 2, 1).reshape(2, 11, NCH * 128)
    conv_p = tail[:, None, 0:3]
    keep = r["conv_keep"].transpose(0, 4, 3, 2, 1).reshape(2, NB, 2, NCH * 128)
    conv_s = np.concatenate([keep, tail[:, 3:, None]], axis=2)
    ssm_p = r["ssm_p"].reshape(2, 1, 128, MH, 64).transpose(0, 1, 3, 4, 2)
    ssm_s = r["ssm_s"].transpose(0, 3, 2, 1, 4).reshape(2, NB, MH, 64, 128)
    kv = r["kvT"].transpose(2, 1, 0).reshape(T, 3, 2, 4, 64)
    new = [kv[:LP, b][None, None] for b in range(3)]
    dec = [kv[LP:, b][None, :, None] for b in range(3)]
    win_s = np.concatenate([r["win_old"].reshape(1, NB, 511, 2, 4, 64), dec[2]], axis=2)
    hg_p = r["hgrn_p"].transpose(1, 0, 2)[None, None]
    hg_s = r["hgrn_s"].transpose(1, 2, 0, 3)[None]
    outs = (y[None, :LP], y[LP:, None], ssm_p, conv_p, new[0], new[1], new[2], hg_p, ssm_s, conv_s, dec[0], dec[1], win_s, hg_s)
    return tuple(np.ascontiguousarray(o) for o in outs)


def kernel(**inputs):
    import concourse.bacc as bacc
    from concourse.bass_utils import run_bass_kernel_spmd

    nc = bacc.Bacc("TRN2", target_bir_lowering=False, num_devices=1)
    arrays = lay_out({k: np.asarray(v) for k, v in inputs.items()})
    I = {k: nc.dram_tensor("in_" + k, a.shape, mybir.dt.from_np(a.dtype), kind="ExternalInput").ap() for k, a in arrays.items()}
    O = {k: nc.dram_tensor("out_" + k, s, F32, kind="ExternalOutput").ap() for k, s in OUTS.items()}
    build(nc, I, O)
    r = run_bass_kernel_spmd(nc, [{"in_" + k: a for k, a in arrays.items()}], core_ids=[0])
    return give_back({k: r.results[0]["out_" + k] for k in OUTS})
```

```python
from contextlib import ExitStack, contextmanager

import numpy as np
import concourse.bass as bass
from concourse import mybir

ALU = mybir.AluOpType
ACT = mybir.ActivationFunctionType
AX = mybir.AxisListType
F32 = mybir.dt.float32
I32 = mybir.dt.int32
U32 = mybir.dt.uint32

D = 1024
LP = 256
NB = 8
T = LP + NB
KT = D // 128
EPS = 1e-6
NEG = -1e30
DI = 2048
CI = DI // 128
NCH = 24
MH = 32
NG = 4
HB = 4
HD = 64
PAST = 1024
NPAGE = PAST // 128
NCMP = 63
NCMPP = 15
NSEL = 17
NSTRIP = 512
HH = 8
HC = 32
NHC = LP // HC
HBS = 6
NE = 16
FF = 512
CAP = 64
UNTAKEN = 1000
CROWDED_FROM = CAP
SLOTS = 6
SLOT = 2048


def constants():
    c = {}
    i = np.arange(128)
    c["ident"] = np.eye(128)
    c["ones"] = np.ones((128, 128))
    c["ones64"] = (i[:, None] // 64 == i[None, :] // 64) * 1.0
    c["ssd_mask"] = np.where(i[None, :] >= i[:, None], 0.0, NEG)
    c["att_mask"] = ((i[None, :] >= i[:, None]) & (i[None, :] // HC == i[:, None] // HC)) * 1.0
    b, hd = i // 16, i % 16
    grp = (hd // 8) * 2 + hd % 2
    c["same_group"] = ((b[:, None] == b[None, :]) & (grp[:, None] == grp[None, :])) * 1.0
    c["of_seq"] = (b[:, None] == np.arange(8)[None, :]) * 1.0
    ov = np.zeros((128, NSEL))
    for k in range(NCMP):
        for j in range(NSEL):
            ov[k, j] = 16 * k < 64 * j + 64 and 16 * k + 32 > 64 * j
    ov[64:] = ov[:64]
    c["overlap"] = ov
    c["block_no"] = np.tile(np.arange(1, NSEL + 1.0), (128, 1))
    c["forced"] = np.tile(np.where((np.arange(NSEL) == 0) | (np.arange(NSEL) == NSEL - 1), 1e9, 0.0), (128, 1))
    q = np.arange(256).reshape(2, 128)[:, ::-1].T
    ends = np.arange(16) * 16 + 31
    v = (q[:, :, None] >= ends[None, None, :]) & (np.arange(16) < NCMPP)
    c["cmp_valid"] = v.reshape(128, 32) * 1.0
    c["earlier"] = (i[:, None] < i[None, :]) * 1.0
    c["last_rows"] = (i[:, None] >= 128 - T % 128) * 1.0
    c["slot_no"] = np.tile(np.arange(CAP) - UNTAKEN * 1.0, (128, 1))
    c["four_down"] = np.tile([4.0, 3.0, 2.0, 1.0], (128, 1))
    c["scan_keep"] = np.tile((np.arange(LP) % HC != 0) * 1.0, (128, 1))
    off, at = {}, 0
    for k, a in c.items():
        off[k] = (at, a.shape[1])
        at += a.shape[1]
    return np.concatenate([np.asarray(a, np.float32) for a in c.values()], axis=1), off


def bucket(dist):
    d = np.maximum(dist, 0)
    ratio = np.log(np.maximum(d, 1).astype(np.float32) / 16) / np.float32(np.log(8.0))
    large = np.minimum(16 + (ratio * 16).astype(np.int32), 31)
    return np.where(d < 16, d, large)


def bucket_onehots():
    dist = 255 - np.arange(NSTRIP)
    a = (bucket(dist)[None, :] == np.arange(32)[:, None]) & (dist >= 0)[None, :]
    b = bucket(PAST - np.arange(PAST + 1))[None, :] == np.arange(32)[:, None]
    return np.concatenate([a, b], axis=1).astype(np.float32)


PCOLS, _at = {}, 0
for _n, _w in [("norm_g", 64), ("conv_w", 2 * NCH * 4), ("conv_b", 2 * NCH), ("m_norm_g", 2 * CI), ("m_d", 2 * CI),
               ("a_log", 2), ("dt_bias", 2), ("q_g", 1), ("k_g", 3), ("h_lb", 32), ("h_norm_g", 1),
               ("pe", 32), ("moe_b", 80)]:
    PCOLS[_n] = (_at, _w)
    _at += _w
NPAR = _at


class Count:

    def __init__(self, sem, step=1):
        self.sem, self.step, self.n, self.start = sem, step, 0, 0
        self.turn = 0

    def one(self):
        self.n += self.step
        return self.sem, self.step

    def of(self, i, per, k):
        return self.sem, i * (per * self.step) + (self.start + k * self.step)

    def now(self):
        return self.sem, self.turn + self.n

    def at(self, k):
        return self.sem, self.start + k * self.step

    @contextmanager
    def each(self, i, per, trips):
        first = self.n
        self.turn = i * (per * self.step)
        yield
        assert self.n == first + per * self.step, (self.n, first, per)
        self.turn = 0
        self.n = first + per * self.step * trips


class Core:

    def __init__(self, nc, ctx):
        self.nc, self.ctx, self.counts, self.blocks = nc, ctx, {}, 0
        self.bank = [ctx.enter_context(nc.psum_tensor(f"bank{i}", [128, 512], F32)) for i in range(8)]

    def sb(self, name, shape, dt=F32, ctx=None):
        return (ctx or self.ctx).enter_context(self.nc.sbuf_tensor(name, shape, dt))

    def count(self, name, step=1):
        if name not in self.counts:
            self.counts[name] = Count(self.ctx.enter_context(self.nc.semaphore(name)), step)
        return self.counts[name]

    @contextmanager
    def block(self):
        for c in self.counts.values():
            c.start = c.n
        with self.nc.Block(no_gpsimd_drain=True) as b:
            yield b


class Weights:

    def __init__(self, core):
        self.core = core
        self.ring = core.sb("ring", [128, SLOTS, SLOT])
        self.full = [core.count(f"slot_full{s}", 16) for s in range(SLOTS)]
        self.free = [core.count(f"slot_free{s}") for s in range(SLOTS)]
        self.plan, self.sent, self.used = [], 0, 0

    def add(self, w, kt, cols):
        self.plan.append((w, kt, cols))

    def view(self, s, kt, cols):
        return self.ring[:, s, 0:kt * cols].rearrange("p (k c) -> p k c", k=kt)

    def send(self, sp, upto):
        while self.sent < min(upto, len(self.plan)):
            s = self.sent % SLOTS
            w, kt, cols = self.plan[self.sent]
            if self.sent >= SLOTS:
                sp.wait_ge(self.free[s].sem, self.sent // SLOTS)
            sp.dma_start(self.view(s, kt, cols), w.rearrange("(k p) c -> p k c", p=128)).then_inc(*self.full[s].one())
            self.sent += 1


def build(nc, I, O):
    with ExitStack() as ctx:
        core = Core(nc, ctx)
        sb, count, bank = core.sb, core.count, core.bank

        cst_np, coff = constants()
        consts = sb("consts", [128, cst_np.shape[1]])
        params = sb("params", [128, NPAR])
        xT = sb("xT", [128, KT, T])
        uT = sb("uT", [128, KT, T])
        w_dt = sb("w_dt", [128, 2, KT, MH])
        w_gl = sb("w_gl", [128, KT, 48])
        w_rt = sb("w_rt", [128, 4, KT, 20])
        eps = sb("eps", [128, 3])
        lb = sb("lb", [128, 16])
        W = Weights(core)

        def cst(name):
            a, n = coff[name]
            return consts[:, a:a + n]

        def par(name, k=0, n=1):
            a = PCOLS[name][0] + k
            return params[:, a:a + n]

        ident, ones = cst("ident"), cst("ones")
        scr = {}

        def scratch(name, shape):
            if name not in scr:
                scr[name] = nc.dram_tensor(name, shape, F32, kind="Internal").ap()
            return scr[name]

        def plan_proj(w, k, n):
            kt = k // 128
            per = SLOT // kt
            for c in range(0, n, per):
                W.add(w[:, c:c + min(per, n - c)], kt, min(per, n - c))

        def plan_moe(layer):
            for e in range(NE):
                for h in range(2):
                    W.add(I["moe_w1"][layer, e][:, 256 * h:256 * h + 256], KT, 256)
                    W.add(I["moe_w3"][layer, e][:, 256 * h:256 * h + 256], KT, 256)
                for h in range(2):
                    W.add(I["moe_w2"][layer, e][:, 512 * h:512 * h + 512], FF // 128, 512)

        for layer in range(4):
            j = layer // 3
            if layer % 3 == 0:
                plan_proj(I["m_w_in"][j], D, 5120)
                plan_proj(I["m_w_out"][j], DI, D)
            elif layer == 1:
                plan_proj(I["n_w_in"], D, 2560)
                plan_proj(I["n_w_out"], D, D)
            else:
                plan_proj(I["h_w_in"], D, 4096)
                plan_proj(I["h_w_out"], D, D)
            plan_moe(layer)

        pe_done, act_done, dve_done = count("pe_done"), count("act_done"), count("dve_done")
        pool_done = count("pool_done")
        in_loaded = count("in_loaded", 16)
        out_sent = count("out_sent", 16)
        misc = count("misc_dma", 16)

        def linker(eng, c):
            def link(ins):
                ins.then_inc(*c.one())
                eng.wait_ge(*c.now())
                return ins
            return link

        with core.block() as block:
            @block.sync
            def _(sp):
                for dst, src in [(consts, I["consts"]), (params, I["params"]), (xT, I["xT"]), (w_dt, I["w_dt"]),
                                 (w_gl, I["w_gl"]), (w_rt, I["w_rt"])]:
                    sp.dma_start(dst[:], src).then_inc(*in_loaded.one())
                W.send(sp, SLOTS)
                sp.wait_ge(*in_loaded.now())

            @block.vector
            def _(dve):
                link = linker(dve, dve_done)
                link(nc.vector.memset(eps[:, 0:1], EPS))
                link(nc.vector.memset(eps[:, 1:2], 64 * EPS))
                link(nc.vector.memset(eps[:, 2:3], 1.0))
        with core.block() as block:
            lbm, lbe = sb("lbm", [128, 8]), sb("lbe", [128, 32])

            @block.vector
            def _(dve):
                link = linker(dve, dve_done)
                lbv = par("h_lb", 0, 32)
                link(nc.vector.tensor_reduce(lbm[:], lbv.rearrange("p (l c) -> p c l", l=4), AX.X, ALU.max))
                for l in range(4):
                    link(nc.vector.tensor_tensor(lbe[:, 8 * l:8 * l + 8], lbv[:, 8 * l:8 * l + 8], lbm[:], ALU.subtract))
                dve.wait_ge(*act_done.at(1))
                link(nc.vector.tensor_reduce(lbm[:], lbe[:].rearrange("p (l c) -> p c l", l=4), AX.X, ALU.add))
                link(nc.vector.reciprocal(lbm[:], lbm[:]))
                link(nc.vector.tensor_tensor(lb[:, 0:8], lbe[:, 8:16], lbe[:, 16:24], ALU.add))
                link(nc.vector.tensor_tensor(lb[:, 0:8], lb[:, 0:8], lbm[:], ALU.mult))
                link(nc.vector.tensor_scalar(lb[:, 8:16], lb[:, 0:8], -1.0, 1.0, ALU.mult, ALU.add))

            @block.scalar
            def _(act):
                act.wait_ge(*dve_done.at(5))
                nc.scalar.activation(lbe[:], lbe[:], ACT.Exp).then_inc(*act_done.one())

        def norm_all(src, chunks, gain, dst, name):
            with ExitStack() as st:
                sq = sb(name + "_sq", [128, 4, T], ctx=st)
                rs = sb(name + "_rs", [128, T], ctx=st)
                parts = chunks // 2
                with core.block() as block:
                    @block.scalar
                    def _(act):
                        for c in range(parts):
                            if c >= 2:
                                act.wait_ge(*pe_done.at(c - 1))
                            nc.scalar.activation(sq[:, 2 * (c % 2):2 * (c % 2) + 2], src[:, 2 * c:2 * c + 2], ACT.Square).then_inc(*act_done.one())
                        act.wait_ge(*pe_done.at(parts))
                        nc.scalar.activation(rs[:], bank[0][:, 0:T], ACT.Sqrt, bias=eps[:, 0:1], scale=1.0 / (128 * chunks)).then_inc(*act_done.one())

                    @block.tensor
                    def _(pe):
                        for c in range(parts):
                            pe.wait_ge(*act_done.at(c + 1))
                            for k in range(2):
                                mm = nc.tensor.matmul(bank[0][:, 0:T], ones, sq[:, 2 * (c % 2) + k], start=(c + k == 0),
                                                      stop=(c == parts - 1 and k == 1))
                            mm.then_inc(*pe_done.one())

                    @block.vector
                    def _(dve):
                        link = linker(dve, dve_done)
                        dve.wait_ge(*act_done.at(parts + 1))
                        link(nc.vector.reciprocal(rs[:], rs[:]))
                        for c in range(chunks):
                            nc.vector.scalar_tensor_tensor(out=dst[:, c], in0=src[:, c], scalar=gain(c), in1=rs[:],
                                                           op0=ALU.mult, op1=ALU.mult).then_inc(*dve_done.one())

        def norm_each(jobs, ones_m, name):
            with ExitStack() as st:
                n = len(jobs)
                sq = sb(name + "_sq", [128, 2, T], ctx=st)
                rs = sb(name + "_rs", [128, 2, T], ctx=st)
                with core.block() as block:
                    @block.scalar
                    def _(act):
                        for k in range(n + 1):
                            if k < n:
                                if k >= 2:
                                    act.wait_ge(*pe_done.at(k - 1))
                                nc.scalar.activation(sq[:, k % 2], jobs[k][0], ACT.Square).then_inc(*act_done.one())
                            if k >= 1:
                                act.wait_ge(*pe_done.at(k))
                                if k >= 3:
                                    act.wait_ge(*dve_done.at(2 * (k - 2)))
                                nc.scalar.activation(rs[:, (k - 1) % 2], bank[(k - 1) % 2][:, 0:T], ACT.Sqrt,
                                                     bias=jobs[k - 1][4], scale=jobs[k - 1][3]).then_inc(*act_done.one())

                    def root_at(k):
                        return 2 * k + 3 if k < n - 1 else 2 * n

                    def square_at(k):
                        return 1 if k == 0 else 2 * k

                    @block.tensor
                    def _(pe):
                        for k in range(n):
                            pe.wait_ge(*act_done.at(square_at(k)))
                            if k >= 2:
                                pe.wait_ge(*act_done.at(root_at(k - 2)))
                            nc.tensor.matmul(bank[k % 2][:, 0:T], ones_m, sq[:, k % 2], start=True, stop=True).then_inc(*pe_done.one())

                    @block.vector
                    def _(dve):
                        for k in range(n):
                            dve.wait_ge(*act_done.at(root_at(k)))
                            nc.vector.reciprocal(rs[:, k % 2], rs[:, k % 2]).then_inc(*dve_done.one())
                            dve.wait_ge(*dve_done.now())
                            nc.vector.scalar_tensor_tensor(out=jobs[k][1], in0=jobs[k][0], scalar=jobs[k][2], in1=rs[:, k % 2],
                                                           op0=ALU.mult, op1=ALU.mult).then_inc(*dve_done.one())


        def project(actT, kt, n_cols, act_step, dve_step, extra=None):
            per = SLOT // kt
            n_tiles = n_cols // 128
            first = W.used
            slots = n_cols // per
            total = n_tiles + (1 if extra else 0)
            took_a, took_v = count("tile_taken_act"), count("tile_taken_dve")
            filled = count("tile_filled")
            with core.block() as block:
                @block.sync
                def _(sp):
                    W.send(sp, first + slots + SLOTS)

                @block.tensor
                def _(pe):
                    for t in range(total):
                        s = (first + t * 128 // per) % SLOTS
                        if t < n_tiles and t * 128 % per == 0:
                            pe.wait_ge(W.full[s].sem, 16 * ((first + t * 128 // per) // SLOTS + 1))
                        if t >= 4:
                            pe.wait_ge(*took_a.at(t - 3))
                            pe.wait_ge(*took_v.at(t - 3))
                        for k in range(kt):
                            if t < n_tiles:
                                c = t * 128 % per
                                lhs, m = W.view(s, kt, per)[:, k, c:c + 128], 128
                            else:
                                lhs, m = extra[0][:, k], extra[1]
                            mm = nc.tensor.matmul(bank[t % 4][0:m, 0:T], lhs, actT[:, k], start=(k == 0), stop=(k == kt - 1))
                        mm.then_inc(*filled.one())

                @block.scalar
                def _(act):
                    for t in range(total):
                        act.wait_ge(*filled.at(t + 1))
                        if t < n_tiles and (t + 1) * 128 % per == 0:
                            act.sem_inc(*W.free[(first + t * 128 // per) % SLOTS].one())
                        ins = act_step(act, t, bank[t % 4])
                        if ins is None:
                            act.sem_inc(*took_a.one())
                        else:
                            ins.then_inc(*took_a.one())

                @block.vector
                def _(dve):
                    for t in range(total):
                        dve.wait_ge(*took_a.at(t + 1))
                        ins = dve_step(dve, t, bank[t % 4])
                        if ins is None:
                            dve.sem_inc(*took_v.one())
                        else:
                            ins.then_inc(*took_v.one())
            W.used += slots

        def add_residual(dve, t, ps):
            return nc.vector.tensor_tensor(xT[:, t], xT[:, t], ps[:, 0:T], ALU.add)

        nothing = lambda eng, t, ps: None

        env = dict(nc=nc, core=core, I=I, O=O, W=W, cst=cst, par=par, xT=xT, uT=uT, eps=eps, lb=lb, w_dt=w_dt, w_gl=w_gl,
                   w_rt=w_rt, scratch=scratch, linker=linker, norm_all=norm_all, norm_each=norm_each, project=project,
                   add_residual=add_residual, nothing=nothing, ident=ident, ones=ones)
        for layer in range(4):
            norm_all(xT, KT, lambda c: par("norm_g", (layer * 2) * 8 + c), uT, f"na{layer}")
            if layer % 3 == 0:
                ssd_layer(env, layer // 3)
            elif layer == 1:
                nsa_layer(env)
            else:
                hgrn_layer(env)
            norm_all(xT, KT, lambda c: par("norm_g", (layer * 2 + 1) * 8 + c), uT, f"nm{layer}")
            moe(env, layer)
        with core.block() as block:
            @block.sync
            def _(sp):
                sp.dma_start(O["yT"], xT[:]).then_inc(*out_sent.one())
                sp.wait_ge(*out_sent.now())


def ssd_layer(env, j):
    (nc, core, I, O, W, cst, par, xT, uT, eps, scratch, linker, ident, ones) = (
        env[k] for k in ("nc", "core", "I", "O", "W", "cst", "par", "xT", "uT", "eps", "scratch", "linker", "ident", "ones"))
    count, bank = core.count, core.bank
    pe_done, act_done, dve_done, pool_done = (count(n) for n in ("pe_done", "act_done", "dve_done", "pool_done"))
    misc, out_sent = count("misc_dma", 16), count("out_sent", 16)
    state_in, state_out = [count(f"state_in{b}", 16) for b in range(HB)], [count(f"state_out{b}", 16) for b in range(HB)]
    group_in, pool_sent = [count(f"group_in{b}", 16) for b in range(2)], count("pool_sent", 16)
    n = f"s{j}_"
    with ExitStack() as layer:
        def sb(name, shape, dt=F32, ctx=layer):
            return core.sb(n + name, shape, dt, ctx)

        xbc = sb("xbc", [128, NCH, T])
        zT = sb("zT", [128, CI, T])
        tail = sb("tail", [128, NCH, 11])
        with ExitStack() as st:
            conv0 = sb("conv0", [128, NCH, 3, NB])
            dtr = sb("dtr", [32, T])
            with core.block() as block:
                @block.gpsimd
                def _(pool):
                    pool.dma_start(conv0[:], I["conv0"][j]).then_inc(*misc.one())
                    pool.wait_ge(*misc.now())

            def act_step(act, t, ps):
                if t < CI:
                    return nc.scalar.activation(zT[:, t], ps[:, 0:T], ACT.Silu)
                if t < CI + NCH:
                    return nc.scalar.copy(tail[:, t - CI], ps[:, 253:T])
                return nc.scalar.copy(dtr[:], ps[0:32, 0:T])

            def dve_step(dve, t, ps):
                if t < CI or t == CI + NCH:
                    return None
                link = linker(dve, dve_done)
                c = t - CI
                o = xbc[:, c]

                def w(k):
                    return par("conv_w", (j * NCH + c) * 4 + k)
                link(nc.vector.tensor_scalar(o, ps[:, 0:T], w(3), par("conv_b", j * NCH + c), ALU.mult, ALU.add))
                for k in (2, 1, 0):
                    s = 3 - k
                    nc.vector.scalar_tensor_tensor(out=o[:, LP:T], in0=conv0[:, c, k], scalar=w(k), in1=o[:, LP:T],
                                                   op0=ALU.mult, op1=ALU.add).then_inc(*dve_done.one())
                    ins = nc.vector.scalar_tensor_tensor(out=o[:, s:LP], in0=ps[:, 0:LP - s], scalar=w(k), in1=o[:, s:LP],
                                                         op0=ALU.mult, op1=ALU.add)
                    if k:
                        link(ins)
                return ins

            env["project"](uT, KT, 5120, act_step, dve_step, extra=(env["w_dt"][:, j], MH))

            dtT = sb("dtT", [32, T])
            daT = sb("daT", [32, T])
            acT = sb("acT", [32, LP])
            stack = sb("stack", [96, LP])
            s1, s2 = sb("s1", [32, T]), sb("s2", [32, T])
            ea1 = sb("ea1", [32, 128])
            acol = sb("acol", [32, 2])
            one_row = sb("one_row", [32, 128])
            d_ac, d_e1, d_dec = scratch("scr_ac", [32, LP]), scratch("scr_e1", [32, 128]), scratch("scr_dec", [2, 32, NB])
            with core.block() as block:
                @block.vector
                def _(dve):
                    link = linker(dve, dve_done)
                    link(nc.vector.memset(one_row[:], 1.0))
                    link(nc.vector.tensor_scalar(dtr[:], dtr[:], par("dt_bias", j)[0:32], None, ALU.add))
                    link(nc.vector.scalar_tensor_tensor(out=s1[:], in0=dtr[:], scalar=-1.0, in1=dtr[:], op0=ALU.mult, op1=ALU.max))
                    dve.wait_ge(*act_done.at(3))
                    link(nc.vector.scalar_tensor_tensor(out=dtT[:], in0=dtr[:], scalar=0.0, in1=s2[:], op0=ALU.max, op1=ALU.add))
                    link(nc.vector.tensor_scalar(acol[:, 1:2], acol[:, 0:1], -1.0, None, ALU.mult))
                    link(nc.vector.tensor_scalar(daT[:], dtT[:], acol[:, 1:2], None, ALU.mult))
                    for c in range(2):
                        link(nc.vector.tensor_tensor_scan(acT[:, 128 * c:128 * c + 128], one_row[:], daT[:, 128 * c:128 * c + 128],
                                                          0.0, ALU.mult, ALU.add))
                    link(nc.vector.tensor_copy(stack[0:32, :], dtT[:, 0:LP]))
                    link(nc.vector.tensor_scalar(stack[64:96, :], acT[:], -1.0, None, ALU.mult))
                    dve.wait_ge(*act_done.at(6))
                    link(nc.vector.tensor_tensor(stack[32:64, :], s1[:, 0:LP], dtT[:, 0:LP], ALU.mult))

                @block.scalar
                def _(act):
                    nc.scalar.activation(acol[:, 0:1], par("a_log", j)[0:32], ACT.Exp).then_inc(*act_done.one())
                    act.wait_ge(*dve_done.at(3))
                    nc.scalar.activation(s2[:], s1[:], ACT.Exp, scale=-1.0).then_inc(*act_done.one())
                    act.wait_ge(*act_done.now())
                    nc.scalar.activation(s2[:], s2[:], ACT.Ln, bias=eps[0:32, 2:3]).then_inc(*act_done.one())
                    nc.scalar.activation(xbc[:, :], xbc[:, :], ACT.Silu).then_inc(*act_done.one())
                    act.wait_ge(*dve_done.at(8))
                    for c in range(2):
                        nc.scalar.activation(s1[:, 128 * c:128 * c + 128], acT[:, 128 * c:128 * c + 128], ACT.Exp, scale=-1.0,
                                             bias=acT[:, 128 * c + 127:128 * c + 128]).then_inc(*act_done.one())
                    nc.scalar.activation(ea1[:], acT[:, 128:LP], ACT.Exp).then_inc(*act_done.one())
                    nc.scalar.activation(daT[:, LP:T], daT[:, LP:T], ACT.Exp).then_inc(*act_done.one())

                @block.gpsimd
                def _(pool):
                    pool.dma_start(O["conv_tail"][j], tail[:]).then_inc(*pool_sent.one())
                    pool.dma_start(O["conv_keep"][j], conv0[:, :, 1:3]).then_inc(*pool_sent.one())
                    pool.wait_ge(*dve_done.at(8))
                    pool.dma_start(d_ac, acT[:]).then_inc(*misc.one())
                    pool.dma_start(d_dec[0], dtT[:, LP:T]).then_inc(*misc.one())
                    pool.wait_ge(*act_done.at(8))
                    pool.dma_start(d_e1, ea1[:]).then_inc(*misc.one())
                    pool.dma_start(d_dec[1], daT[:, LP:T]).then_inc(*misc.one())
                    pool.wait_ge(*misc.now())
                    pool.wait_ge(*pool_sent.now())

        with ExitStack() as st:
            acb = sb("acb", [128, MH, 128], ctx=st)
            e1b = sb("e1b", [128, CI, 128], ctx=st)
            nat = sb("nat", [128, 96], ctx=st)
            xdt = sb("xdt", [128, DI], ctx=st)
            xdd = sb("xdd", [128, DI], ctx=st)
            bn = sb("bn", [128, 512], ctx=st)
            s0 = sb("s0", [128, DI], ctx=st)
            cdb = sb("cdb", [128, MH], ctx=st)
            yt = sb("yt", [128, 512], ctx=st)
            for c in range(2):
                lo = 128 * c
                tl = slice(lo, lo + 128)
                with core.block() as block:
                    @block.gpsimd
                    def _(pool):
                        pool.dma_start(acb[:], d_ac[:, tl].rearrange("(o h) l -> o h l", o=1).to_broadcast([128, MH, 128])).then_inc(*misc.one())
                        if c == 1:
                            for h in range(2):
                                pool.dma_start(e1b[64 * h:64 * h + 64], d_e1.rearrange("(o c h) l -> h o c l", h=2, o=1)[h].to_broadcast([64, CI, 128])).then_inc(*misc.one())
                        pool.wait_ge(*misc.now())

                    @block.tensor
                    def _(pe):
                        nc.tensor.transpose(bank[0][:, 0:96], stack[:, tl], ident[0:96, 0:96]).then_inc(*pe_done.one())
                        for g in range(NG):
                            mm = nc.tensor.transpose(bank[1][:, 128 * g:128 * g + 128], xbc[:, CI + g, tl], ident)
                        mm.then_inc(*pe_done.one())
                        for g in range(NG):
                            mm = nc.tensor.matmul(bank[2][:, 128 * g:128 * g + 128], xbc[:, CI + g, tl], xbc[:, CI + NG + g, tl], start=True, stop=True)
                        mm.then_inc(*pe_done.one())
                        for q in range(4):
                            for i in range(4):
                                mm = nc.tensor.transpose(bank[3 + q][:, 128 * i:128 * i + 128], xbc[:, 4 * q + i, tl], ident)
                            mm.then_inc(*pe_done.one())

                    @block.vector
                    def _(dve):
                        dve.wait_ge(*pe_done.at(1))
                        nc.vector.tensor_copy(nat[:], bank[0][:, 0:96]).then_inc(*dve_done.one())
                        dve.wait_ge(*pe_done.at(2))
                        nc.vector.tensor_copy(bn[:], bank[1][:]).then_inc(*dve_done.one())
                        dve.wait_ge(*dve_done.at(1))
                        for q in range(4):
                            dve.wait_ge(*pe_done.at(4 + q))
                            src = bank[3 + q][:].rearrange("p (h d) -> p h d", h=8)
                            for out, r in ((xdt, 0), (xdd, 32)):
                                nc.vector.tensor_tensor(out[:, 512 * q:512 * q + 512].rearrange("p (h d) -> p h d", h=8), src,
                                                        nat[:, r + 8 * q:r + 8 * q + 8].rearrange("p (h o) -> p h o", o=1).to_broadcast([128, 8, 64]),
                                                        ALU.mult).then_inc(*dve_done.one())
                        dve.wait_ge(*misc.now())
                        dve.wait_ge(*act_done.at(1))
                        for g in range(NG):
                            nc.vector.tensor_tensor(acb[:, 8 * g:8 * g + 8], acb[:, 8 * g:8 * g + 8],
                                                    cst("ssd_mask").rearrange("p (o l) -> p o l", o=1).to_broadcast([128, 8, 128]),
                                                    ALU.add).then_inc(*dve_done.one())
                        for g in range(NG):
                            dve.wait_ge(*act_done.at(1 + 8 * (g + 1)))
                            nc.vector.tensor_tensor(acb[:, 8 * g:8 * g + 8], acb[:, 8 * g:8 * g + 8],
                                                    bank[2][:, 128 * g:128 * g + 128].rearrange("p (o l) -> p o l", o=1).to_broadcast([128, 8, 128]),
                                                    ALU.mult).then_inc(*dve_done.one())

                    @block.scalar
                    def _(act):
                        act.wait_ge(*misc.now())
                        nc.scalar.activation(cdb[:], acb[:, :, 127:128].rearrange("p h o -> p (h o)"), ACT.Exp).then_inc(*act_done.one())
                        for g in range(NG):
                            act.wait_ge(*dve_done.at(11 + g))
                            for h in range(8 * g, 8 * g + 8):
                                nc.scalar.activation(acb[:, h], acb[:, h], ACT.Exp, bias=nat[:, 64 + h:65 + h]).then_inc(*act_done.one())

                with core.block() as block:
                    @block.tensor
                    def _(pe):
                        for q in range(4):
                            for i in range(4):
                                for h in range(2):
                                    hd = 2 * (4 * q + i) + h
                                    mm = nc.tensor.matmul(bank[q % 2][64 * h:64 * h + 64, 128 * i:128 * i + 128], xdt[:, 64 * hd:64 * hd + 64],
                                                          acb[:, hd], start=True, stop=True)
                            mm.then_inc(*pe_done.one())
                            if c == 1:
                                for i in range(4):
                                    k = 4 * q + i
                                    mm = nc.tensor.matmul(bank[2 + q % 2][:, 128 * i:128 * i + 128], s0[:, 128 * k:128 * k + 128],
                                                          xbc[:, CI + NG + q, tl], start=True, stop=True)
                                mm.then_inc(*pe_done.one())
                            nc.tensor.matmul(bank[4 + q][:], bn[:, 128 * q:128 * q + 128], xdd[:, 512 * q:512 * q + 512], start=True,
                                             stop=True).then_inc(*pe_done.one())
                            if q in (1, 2):
                                pe.wait_ge(*dve_done.at((5 + c) * q))

                    @block.vector
                    def _(dve):
                        link = linker(dve, dve_done)
                        per = 2 + c
                        for q in range(4):
                            dve.wait_ge(*pe_done.at(per * q + 1))
                            for i in range(4):
                                k = 4 * q + i
                                nc.vector.scalar_tensor_tensor(out=xbc[:, k, tl], in0=xbc[:, k, tl], scalar=par("m_d", j * CI + k),
                                                               in1=bank[q % 2][:, 128 * i:128 * i + 128], op0=ALU.mult,
                                                               op1=ALU.add).then_inc(*dve_done.one())
                            if c == 1:
                                dve.wait_ge(*pe_done.at(per * q + 2))
                                link(nc.vector.tensor_tensor(yt[:].rearrange("p (k l) -> p k l", k=4), bank[2 + q % 2][:].rearrange("p (k l) -> p k l", k=4),
                                                             e1b[:, 4 * q:4 * q + 4], ALU.mult))
                                link(nc.vector.tensor_tensor(xbc[:, 4 * q:4 * q + 4, tl], xbc[:, 4 * q:4 * q + 4, tl],
                                                             yt[:].rearrange("p (k l) -> p k l", k=4), ALU.add))
                            else:
                                dve.wait_ge(*pe_done.at(per * q + 2))
                                link(nc.vector.tensor_copy(s0[:, 512 * q:512 * q + 512], bank[4 + q][:]))
                        if c == 1:
                            for q in range(4):
                                sl = s0[:, 512 * q:512 * q + 512]
                                dve.wait_ge(*pe_done.at(12))
                                link(nc.vector.tensor_tensor(sl.rearrange("p (h d) -> p h d", h=8), sl.rearrange("p (h d) -> p h d", h=8),
                                                             cdb[:, 8 * q:8 * q + 8].rearrange("p (h o) -> p h o", o=1).to_broadcast([128, 8, 64]), ALU.mult))
                                link(nc.vector.tensor_tensor(sl, sl, bank[4 + q][:], ALU.add))
            with core.block() as block:
                @block.sync
                def _(sp):
                    sp.dma_start(O["ssm_p"][j], s0[:]).then_inc(*out_sent.one())
                    sp.wait_ge(*out_sent.now())

        with ExitStack() as st:
            dtb = sb("dtb", [128, CI, NB], ctx=st)
            dab = sb("dab", [128, CI, NB], ctx=st)
            bcr = sb("bcr", [64, 128], ctx=st)
            bcp = sb("bcp", [128, 64], ctx=st)
            bg, cg = sb("bg", [128, 2, NB, 128], ctx=st), sb("cg", [128, 2, NB, 128], ctx=st)
            hbuf = sb("hbuf", [128, HB, 2, NB, 128], ctx=st)
            tmp = sb("tmp", [128, 2, NB, 128], ctx=st)
            ys = sb("ys", [128, CI, NB], ctx=st)
            d_bc = scratch("scr_bc", [64, 128])

            def load_state(sp, k):
                sp.dma_start(hbuf[:, k % HB], I["ssm0"][j, :, 2 * k:2 * k + 2]).then_inc(*state_in[k % HB].one())
            with core.block() as block:
                @block.sync
                def _(sp):
                    for k in range(HB - 1):
                        load_state(sp, k)

                @block.tensor
                def _(pe):
                    pe.wait_ge(*dve_done.at(1))
                    nc.tensor.transpose(bank[0][0:64, 0:128], bcp[:], ident).then_inc(*pe_done.one())

                @block.vector
                def _(dve):
                    nc.vector.tensor_copy(bcp[:].rearrange("p (k b) -> p k b", k=8), xbc[:, CI:NCH, LP:T]).then_inc(*dve_done.one())
                    dve.wait_ge(*pe_done.at(1))
                    nc.vector.tensor_copy(bcr[:], bank[0][0:64, 0:128]).then_inc(*dve_done.one())
                    dve.wait_ge(*misc.at(4))
                    nc.vector.tensor_tensor(dtb[:], dtb[:], xbc[:, 0:CI, LP:T], ALU.mult).then_inc(*dve_done.one())

                @block.gpsimd
                def _(pool):
                    for k, t in ((0, dtb), (1, dab)):
                        for h in range(2):
                            pool.dma_start(t[64 * h:64 * h + 64], d_dec[k].rearrange("(o c h) b -> h o c b", h=2, o=1)[h].to_broadcast([64, CI, NB])).then_inc(*misc.one())
                    pool.wait_ge(*dve_done.at(2))
                    pool.dma_start(d_bc, bcr[:]).then_inc(*pool_sent.one())
                    pool.wait_ge(*misc.now())
                    pool.wait_ge(*pool_sent.now())

            with core.block() as block:
                @block.gpsimd
                def _(pool):
                    for g in range(NG):
                        if g >= 2:
                            pool.wait_ge(*dve_done.at(6 * (g - 1)))
                        for t, r in ((bg, 0), (cg, 32)):
                            pool.dma_start(t[:, g % 2].rearrange("p b n -> p (b n)"), d_bc[r + 8 * g:r + 8 * g + 8].rearrange("(o b) n -> o (b n)", o=1)
                                           .to_broadcast([128, NB * 128])).then_inc(*group_in[g % 2].one())

                @block.sync
                def _(sp):
                    for k in range(8):
                        if k + HB - 1 < 8:
                            if k >= 1:
                                sp.wait_ge(*state_out[(k - 1) % HB].at((k - 1) // HB + 1))
                                sp.wait_ge(*dve_done.at(3 * (k - 1) + 2))
                            load_state(sp, k + HB - 1)
                        sp.wait_ge(*dve_done.at(3 * k + 1))
                        sp.dma_start(O["ssm_s"][j, :, 2 * k:2 * k + 2], hbuf[:, k % HB]).then_inc(*state_out[k % HB].one())
                    for b in range(HB):
                        sp.wait_ge(*state_out[b].now())

                @block.scalar
                def _(act):
                    for k in range(8):
                        act.wait_ge(*state_in[k % HB].at(k // HB + (1 if k % HB == HB - 1 else 0)))
                        for q in range(2):
                            for b in range(NB):
                                h = hbuf[:, k % HB, q, b]
                                a = nc.scalar.activation(h, h, ACT.Copy, scale=dab[:, 2 * k + q, b:b + 1])
                        a.then_inc(*act_done.one())

                @block.vector
                def _(dve):
                    link = linker(dve, dve_done)
                    for k in range(8):
                        g = k // 2
                        dve.wait_ge(*group_in[g % 2].at(2 * (g // 2 + 1)))
                        dve.wait_ge(*act_done.at(k + 1))
                        for q in range(2):
                            for b in range(NB):
                                h = hbuf[:, k % HB, q, b]
                                add = nc.vector.scalar_tensor_tensor(out=h, in0=bg[:, g % 2, b], scalar=dtb[:, 2 * k + q, b:b + 1], in1=h,
                                                                     op0=ALU.mult, op1=ALU.add)
                        link(add)
                        for q in range(2):
                            mul = nc.vector.tensor_tensor(tmp[:, q], hbuf[:, k % HB, q], cg[:, g % 2], ALU.mult)
                        link(mul)
                        link(nc.vector.tensor_reduce(ys[:, 2 * k:2 * k + 2], tmp[:], AX.X, ALU.add))
            with core.block() as block:
                @block.vector
                def _(dve):
                    link = linker(dve, dve_done)
                    for k in range(CI):
                        nc.vector.scalar_tensor_tensor(out=xbc[:, k, LP:T], in0=xbc[:, k, LP:T], scalar=par("m_d", j * CI + k), in1=ys[:, k],
                                                       op0=ALU.mult, op1=ALU.add).then_inc(*dve_done.one())
                    dve.wait_ge(*dve_done.now())
                    link(nc.vector.tensor_tensor(zT[:], zT[:], xbc[:, 0:CI], ALU.mult))
        env["norm_all"](zT, CI, lambda c: par("m_norm_g", j * CI + c), zT, n + "n")
        env["project"](zT, CI, D, env["nothing"], env["add_residual"])


def moe(env, layer):
    (nc, core, I, W, cst, par, xT, uT, scratch, linker, ident, ones) = (
        env[k] for k in ("nc", "core", "I", "W", "cst", "par", "xT", "uT", "scratch", "linker", "ident", "ones"))
    count, bank = core.count, core.bank
    pe_done, act_done, dve_done = (count(n) for n in ("pe_done", "act_done", "dve_done"))
    n = f"e{layer}_"
    TT = 3
    tok0 = (0, 128, T - 128)
    PAIR = 2 * CAP
    with ExitStack() as st:
        def sb(name, shape, dt=F32):
            return core.sb(n + name, shape, dt, st)

        lgT = sb("lgT", [20, T])
        lg = sb("lg", [128, TT, 20])
        m4 = sb("m4", [128, TT, 4])
        ex = sb("ex", [128, TT, 4])
        v = sb("v", [128, TT, 8])
        le, k1, k2 = sb("le", [128, TT, 4]), sb("k1", [128, TT, 4]), sb("k2", [128, TT, 4])
        leg = sb("leg", [128, TT, 16])
        comb = sb("comb", [128, TT, 16])
        taken = sb("taken", [128, TT + 1, NE])
        row = sb("row", [128, TT * NE])
        most = sb("most", [128, 1])
        crowded = sb("crowded", [1, 1], mybir.dt.int32)
        u_nat = sb("u_nat", [128, TT, D])
        to_row = sb("to_row", [128, TT, NE * CAP])

        def one(c):
            return v[:, :, c:c + 1]

        def four(c):
            return v[:, :, c:c + 1].to_broadcast([128, TT, 4])
        down = cst("four_down").rearrange("p (o e) -> p o e", o=1).to_broadcast([128, TT, 4])
        mark = {}
        with core.block() as block:
            @block.vector
            def _(dve):
                link = linker(dve, dve_done)
                TTn = nc.vector.tensor_tensor

                def first_of(mask):
                    link(TTn(mask, mask, down, ALU.mult))
                    link(nc.vector.tensor_reduce(one(7), mask, AX.X, ALU.max))
                    link(TTn(mask, mask, four(7), ALU.is_equal))
                link(nc.vector.memset(taken[:, TT], 0.0))
                dve.wait_ge(*pe_done.at(2))
                link(TTn(lg[:], bank[1][:, 0:96].rearrange("p (t c) -> p t c", t=TT)[:, :, 0:20],
                         par("moe_b", 20 * layer, 20).rearrange("p (o c) -> p o c", o=1).to_broadcast([128, TT, 20]), ALU.add))
                link(nc.vector.tensor_reduce(one(0), lg[:, :, 0:4], AX.X, ALU.max))
                link(TTn(ex[:], lg[:, :, 0:4], four(0), ALU.subtract))
                mark["group exponents"] = dve_done.now()
                link(TTn(m4[:], lg[:, :, 0:4], four(0), ALU.is_equal))
                first_of(m4[:])
                for t in range(TT):
                    link(TTn(leg[:, t].rearrange("p (g e) -> p g e", g=4), lg[:, t, 4:20].rearrange("p (g e) -> p g e", g=4),
                             m4[:, t].rearrange("p (g o) -> p g o", o=1).to_broadcast([128, 4, 4]), ALU.mult))
                link(nc.vector.tensor_reduce(le[:], leg[:].rearrange("p t (g e) -> p t e g", g=4), AX.X, ALU.add))
                link(nc.vector.tensor_reduce(one(1), le[:], AX.X, ALU.max))
                link(TTn(k1[:], le[:], four(1), ALU.is_equal))
                first_of(k1[:])
                link(nc.vector.scalar_tensor_tensor(out=le[:], in0=k1[:], scalar=NEG, in1=le[:], op0=ALU.mult, op1=ALU.add))
                link(nc.vector.tensor_reduce(one(2), le[:], AX.X, ALU.max))
                link(TTn(k2[:], le[:], four(2), ALU.is_equal))
                link(TTn(one(4), one(2), one(1), ALU.subtract))
                mark["second's exponent"] = dve_done.now()
                first_of(k2[:])
                link(TTn(leg[:, :, 0:4], k1[:], k2[:], ALU.add))
                for t in range(TT):
                    link(TTn(taken[:, t].rearrange("p (g e) -> p g e", g=4), m4[:, t].rearrange("p (g o) -> p g o", o=1).to_broadcast([128, 4, 4]),
                             leg[:, t, 0:4].rearrange("p (o e) -> p o e", o=1).to_broadcast([128, 4, 4]), ALU.mult))
                link(nc.vector.tensor_scalar(taken[:, TT - 1], taken[:, TT - 1], cst("last_rows"), None, ALU.mult))
                mark["taken"] = dve_done.now()
                dve.wait_ge(*act_done.at(8))
                link(nc.vector.tensor_reduce(one(3), ex[:], AX.X, ALU.add))
                link(nc.vector.scalar_tensor_tensor(out=one(3), in0=one(4), scalar=1.0, in1=one(3), op0=ALU.add, op1=ALU.mult))
                link(nc.vector.reciprocal(one(3), one(3)))
                link(TTn(k2[:], k2[:], four(4), ALU.mult))
                link(TTn(k1[:], k1[:], k2[:], ALU.add))
                link(TTn(k1[:], k1[:], four(3), ALU.mult))
                for t in range(TT):
                    link(TTn(comb[:, t].rearrange("p (g e) -> p g e", g=4), m4[:, t].rearrange("p (g o) -> p g o", o=1).to_broadcast([128, 4, 4]),
                             k1[:, t].rearrange("p (o e) -> p o e", o=1).to_broadcast([128, 4, 4]), ALU.mult))
                dve.wait_ge(*pe_done.at(9))
                link(nc.vector.scalar_tensor_tensor(out=row[:], in0=taken[:, 0:TT].rearrange("p t e -> p (t e)"), scalar=-float(UNTAKEN),
                                                    in1=bank[0][:, 0:TT * NE], op0=ALU.mult, op1=ALU.add))
                link(nc.vector.tensor_reduce(most[:], bank[0][:, TT * NE:(TT + 1) * NE], AX.X, ALU.max))
                link(nc.vector.tensor_scalar(crowded[:], most[0:1], CROWDED_FROM + 0.5, None, ALU.is_gt))
                link(TTn(to_row[:].rearrange("p t (e r) -> p (t e) r", r=CAP), cst("slot_no").rearrange("p (o r) -> p o r", o=1).to_broadcast([128, TT * NE, CAP]),
                         row[:].rearrange("p (m o) -> p m o", o=1).to_broadcast([128, TT * NE, CAP]), ALU.is_equal))

            @block.tensor
            def _(pe):
                for k in range(KT):
                    mm = nc.tensor.matmul(bank[0][0:20, 0:T], env["w_rt"][:, layer, k], uT[:, k], start=(k == 0), stop=(k == KT - 1))
                mm.then_inc(*pe_done.one())
                pe.wait_ge(*act_done.at(1))
                for t in range(TT):
                    mm = nc.tensor.transpose(bank[1][:, 32 * t:32 * t + 20], lgT[:, tok0[t]:tok0[t] + 128], ident[0:20, 0:20])
                mm.then_inc(*pe_done.one())
                for t in range(TT):
                    for h in range(2):
                        for k in range(4):
                            mm = nc.tensor.transpose(bank[2 + 2 * t + h][:, 128 * k:128 * k + 128], uT[:, 4 * h + k, tok0[t]:tok0[t] + 128], ident)
                        mm.then_inc(*pe_done.one())
                pe.wait_ge(*mark["taken"])
                at = taken[:].rearrange("p t e -> p (t e)")
                nc.tensor.matmul(bank[0][:, 0:(TT + 1) * NE], cst("earlier"), at, start=True, stop=False)
                for d in range(1, TT + 1):
                    mm = nc.tensor.matmul(bank[0][:, d * NE:(TT + 1) * NE], ones, at[:, 0:(TT + 1 - d) * NE], start=False, stop=(d == TT))
                mm.then_inc(*pe_done.one())

            @block.scalar
            def _(act):
                act.wait_ge(*pe_done.at(1))
                nc.scalar.activation(lgT[:], bank[0][0:20, 0:T], ACT.Copy).then_inc(*act_done.one())

                def unload(q):
                    act.wait_ge(*pe_done.at(3 + q))
                    nc.scalar.activation(u_nat[:, q // 2, 512 * (q % 2):512 * (q % 2) + 512], bank[2 + q][:], ACT.Copy).then_inc(*act_done.one())
                unload(0)
                unload(1)
                act.wait_ge(*mark["group exponents"])
                nc.scalar.activation(ex[:], ex[:], ACT.Exp).then_inc(*act_done.one())
                for q in range(2, 5):
                    unload(q)
                act.wait_ge(*mark["second's exponent"])
                nc.scalar.activation(one(4), one(4), ACT.Exp).then_inc(*act_done.one())
                unload(5)

        combT = sb("combT", [16, T])
        combb = sb("combb", [128, NE, T])
        d_comb = scratch("scr_comb", [16, T])
        hs = sb("hs", [128, 4, T])
        sl = sb("sl", [128, 2, T])
        w_row = sb("w_row", [128, TT, NE * CAP])
        from_row = sb("from_row", [PAIR, NE // 2, T])
        xg = sb("xg", [128, KT, PAIR])
        sg = sb("sg", [CAP, FF])
        hg = sb("hg", [CAP, FF])
        hT = sb("hT", [128, 4, CAP])
        yg = sb("yg", [PAIR, D])
        first = W.used
        slot = [(first + k) % SLOTS for k in range(6)]
        fills = [(first + k) // SLOTS for k in range(6)]

        h_filled, y_filled, comb_turned = count("h_filled"), count("y_filled"), count("comb_turned")
        silu_done = count("silu_done")
        h_used, weighted, y_used, combT_ready = count("h_used"), count("weighted"), count("y_used"), count("combT_ready")
        comb_spread = count("comb_spread", 16)
        up_filled, turned, down_filled = count("up_filled"), count("turned"), count("down_filled")
        gathered, back_filled, weights_turned = count("gathered"), count("back_filled"), count("weights_turned")
        gate_ready, hT_ready, yg_ready, from_row_ready = count("gate_ready"), count("hT_ready"), count("yg_ready"), count("from_row_ready")
        hg_ready, xg_ready, x_added, w_row_ready = count("hg_ready"), count("xg_ready"), count("x_added"), count("w_row_ready")
        dense_total = {h_filled: 4 * NE, y_filled: 8 * NE, comb_turned: 1, silu_done: 4 * NE, h_used: 4 * NE + 2, weighted: 4 * NE + 2,
                       y_used: 8 * NE + 4, combT_ready: 2, comb_spread: 32}
        gathered_total = {up_filled: 2 * NE, turned: NE, down_filled: 2 * NE, gathered: NE, back_filled: 8 * NE // 2, weights_turned: NE // 2,
                          gate_ready: 2 * NE, hT_ready: NE, yg_ready: 2 * NE + 2, from_row_ready: NE // 2,
                          hg_ready: 2 * NE, xg_ready: NE, x_added: 8 * NE // 2 + 4, w_row_ready: 1}

        def leave(eng, totals, counts):
            for c in counts:
                eng.sem_inc(c.sem, totals[c])
        PAIRS = NE // 2
        with core.block() as block:
            @block.sync
            def _(sp):
                assert W.sent == first + 6, (W.sent, first)
                with sp.Fori(0, NE - 1) as e:
                    for k in range(6):
                        s = slot[k]
                        sp.wait_ge(W.free[s].sem, e + (fills[k] + 1))
                        if k < 4:
                            w = I[("moe_w1", "moe_w3")[k % 2]][layer, bass.ds(e + 1, 1), :, 256 * (k // 2):256 * (k // 2) + 256]
                            view = W.view(s, KT, 256)
                        else:
                            w = I["moe_w2"][layer, bass.ds(e + 1, 1), :, 512 * (k - 4):512 * (k - 4) + 512]
                            view = W.view(s, FF // 128, 512)
                        sp.dma_start(view, w.rearrange("e (k p) c -> p (e k) c", p=128)).then_inc(W.full[s].sem, 16)
                W.sent = first + 6 * NE
                W.send(sp, first + 6 * NE + SLOTS)

            @block.tensor
            def _(pe):
                def gather(p, h, chunks=range(4)):
                    for c in chunks:
                        for t in range(TT):
                            k = 4 * h + c
                            mm = nc.tensor.matmul(bank[(7, 0)[h]][:, PAIR * c:PAIR * c + PAIR], u_nat[:, t, 128 * k:128 * k + 128],
                                                  to_row[:, t, bass.ds(p * PAIR, PAIR)], start=(t == 0), stop=(t == TT - 1))
                    if c == 3:
                        mm.then_inc(*gathered.one())

                def pair(p, last):
                    pe.wait_ge(*xg_ready.of(p, 2, 2))
                    for j in range(2):
                        for h in range(2):
                            for i in (2 * h, 2 * h + 1):
                                pe.wait_ge(W.full[slot[i]].sem, p * 32 + (16 * j + 16 * (fills[i] + 1)))
                                if j == 0:
                                    pe.wait_ge(*x_added.of(p, 8, 1 + 2 * h))
                                w = W.view(slot[i], KT, 256)
                                for k in range(KT):
                                    mm = nc.tensor.matmul(bank[i][0:CAP, 0:256], xg[:, k, CAP * j:CAP * j + CAP], w[:, k], start=(k == 0),
                                                          stop=(k == KT - 1))
                            mm.then_inc(*up_filled.one())
                        pe.wait_ge(*hg_ready.of(p, 4, 2 * j + 1))
                        if not last:
                            gather(p + 1, j, range(2))
                        if j == 0:
                            pe.wait_ge(*x_added.of(p, 8, 4))
                        pe.wait_ge(*hg_ready.of(p, 4, 2 * j + 2))
                        if not last:
                            gather(p + 1, j, range(2, 3))
                        for f in range(4):
                            mm = nc.tensor.transpose(bank[4][:, CAP * f:CAP * f + CAP], hg[:, 128 * f:128 * f + 128], ident[0:CAP, 0:CAP])
                        mm.then_inc(*turned.one())
                        if not last:
                            gather(p + 1, j, range(3, 4))
                        pe.wait_ge(*hT_ready.of(p, 2, j + 1))
                        for h in range(2):
                            pe.wait_ge(W.full[slot[4 + h]].sem, p * 32 + (16 * j + 16 * (fills[4 + h] + 1)))
                            pe.wait_ge(*yg_ready.of(p, 4, 2 * j + h + 1))
                            w = W.view(slot[4 + h], 4, 512)
                            for f in range(4):
                                mm = nc.tensor.matmul(bank[5 + h][0:CAP, :], hT[:, f], w[:, f], start=(f == 0), stop=(f == 3))
                            mm.then_inc(*down_filled.one())
                    for c in range(KT):
                        if c % 4 == 0:
                            pe.wait_ge(*yg_ready.of(p, 4, 5 + c // 4))
                        pe.wait_ge(*x_added.of(p, 8, c + 1))
                        nc.tensor.matmul(bank[1 + c % 4][:, 0:T], yg[:, 128 * c:128 * c + 128],
                                         from_row[:, bass.ds(p, 1)].rearrange("r o t -> r (o t)"), start=True, stop=True).then_inc(*back_filled.one())

                def gathered_program():
                    gather(0, 0)
                    gather(0, 1)
                    pe.wait_ge(*w_row_ready.at(1))
                    for q in range(PAIRS):
                        if q >= 4:
                            pe.wait_ge(*from_row_ready.at(q - 3))
                        for t in (2, 1, 0):
                            mm = nc.tensor.transpose(bank[1 + q % 4][:, tok0[t]:tok0[t] + 128], w_row[:, t, PAIR * q:PAIR * q + PAIR], ident)
                        mm.then_inc(*weights_turned.one())
                    pe.wait_ge(*from_row_ready.at(PAIRS))
                    with pe.Fori(0, PAIRS - 1) as p, ExitStack() as turn:
                        for c, per in ((up_filled, 4), (turned, 2), (down_filled, 4), (gathered, 2), (back_filled, 8)):
                            turn.enter_context(c.each(p, per, PAIRS - 1))
                        pair(p, False)
                    pair(PAIRS - 1, True)
                    leave(pe, dense_total, (h_filled, y_filled, comb_turned))

                def dense_program():
                    for t in range(TT):
                        mm = nc.tensor.transpose(bank[1][0:16, 128 * t:128 * t + 128], comb[:, t], ident)
                    mm.then_inc(*comb_turned.one())
                    with pe.Fori(0, NE) as e, h_filled.each(e, 4, NE), y_filled.each(e, 8, NE):
                        for f in range(4):
                            sa, sb_ = slot[2 * (f // 2)], slot[2 * (f // 2) + 1]
                            if f % 2 == 0:
                                pe.wait_ge(W.full[sa].sem, e * 16 + 16 * (fills[2 * (f // 2)] + 1))
                                pe.wait_ge(W.full[sb_].sem, e * 16 + 16 * (fills[2 * (f // 2) + 1] + 1))
                            pe.wait_ge(h_used.sem, e * 4 + (h_used.start + f + 1))
                            for s, b in ((sa, 0), (sb_, 2)):
                                w = W.view(s, KT, 256)
                                for k in range(KT):
                                    mm = nc.tensor.matmul(bank[b + f % 2][:, 0:T], w[:, k, 128 * (f % 2):128 * (f % 2) + 128], uT[:, k],
                                                          start=(k == 0), stop=(k == KT - 1))
                            mm.then_inc(*h_filled.one())
                        pe.wait_ge(h_used.sem, e * 4 + (h_used.start + 2 + 3))
                        pe.wait_ge(W.full[slot[4]].sem, e * 16 + 16 * (fills[4] + 1))
                        w = W.view(slot[4], 4, 512)
                        for c in range(3):
                            pe.wait_ge(y_used.sem, e * 8 + (y_used.start + c + 1))
                            for f in range(3):
                                nc.tensor.matmul(bank[4 + c][:, 0:T], w[:, f, 128 * c:128 * c + 128], hs[:, f], start=(f == 0), stop=False)
                        pe.wait_ge(h_used.sem, e * 4 + (h_used.start + 2 + 4))
                        for c in range(3):
                            nc.tensor.matmul(bank[4 + c][:, 0:T], w[:, 3, 128 * c:128 * c + 128], hs[:, 3], start=False,
                                             stop=True).then_inc(*y_filled.one())
                        for c in range(3, 8):
                            s = slot[4 + c // 4]
                            if c == 4:
                                pe.wait_ge(W.full[s].sem, e * 16 + 16 * (fills[5] + 1))
                            pe.wait_ge(y_used.sem, e * 8 + (y_used.start + c + 1))
                            w = W.view(s, 4, 512)
                            for f in range(4):
                                mm = nc.tensor.matmul(bank[4 + c % 4][:, 0:T], w[:, f, 128 * (c % 4):128 * (c % 4) + 128], hs[:, f], start=(f == 0),
                                                      stop=(f == 3))
                            mm.then_inc(*y_filled.one())
                    leave(pe, gathered_total, (up_filled, turned, down_filled, gathered, back_filled, weights_turned))
                is_crowded = pe.value_load(crowded[0:1, 0:1], min_val=0, max_val=1)
                with pe.If(is_crowded < 1):
                    gathered_program()
                with pe.If(is_crowded > 0):
                    dense_program()

            @block.scalar
            def _(act):
                def pair(p):
                    for j in range(2):
                        for h in range(2):
                            act.wait_ge(*up_filled.of(p, 4, 2 * j + h + 1))
                            for s in slot[2 * h:2 * h + 2]:
                                act.sem_inc(W.free[s].sem, 1)
                            nc.scalar.activation(sg[:, 256 * h:256 * h + 256], bank[2 * h][0:CAP, 0:256], ACT.Silu).then_inc(*gate_ready.one())
                        act.wait_ge(*turned.of(p, 2, j + 1))
                        nc.scalar.activation(hT[:], bank[4][:, 0:4 * CAP].rearrange("p (f r) -> p f r", f=4), ACT.Copy).then_inc(*hT_ready.one())
                        for h in range(2):
                            act.wait_ge(*down_filled.of(p, 4, 2 * j + h + 1))
                            act.sem_inc(W.free[slot[4 + h]].sem, 1)
                            nc.scalar.activation(yg[CAP * j:CAP * j + CAP, 512 * h:512 * h + 512], bank[5 + h][0:CAP, :],
                                                 ACT.Copy).then_inc(*yg_ready.one())

                def gathered_program():
                    for _ in range(2):
                        act.sem_inc(*yg_ready.one())
                    for q in range(PAIRS):
                        act.wait_ge(*weights_turned.at(q + 1))
                        nc.scalar.activation(from_row[:, q], bank[1 + q % 4][:, 0:T], ACT.Copy).then_inc(*from_row_ready.one())
                    with act.Fori(0, PAIRS) as p, gate_ready.each(p, 4, PAIRS), hT_ready.each(p, 2, PAIRS), yg_ready.each(p, 4, PAIRS):
                        pair(p)
                    leave(act, dense_total, (silu_done, comb_spread))

                def dense_program():
                    act.wait_ge(*combT_ready.at(2))
                    act.dma_start(d_comb, combT[:]).then_inc(*comb_spread.one())
                    act.wait_ge(*comb_spread.now())
                    act.dma_start(combb[:], d_comb.rearrange("(o e) t -> o e t", o=1).to_broadcast([128, NE, T])).then_inc(*comb_spread.one())
                    with act.Fori(0, NE) as e, silu_done.each(e, 4, NE):
                        for f in range(4):
                            act.wait_ge(h_filled.sem, e * 4 + (h_filled.start + f + 1))
                            if f % 2:
                                for s in slot[f - 1:f + 1]:
                                    act.sem_inc(W.free[s].sem, 1)
                            act.wait_ge(weighted.sem, e * 4 + (weighted.start + f + 1))
                            nc.scalar.activation(sl[:, f % 2], bank[f % 2][:, 0:T], ACT.Silu).then_inc(*silu_done.one())
                    leave(act, gathered_total, (gate_ready, hT_ready, yg_ready, from_row_ready))
                is_crowded = act.value_load(crowded[0:1, 0:1], min_val=0, max_val=1)
                with act.If(is_crowded < 1):
                    gathered_program()
                with act.If(is_crowded > 0):
                    dense_program()

            @block.vector
            def _(dve):
                def pair(p, last):
                    for j in range(2):
                        for h in range(2):
                            dve.wait_ge(*gate_ready.of(p, 4, 2 * j + h + 1))
                            nc.vector.tensor_tensor(hg[:, 256 * h:256 * h + 256], sg[:, 256 * h:256 * h + 256], bank[2 * h + 1][0:CAP, 0:256],
                                                    ALU.mult).then_inc(*hg_ready.one())
                    if not last:
                        for h in range(2):
                            dve.wait_ge(*gathered.of(p, 2, 3 + h))
                            nc.vector.tensor_copy(xg[:, 4 * h:4 * h + 4], bank[(7, 0)[h]][:].rearrange("p (k r) -> p k r", k=4)).then_inc(*xg_ready.one())
                    for c in range(KT):
                        dve.wait_ge(*back_filled.of(p, 8, c + 1))
                        nc.vector.tensor_tensor(xT[:, c], xT[:, c], bank[1 + c % 4][:, 0:T], ALU.add).then_inc(*x_added.one())

                def gathered_program():
                    for _ in range(4):
                        dve.sem_inc(*x_added.one())
                    nc.vector.tensor_tensor(w_row[:].rearrange("p t (e r) -> p (t e) r", r=CAP), to_row[:].rearrange("p t (e r) -> p (t e) r", r=CAP),
                                            comb[:].rearrange("p t (e o) -> p (t e) o", o=1).to_broadcast([128, TT * NE, CAP]),
                                            ALU.mult).then_inc(*w_row_ready.one())
                    for h in range(2):
                        dve.wait_ge(*gathered.at(1 + h))
                        nc.vector.tensor_copy(xg[:, 4 * h:4 * h + 4], bank[(7, 0)[h]][:].rearrange("p (k r) -> p k r", k=4)).then_inc(*xg_ready.one())
                    with dve.Fori(0, PAIRS - 1) as p, hg_ready.each(p, 4, PAIRS - 1), xg_ready.each(p, 2, PAIRS - 1), x_added.each(p, 8, PAIRS - 1):
                        pair(p, False)
                    pair(PAIRS - 1, True)
                    leave(dve, dense_total, (h_used, weighted, y_used, combT_ready))

                def dense_program():
                    dve.wait_ge(*comb_turned.at(1))
                    nc.vector.tensor_copy(combT[:, 0:256], bank[1][0:16, 0:256]).then_inc(*combT_ready.one())
                    nc.vector.tensor_copy(combT[:, 256:T], bank[1][0:16, 376:384]).then_inc(*combT_ready.one())
                    dve.wait_ge(*comb_spread.at(2))
                    for _ in range(2):
                        dve.sem_inc(*h_used.one())
                        dve.sem_inc(*weighted.one())
                    for _ in range(4):
                        dve.sem_inc(*y_used.one())
                    with dve.Fori(0, NE) as e, weighted.each(e, 4, NE), h_used.each(e, 4, NE), y_used.each(e, 8, NE):
                        cb = combb[:, bass.ds(e, 1)].rearrange("p e t -> p (e t)")
                        for f in range(4):
                            dve.wait_ge(silu_done.sem, e * 4 + (silu_done.start + f + 1))
                            nc.vector.tensor_tensor(hs[:, f], sl[:, f % 2], cb, ALU.mult).then_inc(*weighted.one())
                            dve.wait_ge(*weighted.now())
                            nc.vector.tensor_tensor(hs[:, f], hs[:, f], bank[2 + f % 2][:, 0:T], ALU.mult).then_inc(*h_used.one())
                        for c in range(8):
                            dve.wait_ge(y_filled.sem, e * 8 + (y_filled.start + c + 1))
                            if c % 4 == 3:
                                dve.sem_inc(W.free[slot[4 + c // 4]].sem, 1)
                            nc.vector.tensor_tensor(xT[:, c], xT[:, c], bank[4 + c % 4][:, 0:T], ALU.add).then_inc(*y_used.one())
                    leave(dve, gathered_total, (hg_ready, xg_ready, x_added, w_row_ready))
                is_crowded = dve.value_load(crowded[0:1, 0:1], min_val=0, max_val=1)
                with dve.If(is_crowded < 1):
                    gathered_program()
                with dve.If(is_crowded > 0):
                    dense_program()

        for c, total in (*dense_total.items(), *gathered_total.items()):
            assert c.n == c.start + total, (c.sem, c.n, c.start, total)
        W.used += 6 * NE


def nsa_layer(env):
    (nc, core, I, O, W, cst, par, xT, uT, eps, scratch, linker, ident, ones) = (
        env[k] for k in ("nc", "core", "I", "O", "W", "cst", "par", "xT", "uT", "eps", "scratch", "linker", "ident", "ones"))
    count, bank = core.count, core.bank
    pe_done, act_done, dve_done, pool_done = (count(n) for n in ("pe_done", "act_done", "dve_done", "pool_done"))
    misc, out_sent, in_loaded, pool_sent = count("misc_dma", 16), count("out_sent", 16), count("in_loaded", 16), count("pool_sent", 16)
    ones64 = cst("ones64")
    V = nc.vector
    with ExitStack() as layer:
        def sb(name, shape, dt=F32, ctx=layer):
            return core.sb("n_" + name, shape, dt, ctx)

        qT = sb("qT", [128, 8, T])
        kvT = sb("kvT", [128, 12, T])
        glT = sb("glT", [48, T])
        cw2 = sb("cw2", [64, 2, 64])
        rel = sb("rel", [32, 8, 16])
        onehots = sb("onehots", [32, NSTRIP + PAST + 1])
        pages = sb("pages", [1, 64], I32)
        pebias = sb("pebias", [64, 2])
        cw1 = sb("cw1", [128, 2, 8, 2, 64])
        d_strip, d_gl = scratch("scr_strip", [16, NSTRIP]), scratch("scr_gl", [48, NB])
        with core.block() as block:
            @block.gpsimd
            def _(pool):
                for dst, src in ((cw2[:], I["cmp_w2"]), (cw1[:], I["cmp_w1"]), (onehots[:], I["onehots"]), (pages[:], I["pages"]),
                                 (rel[:], I["rel"].rearrange("r (o h) -> r o h", o=1).to_broadcast([32, 8, 16]))):
                    pool.dma_start(dst, src).then_inc(*misc.one())
                pool.wait_ge(*misc.now())

        def act_step(act, t, ps):
            if t < 8:
                return nc.scalar.copy(qT[:, t], ps[:, 0:T])
            if t < 20:
                return nc.scalar.copy(kvT[:, t - 8], ps[:, 0:T])
            return nc.scalar.activation(glT[:], ps[0:48, 0:T], ACT.Sigmoid)

        env["project"](uT, KT, 2560, act_step, lambda eng, t, ps: None, extra=(env["w_gl"], 48))
        jobs = [(qT[:, c], qT[:, c], par("q_g"), 1.0, eps[:, 1:2]) for c in range(8)]
        jobs += [(kvT[:, c], kvT[:, c], par("k_g", b), 1 / 64, eps[:, 0:1]) for c, b in ((4, 1), (5, 1), (8, 2), (9, 2))]
        env["norm_each"](jobs, ones64, "nq")

        with ExitStack() as st:
            kcs = sb("kcs", [128, 2, 512], ctx=st)
            vcs = sb("vcs", [128, 4, 256], ctx=st)
            vnew = sb("vnew", [8, 2, 2, 128], ctx=st)
            dbias = sb("dbias", [128, PAST + 1], ctx=st)
            gdec = sb("gdec", [128, 3], ctx=st)
            page = sb("page", [128, 2, NPAGE, 512], ctx=st)
            page_in = [count(f"page_in{b}", 16) for b in range(4)]

            def load_pages(eng, cache, b, dst, loaded, cols, waits):
                _, numbers = nc.values_load_multi_w_load_instructions(pages[0:1, NPAGE * b:NPAGE * b + NPAGE], engines=[eng.engine],
                                                                      min_val=0, max_val=cache.shape[0] - 1)
                for w in waits:
                    eng.wait_ge(*w)
                for k, v in enumerate(numbers):
                    eng.dma_start(dst[:, k:k + 1], cache[bass.ds(v, 1), :, cols].rearrange("n p c -> p n c")).then_inc(*loaded.one())

            def part(u):
                return page[:, u // 2 % 2, :, 256 * (u % 2):256 * (u % 2) + 256]

            def stream(eng, turns, half, before):
                cols = slice(256 * half, 256 * half + 256)
                for u in turns:
                    b = u % NB
                    free = [before(u - 4)] if u >= 4 else []
                    if u < NB:
                        load_pages(eng, I["cache_sel"], b, part(u), page_in[u % 4], cols, free)
                    else:
                        eng.wait_ge(*free[0])
                        eng.dma_start(part(u)[:, 0:4], I["cache_win"][b, :, :, cols]).then_inc(*page_in[u % 4].one())

            early, sp_turns, act_turns = (0, 2), (4, 6, 7, 9, 11, 13, 15), (1, 3, 5, 8, 10, 12, 14)

            def streamed(u):
                c = page_in[u % 4]
                loads = NPAGE * min(u // 4 + 1, 2) + max(u // 4 - 1, 0)
                return c.sem, c.start + 16 * (loads - (NPAGE if u % 4 in early else 0))

            with ExitStack() as st2:
                hid = sb("hid", [64, 2, 4, NB, 64], ctx=st2)
                half0 = sb("half0", [64, 2, 4, 64], ctx=st2)
                hidden = count("hidden_done")
                third_buffer = ExitStack()
                third = sb("third", [128, NPAGE, 512], ctx=third_buffer)

                def whole(b):
                    return third[:] if b % 3 == 2 else page[:, b % 3]

                def before(b):
                    return pe_done.at(2 + 2 * b)

                with core.block() as block:
                    @block.sync
                    def _(sp):
                        sp.dma_start(O["kvT"], kvT[:]).then_inc(*out_sent.one())
                        for b in range(NB):
                            load_pages(sp, I["cache_cmp"], b, whole(b), page_in[b % 3], slice(0, 512), [before(b - 2)] if b >= 3 else [])

                    @block.tensor
                    def _(pe):
                        for kv in range(2):
                            for h in range(2):
                                for r in range(8):
                                    mm = nc.tensor.matmul(bank[4][0:64, kv:kv + 1], cw1[:, kv, r, h], par("pe", 16 * kv + 8 * h + r),
                                                          start=(h + r == 0), stop=(h == 1 and r == 7))
                        mm.then_inc(*pe_done.one())
                        for br in range(2):
                            for p in range(2):
                                k = 2 * br + p
                                mm = nc.tensor.transpose(bank[5][0:8, 128 * k:128 * k + 128], kvT[:, 6 + 4 * br + p, LP:T], ident)
                        for k in range(2):
                            nc.tensor.matmul(bank[6 + k][:], rel[:].rearrange("r b h -> r (b h)"), onehots[:, NSTRIP + 512 * k:NSTRIP + 512 * k + 512],
                                             start=True, stop=True)
                        mm = nc.tensor.matmul(bank[4][:, 8:9], rel[:].rearrange("r b h -> r (b h)"), onehots[:, NSTRIP + PAST:NSTRIP + PAST + 1],
                                              start=True, stop=True)
                        mm.then_inc(*pe_done.one())
                        for b in range(NB):
                            pe.wait_ge(page_in[b % 3].sem, page_in[b % 3].start + 16 * NPAGE * (b // 3 + 1))
                            for kv in range(2):
                                if b >= 2:
                                    pe.wait_ge(*hidden.at(2 * (b - 2) + kv + 1))
                                x = whole(b).rearrange("p n (v r g c) -> p v r g n c", v=2, r=8, g=4)[:, kv]
                                for r in range(8):
                                    mm = nc.tensor.matmul(bank[2 * (b % 2) + kv][:, 0:256], cw1[:, kv, r].rearrange("p h e -> p (h e)"), x[:, r],
                                                          start=(r == 0), stop=(r == 7))
                                mm.then_inc(*pe_done.one())

                    @block.scalar
                    def _(act):
                        act.wait_ge(*dve_done.at(1))
                        for b in range(NB):
                            for kv in range(2):
                                k = 2 * b + kv
                                act.wait_ge(*pe_done.at(3 + k))
                                if k >= 2:
                                    act.wait_ge(*hidden.at(k - 1))
                                nc.scalar.copy(half0[:, kv], bank[2 * (b % 2) + kv][0:64, 0:256].rearrange("p (g c) -> p g c", g=4)).then_inc(*act_done.one())
                                act.wait_ge(*hidden.at(k + 1))
                                h = hid[:, kv, :, b, 0:NCMP]
                                nc.scalar.activation(h, h, ACT.Silu, bias=pebias[:, kv:kv + 1]).then_inc(*act_done.one())

                    @block.vector
                    def _(dve):
                        dve.wait_ge(*pe_done.at(2))
                        V.tensor_copy(pebias[:], bank[4][0:64, 0:2]).then_inc(*dve_done.one())
                        V.memset(hid[:, :, :, :, NCMP:64], 0.0).then_inc(*dve_done.one())
                        V.tensor_copy(vnew[:], bank[5][0:8].rearrange("p (a b c) -> p a b c", a=2, b=2)).then_inc(*dve_done.one())
                        for k in range(2):
                            V.tensor_copy(dbias[:, 512 * k:512 * k + 512], bank[6 + k][:]).then_inc(*dve_done.one())
                        V.tensor_copy(dbias[:, PAST:PAST + 1], bank[4][:, 8:9]).then_inc(*dve_done.one())
                        for b in range(NB):
                            for kv in range(2):
                                k = 2 * b + kv
                                dve.wait_ge(*act_done.at(2 * k + 1))
                                V.tensor_tensor(hid[:, kv, :, b, 0:NCMP], half0[:, kv, :, 0:NCMP],
                                                bank[2 * (b % 2) + kv][64:128, 0:256].rearrange("p (g c) -> p g c", g=4)[:, :, 1:64],
                                                ALU.add).then_inc(*hidden.one())

                    @block.gpsimd
                    def _(pool):
                        pool.dma_start(d_gl, glT[:, LP:T]).then_inc(*pool_sent.one())
                        pool.wait_ge(*pool_sent.now())
                        for b in range(NB):
                            src = bass.AP(d_gl.tensor, b, [[NB, 16], [16 * NB, 3]])
                            pool.dma_start(gdec[16 * b:16 * b + 16, :], src, allow_slow_non_contiguous=True).then_inc(*misc.one())
                        pool.wait_ge(*misc.now())

                third_buffer.close()
                with ExitStack() as st3:
                    kc = sb("kc", [64, 4, 512], ctx=st3)
                    sq = sb("sq", [64, 4, 512], ctx=st3)
                    rs = sb("rs", [64, 4, 512], ctx=st3)
                    with core.block() as block:
                        @block.sync
                        def _(sp):
                            stream(sp, early, 0, None)

                        @block.tensor
                        def _(pe):
                            for g in range(4):
                                nc.tensor.matmul(bank[g][0:64, :], cw2[:, 0], hid[:, 0, g].rearrange("p b c -> p (b c)"), start=True,
                                                 stop=True).then_inc(*pe_done.one())
                            for q in range(4):
                                for g in range(4):
                                    mm = nc.tensor.matmul(bank[4 + q][:, 64 * g:64 * g + 64], hid[:, 1, g, 2 * q:2 * q + 2].rearrange("p b c -> p (b c)"),
                                                          cw2[:, 1], start=True, stop=True)
                                mm.then_inc(*pe_done.one())
                            for g in range(4):
                                pe.wait_ge(*act_done.at(2 * g + 2))
                                nc.tensor.matmul(bank[g][0:64, :], ones64[0:64, 0:64], sq[:, g], start=True, stop=True).then_inc(*pe_done.one())

                        @block.scalar
                        def _(act):
                            for g in range(4):
                                act.wait_ge(*pe_done.at(g + 1))
                                nc.scalar.copy(kc[:, g], bank[g][0:64, :]).then_inc(*act_done.one())
                                nc.scalar.activation(sq[:, g], bank[g][0:64, :], ACT.Square).then_inc(*act_done.one())
                            for g in range(4):
                                act.wait_ge(*pe_done.at(9 + g))
                                nc.scalar.activation(rs[:, g], bank[g][0:64, :], ACT.Sqrt, bias=eps[0:64, 0:1], scale=1 / 64).then_inc(*act_done.one())

                        @block.vector
                        def _(dve):
                            for q in range(4):
                                dve.wait_ge(*pe_done.at(5 + q))
                                V.tensor_copy(vcs[:, q], bank[4 + q][:, 0:256]).then_inc(*dve_done.one())
                            for g in range(4):
                                dve.wait_ge(*act_done.at(9 + g))
                                V.reciprocal(rs[:, g], rs[:, g]).then_inc(*dve_done.one())
                                dve.wait_ge(*dve_done.now())
                                V.scalar_tensor_tensor(out=kcs[64 * (g % 2):64 * (g % 2) + 64, g // 2], in0=kc[:, g], scalar=par("k_g", 0)[0:64],
                                                       in1=rs[:, g], op0=ALU.mult, op1=ALU.mult).then_inc(*dve_done.one())

            qblk = sb("qblk", [128, 2, NB, 128], ctx=st)
            pc = sb("pc", [128, 2, 64], ctx=st)
            pcg = sb("pcg", [128, 2, 64], ctx=st)
            pcT = sb("pcT", [128, 2, 128], ctx=st)
            imp = sb("imp", [128, 6, NSEL], ctx=st)
            st_ = sb("stat", [128, 16], ctx=st)
            ss = sb("ss", [128, PAST + 1], ctx=st)
            sw = sb("sw", [128, 513], ctx=st)
            pT = sb("pT", [128, 12, 128], ctx=st)
            dg = sb("dg", [128, 2, 128], ctx=st)
            pn = sb("pn", [8, 2, 128], ctx=st)

            mark = {}
            with core.block() as block:
                @block.sync
                def _(sp):
                    stream(sp, sp_turns, 0, lambda u: pe_done.at(u + 1))

                @block.scalar
                def _(act):
                    stream(act, act_turns, 0, lambda u: pe_done.at(u + 1))

                @block.vector
                def _(dve):
                    link = linker(dve, dve_done)
                    link(V.memset(qblk[:], 0.0))
                    flat = qblk[:].rearrange("p a b c -> p a (b c)")
                    for p in range(2):
                        for h in range(4):
                            for g2 in range(2):
                                o = 8 * p + 2 * h + g2
                                ins = V.tensor_copy(flat[64 * g2:64 * g2 + 64, p, o:o + 144 * 7 + 1:144], qT[64 * g2:64 * g2 + 64, 4 * p + h, LP:T])
                                ins.then_inc(*dve_done.one())
                    mark["qblk"] = dve_done.now()

                @block.tensor
                def _(pe):
                    pe.wait_ge(*mark["qblk"])
                    for u in range(2 * NB):
                        b = u % NB
                        pe.wait_ge(*streamed(u))
                        for p in range(2):
                            st0, sp0 = (b == 0 and p == 0), (b == NB - 1 and p == 1)
                            k = part(u)[:, :, 128 * p:128 * p + 128]
                            kw = dict(start=st0, stop=sp0, skip_group_check=True)
                            if u < NB:
                                for i in range(2):
                                    nc.tensor.matmul(bank[i][:], qblk[:, p, b], k[:, 4 * i:4 * i + 4], **kw)
                                mm = nc.tensor.matmul(bank[3][:, 0:1], qblk[:, p, b], kvT[:, 4 + p, LP + b:LP + b + 1], **kw)
                            else:
                                nc.tensor.matmul(bank[2][:], qblk[:, p, b], k[:, 0:4], **kw)
                                mm = nc.tensor.matmul(bank[4][:, 0:1], qblk[:, p, b], kvT[:, 8 + p, LP + b:LP + b + 1], **kw)
                        mm.then_inc(*pe_done.one())
                    for b in range(NB):
                        for p in range(2):
                            mm = nc.tensor.matmul(bank[5][:, 0:64], qblk[:, p, b], kcs[:, p, 64 * b:64 * b + 64], start=(b + p == 0),
                                                  stop=(b == NB - 1 and p == 1), skip_group_check=True)
                    mm.then_inc(*pe_done.one())

            with core.block() as block:
                @block.sync
                def _(sp):
                    stream(sp, early, 1, None)

                @block.vector
                def _(dve):
                    link = linker(dve, dve_done)
                    c63 = pc[:, 0, 0:NCMP]
                    link(V.memset(pc[:], 0.0))
                    link(V.tensor_tensor(c63, bank[5][:, 0:NCMP], dbias[:, 31:31 + 16 * 62 + 1:16], ALU.add))
                    link(V.tensor_reduce(st_[:, 0:1], c63, AX.X, ALU.max))
                    link(V.tensor_scalar(st_[:, 0:1], st_[:, 0:1], -1.0, None, ALU.mult))
                    mark["cmp max"] = dve_done.now()
                    for k in range(2):
                        V.tensor_tensor(ss[:, 512 * k:512 * k + 512], bank[k][:], dbias[:, 512 * k:512 * k + 512], ALU.add).then_inc(*dve_done.one())
                    V.tensor_tensor(ss[:, PAST:PAST + 1], bank[3][:, 0:1], dbias[:, PAST:PAST + 1], ALU.add).then_inc(*dve_done.one())
                    V.tensor_tensor(sw[:, 0:512], bank[2][:], dbias[:, 512:PAST], ALU.add).then_inc(*dve_done.one())
                    link(V.tensor_tensor(sw[:, 512:513], bank[4][:, 0:1], dbias[:, PAST:PAST + 1], ALU.add))
                    link(V.tensor_reduce(st_[:, 2:3], sw[:], AX.X, ALU.max))
                    link(V.tensor_scalar(st_[:, 2:3], st_[:, 2:3], -1.0, None, ALU.mult))
                    mark["win max"] = dve_done.now()
                    dve.wait_ge(*act_done.at(1))
                    link(V.reciprocal(st_[:, 4:5], st_[:, 3:4]))
                    link(V.tensor_scalar(c63, c63, st_[:, 4:5], None, ALU.mult))
                    link(V.tensor_copy(pc[:, 1], pc[:, 0]))
                    link(V.tensor_scalar(pcg[:], pc[:], gdec[:, 0:1], None, ALU.mult))
                    mark["pc"] = dve_done.now()
                    dve.wait_ge(*pe_done.at(1))
                    link(V.tensor_copy(pcT[:, 0], bank[5][:, 0:128]))
                    link(V.memset(pcT[:, 1], 0.0))
                    for k in range(2):
                        o = pcT[64 * k:64 * k + 64, 1].rearrange("p (b s h) -> p s b h", s=2, h=16)[:, k]
                        link(V.tensor_copy(o, bank[5][64 * k:64 * k + 64, 128:256].rearrange("p (b s h) -> p s b h", s=2, h=16)[:, k]))
                    mark["pcT"] = dve_done.now()
                    dve.wait_ge(*pe_done.at(2))
                    link(V.tensor_copy(imp[:, 0], bank[6][:, 0:NSEL]))
                    mark["imp of heads"] = dve_done.now()
                    dve.wait_ge(*pe_done.at(3))
                    link(V.tensor_tensor(imp[:, 1], bank[6][:, 32:32 + NSEL], cst("forced"), ALU.add))
                    link(V.tensor_reduce(st_[:, 5:6], imp[:, 1], AX.X, ALU.min))
                    link(V.tensor_scalar(imp[:, 2], imp[:, 1], st_[:, 5:6], None, ALU.is_equal))
                    link(V.tensor_tensor(imp[:, 2], imp[:, 2], cst("block_no"), ALU.mult))
                    link(V.tensor_reduce(st_[:, 6:7], imp[:, 2], AX.X, ALU.max))
                    link(V.tensor_scalar(imp[:, 3], cst("block_no"), st_[:, 6:7], NEG, ALU.is_equal, ALU.mult))
                    blocks = ss[:, 0:PAST].rearrange("p (j r) -> p j r", r=64)
                    link(V.tensor_tensor(blocks, blocks, imp[:, 3, 0:16].rearrange("p (j o) -> p j o", o=1).to_broadcast([128, 16, 64]), ALU.add))
                    link(V.tensor_reduce(st_[:, 1:2], ss[:], AX.X, ALU.max))
                    link(V.tensor_scalar(st_[:, 1:2], st_[:, 1:2], -1.0, None, ALU.mult))
                    mark["sel max"] = dve_done.now()
                    dve.wait_ge(*act_done.at(2))
                    link(V.reciprocal(st_[:, 8:9], st_[:, 7:8]))
                    link(V.tensor_scalar(sw[:], sw[:], st_[:, 8:9], gdec[:, 2:3], ALU.mult, ALU.mult))
                    link(V.tensor_scalar(dg[:, 1], ident, sw[:, 512:513], None, ALU.mult))
                    mark["win weights"] = dve_done.now()
                    dve.wait_ge(*act_done.at(3))
                    link(V.reciprocal(st_[:, 10:11], st_[:, 9:10]))
                    link(V.tensor_scalar(ss[:], ss[:], st_[:, 10:11], gdec[:, 1:2], ALU.mult, ALU.mult))
                    link(V.tensor_scalar(dg[:, 0], ident, ss[:, PAST:PAST + 1], None, ALU.mult))
                    mark["sel weights"] = dve_done.now()
                    for k, b in ((2, 2), (0, 0), (1, 1)):
                        dve.wait_ge(*pe_done.at(4 if k == 2 else 5))
                        link(V.tensor_copy(pT[:, 4 * k:4 * k + 4].rearrange("p a b -> p (a b)"), bank[b][:]))
                    link(V.tensor_copy(pn[:].rearrange("p a b -> p (a b)"), bank[3][0:8, 0:256]))

                @block.scalar
                def _(act):
                    act.wait_ge(*mark["cmp max"])
                    nc.scalar.activation(pc[:, 0, 0:NCMP], pc[:, 0, 0:NCMP], ACT.Exp, bias=st_[:, 0:1], accum_out=st_[:, 3:4]).then_inc(*act_done.one())
                    act.wait_ge(*mark["win max"])
                    nc.scalar.activation(sw[:], sw[:], ACT.Exp, bias=st_[:, 2:3], accum_out=st_[:, 7:8]).then_inc(*act_done.one())
                    act.wait_ge(*mark["sel max"])
                    nc.scalar.activation(ss[:], ss[:], ACT.Exp, bias=st_[:, 1:2], accum_out=st_[:, 9:10]).then_inc(*act_done.one())

                @block.tensor
                def _(pe):
                    pe.wait_ge(*mark["pc"])
                    nc.tensor.transpose(bank[5][:, 0:128], pc[:].rearrange("p a b -> p (a b)"), ident)
                    nc.tensor.transpose(bank[5][:, 128:256], pcg[:].rearrange("p a b -> p (a b)"), ident).then_inc(*pe_done.one())
                    pe.wait_ge(*mark["pcT"])
                    nc.tensor.matmul(bank[6][:, 0:NSEL], pcT[0:64, 0], cst("overlap")[0:64], start=True, stop=True).then_inc(*pe_done.one())
                    pe.wait_ge(*mark["imp of heads"])
                    nc.tensor.matmul(bank[6][:, 32:32 + NSEL], cst("same_group"), imp[:, 0], start=True, stop=True).then_inc(*pe_done.one())
                    pe.wait_ge(*mark["win weights"])
                    for k in range(4):
                        mm = nc.tensor.transpose(bank[2][:, 128 * k:128 * k + 128], sw[:, 128 * k:128 * k + 128], ident)
                    mm.then_inc(*pe_done.one())
                    pe.wait_ge(*mark["sel weights"])
                    for k in range(8):
                        nc.tensor.transpose(bank[k // 4][:, 128 * (k % 4):128 * (k % 4) + 128], ss[:, 128 * k:128 * k + 128], ident)
                    for k in range(2):
                        mm = nc.tensor.matmul(bank[3][0:8, 128 * k:128 * k + 128], cst("of_seq"), dg[:, k], start=True, stop=True)
                    mm.then_inc(*pe_done.one())

            orow = sb("orow", [16, NB, 256], ctx=st)
            rows_copied = count("rows_copied")

            def rows_of(b):
                return bank[b // 2][0:16, 256 * (b % 2):256 * (b % 2) + 256]

            def turn_rows(pe, i):
                pe.wait_ge(*rows_copied.at(i + 1))
                for b in (2 * i, 2 * i + 1):
                    for p in range(2):
                        mm = nc.tensor.matmul(bank[6 + p][:, 16 * b:16 * b + 16], orow[:, b, 128 * p:128 * p + 128], ident[0:16, 0:16],
                                              start=False, stop=(b == NB - 1), skip_group_check=True)
                if i == NB // 2 - 1:
                    mm.then_inc(*pe_done.one())

            with core.block() as block:
                @block.sync
                def _(sp):
                    stream(sp, sp_turns, 1, lambda u: pe_done.at(u + 1))

                @block.scalar
                def _(act):
                    stream(act, act_turns, 1, lambda u: pe_done.at(u + 1))

                @block.tensor
                def _(pe):
                    kw = dict(stop=False, skip_group_check=True)
                    for p in range(2):
                        for br in range(2):
                            nc.tensor.matmul(bank[6 + p][:, 0:128], vnew[:, br, p], pn[:, br], start=(br == 0), **kw)
                        for q in range(4):
                            nc.tensor.matmul(bank[6 + p][:, 32 * q:32 * q + 32], vcs[:, q, 128 * p:128 * p + 128], pcT[:, 1, 32 * q:32 * q + 32],
                                             start=False, **kw)
                    for u in range(2 * NB):
                        b = u % NB
                        pe.wait_ge(*streamed(u))
                        n, k0 = (8, 0) if u < NB else (4, 8)
                        for k in range(n):
                            mm = nc.tensor.matmul(rows_of(b), pT[:, k0 + k, 16 * b:16 * b + 16], part(u)[:, k], start=(u < NB and b % 2 == 0 and k == 0),
                                                  stop=(u >= NB and k == n - 1), skip_group_check=True)
                        mm.then_inc(*pe_done.one())
                        if u >= NB + 3 and b % 2:
                            turn_rows(pe, b // 2 - 1)
                    turn_rows(pe, NB // 2 - 1)

                @block.vector
                def _(dve):
                    for i in range(NB // 2):
                        dve.wait_ge(*pe_done.at(NB + 2 * i + 2))
                        V.tensor_copy(orow[:, 2 * i:2 * i + 2], bank[i][0:16].rearrange("p (b c) -> p b c", b=2)).then_inc(*rows_copied.one())
                    dve.wait_ge(*pe_done.at(2 * NB + 1))
                    for p in range(2):
                        for g2 in range(2):
                            src = bank[6 + p][64 * g2:64 * g2 + 64, 0:128].rearrange("p (b a h g) -> p a g h b", a=2, h=4, g=2)[:, p, g2]
                            V.tensor_copy(uT[64 * g2:64 * g2 + 64, 4 * p:4 * p + 4, LP:T], src).then_inc(*dve_done.one())

        with ExitStack() as st:
            bias = sb("bias", [128, 2, 16, LP], ctx=st)
            qR = sb("qR", [128, 2, 8, 128], ctx=st)
            gR = sb("gR", [48, 2, 128], ctx=st)
            strip = sb("strip", [16, NSTRIP], ctx=st)
            vn = sb("vn", [128, 2, 2, 256], ctx=st)
            gate = sb("gate", [128, 2, 48], ctx=st)
            oacc = sb("oacc", [128, 2, D], ctx=st)
            hidp = sb("hidp", [64, 2, 4, 16], ctx=st)
            kcp = sb("kcp", [128, 2, 16], ctx=st)
            kk = sb("kk", [64, 3, 64], ctx=st)
            vblk = sb("vblk", [128, 4, 4, 64], ctx=st)
            with ExitStack() as st2:
                w1d = sb("w1d", [128, 2, 32, 64], ctx=st2)
                with core.block() as block:
                    @block.gpsimd
                    def _(pool):
                        pool.dma_start(w1d[:], I["cmp_w1d"]).then_inc(*misc.one())
                        pool.wait_ge(*misc.now())
                        pool.wait_ge(*dve_done.at(6))
                        pool.dma_start(d_strip, strip[:]).then_inc(*pool_sent.one())
                        pool.wait_ge(*pool_sent.now())
                        for t in range(2):
                            src = bass.AP(d_strip.tensor, 128 - 128 * t, [[1, 128], [NSTRIP, 16], [1, LP]])
                            pool.dma_start(bias[:, t], src).then_inc(*misc.one())
                        pool.wait_ge(*misc.now())

                    @block.tensor
                    def _(pe):
                        nc.tensor.matmul(bank[0][0:16, :], rel[:, 0], onehots[:, 0:NSTRIP], start=True, stop=True).then_inc(*pe_done.one())
                        for br in range(2):
                            for t in range(2):
                                for p in range(2):
                                    k = 2 * t + p
                                    mm = nc.tensor.transpose(bank[1 + br][:, 128 * k:128 * k + 128], kvT[:, 6 + 4 * br + p, 128 * t:128 * t + 128], ident)
                        pe.wait_ge(*dve_done.at(4))
                        for t in range(2):
                            mm = nc.tensor.transpose(bank[3][:, 48 * t:48 * t + 48], gR[:, t], ident[0:48, 0:48])
                        mm.then_inc(*pe_done.one())
                        pe.wait_ge(*misc.at(1))
                        for kv in range(2):
                            for g2 in range(2):
                                rows = slice(64 * g2, 64 * g2 + 64)
                                for r in range(32):
                                    mm = nc.tensor.matmul(bank[4 + 2 * kv + g2][0:64, 0:30], w1d[rows, kv, r],
                                                          kvT[rows, 2 * kv:2 * kv + 2, r:r + 16 * 14 + 1:16], start=(r == 0), stop=(r == 31))
                                mm.then_inc(*pe_done.one())
                        pe.wait_ge(*act_done.at(4))
                        nc.tensor.matmul(bank[0][0:64, 0:64], cw2[:, 0], hidp[:, 0].rearrange("p g c -> p (g c)"), start=True, stop=True) \
                            .then_inc(*pe_done.one())
                        for g in range(4):
                            mm = nc.tensor.matmul(bank[1][0:16, 64 * g:64 * g + 64], hidp[:, 1, g], cw2[:, 1], start=True, stop=True)
                        mm.then_inc(*pe_done.one())
                        pe.wait_ge(*act_done.at(6))
                        nc.tensor.matmul(bank[2][0:64, 0:64], ones64[0:64, 0:64], kk[:, 1], start=True, stop=True).then_inc(*pe_done.one())

                    @block.scalar
                    def _(act):
                        for kv in range(2):
                            for g2 in range(2):
                                act.wait_ge(*pe_done.at(3 + 2 * kv + g2))
                                act.wait_ge(*dve_done.at(10))
                                nc.scalar.activation(hidp[:, kv, g2:4:2, 0:NCMPP], bank[4 + 2 * kv + g2][0:64, 0:30].rearrange("p (a c) -> p a c", a=2),
                                                     ACT.Silu, bias=pebias[:, kv:kv + 1]).then_inc(*act_done.one())
                        act.wait_ge(*pe_done.at(7))
                        nc.scalar.copy(kk[:, 0], bank[0][0:64, 0:64]).then_inc(*act_done.one())
                        nc.scalar.activation(kk[:, 1], bank[0][0:64, 0:64], ACT.Square).then_inc(*act_done.one())
                        act.wait_ge(*pe_done.at(9))
                        nc.scalar.activation(kk[:, 2], bank[2][0:64, 0:64], ACT.Sqrt, bias=eps[0:64, 0:1], scale=1 / 64).then_inc(*act_done.one())

                    @block.vector
                    def _(dve):
                        link = linker(dve, dve_done)
                        for t in range(2):
                            back = slice(127, None, -1) if t == 0 else slice(255, 127, -1)
                            V.tensor_copy(qR[:, t], qT[:, :, back]).then_inc(*dve_done.one())
                            V.tensor_copy(gR[:, t], glT[:, back]).then_inc(*dve_done.one())
                        dve.wait_ge(*pe_done.at(1))
                        link(V.tensor_copy(strip[:, 0:LP], bank[0][0:16, 0:LP]))
                        link(V.memset(strip[:, LP:NSTRIP], NEG))
                        dve.wait_ge(*pe_done.at(2))
                        for br in range(2):
                            V.tensor_copy(vn[:, br].rearrange("p t c -> p (t c)"), bank[1 + br][:]).then_inc(*dve_done.one())
                        V.tensor_copy(gate[:].rearrange("p t c -> p (t c)"), bank[3][:, 0:96]).then_inc(*dve_done.one())
                        link(V.memset(hidp[:], 0.0))
                        link(V.memset(vblk[:], 0.0))
                        dve.wait_ge(*pe_done.at(8))
                        for g in range(4):
                            for h in range(4):
                                V.tensor_copy(vblk[32 * h:32 * h + 16, g, h], bank[1][0:16, 64 * g:64 * g + 64]).then_inc(*dve_done.one())
                        dve.wait_ge(*act_done.at(7))
                        link(V.reciprocal(kk[:, 2], kk[:, 2]))
                        for g in range(4):
                            V.scalar_tensor_tensor(out=kcp[64 * (g % 2):64 * (g % 2) + 64, g // 2], in0=kk[:, 0, 16 * g:16 * g + 16],
                                                   scalar=par("k_g", 0)[0:64], in1=kk[:, 2, 16 * g:16 * g + 16], op0=ALU.mult,
                                                   op1=ALU.mult).then_inc(*dve_done.one())

            with ExitStack() as st2:
                sc = sb("sc", [128, 2, 16, 16], ctx=st2)
                p32 = sb("p32", [128, 2, 4, 4, 32], ctx=st2)
                p32T = sb("p32T", [128, 2, 4, 128], ctx=st2)
                s1 = sb("s1", [128, 2, 16, 2], ctx=st2)
                mark = {}
                with core.block() as block:
                    @block.vector
                    def _(dve):
                        link = linker(dve, dve_done)
                        link(V.memset(sc[:], NEG))
                        link(V.memset(p32[:], 0.0))
                        dve.wait_ge(*pe_done.at(1))
                        for t in range(2):
                            for g2 in range(2):
                                link(V.tensor_tensor(sc[:, t, g2:16:2, 0:NCMPP], bank[7 * g2][:, 128 * t:128 * t + 128].rearrange("p (h c) -> p h c", h=8)[:, :, 0:NCMPP],
                                                     bias[:, t, g2:16:2, 31:LP:16], ALU.add))
                        link(V.tensor_reduce(s1[:, :, :, 0], sc[:], AX.X, ALU.max))
                        for t in range(2):
                            link(V.tensor_tensor(sc[:, t], sc[:, t], s1[:, t, :, 0:1].to_broadcast([128, 16, 16]), ALU.subtract))
                        mark["shifted"] = dve_done.now()
                        dve.wait_ge(*act_done.at(1))
                        for t in range(2):
                            link(V.tensor_tensor(sc[:, t], sc[:, t], cst("cmp_valid")[:, 16 * t:16 * t + 16].rearrange("p (o c) -> p o c", o=1)
                                                 .to_broadcast([128, 16, 16]), ALU.mult))
                        link(V.tensor_reduce(s1[:, :, :, 0], sc[:], AX.X, ALU.add))
                        link(V.tensor_scalar(s1[:, :, :, 0], s1[:, :, :, 0], 1e-30, None, ALU.max))
                        link(V.reciprocal(s1[:, :, :, 1], s1[:, :, :, 0]))
                        for t in range(2):
                            link(V.tensor_tensor(s1[:, t, :, 1], s1[:, t, :, 1], gate[:, t, 0:16], ALU.mult))
                            for g in range(4):
                                hd = slice(8 * (g // 2) + g % 2, 8 * (g // 2) + g % 2 + 7, 2)
                                link(V.tensor_tensor(p32[:, t, g, :, 0:16], sc[:, t, hd], s1[:, t, hd, 1:2].to_broadcast([128, 4, 16]), ALU.mult))
                        mark["weights"] = dve_done.now()
                        for t in range(2):
                            dve.wait_ge(*pe_done.at(2 + t))
                            link(V.tensor_copy(p32T[:, t].rearrange("p g q -> p (g q)"), bank[1 + t][:]))
                        mark["turned"] = dve_done.now()
                        for t in range(2):
                            for g in range(4):
                                dve.wait_ge(*pe_done.at(4 + 2 * t + g // 2))
                                V.tensor_copy(oacc[:, t].rearrange("p (a h b d) -> p a b h d", a=2, h=4, b=2)[:, g // 2, g % 2],
                                              bank[3 + 2 * t + g // 2][:, 256 * (g % 2):256 * (g % 2) + 256].rearrange("p (h d) -> p h d", h=4)) \
                                    .then_inc(*dve_done.one())

                    @block.scalar
                    def _(act):
                        act.wait_ge(*mark["shifted"])
                        nc.scalar.activation(sc[:], sc[:], ACT.Exp).then_inc(*act_done.one())

                    @block.tensor
                    def _(pe):
                        for t in range(2):
                            for hd in range(16):
                                p, h, g2 = hd // 8, hd % 8 // 2, hd % 2
                                rows = slice(64 * g2, 64 * g2 + 64)
                                o = 128 * t + 16 * (hd // 2)
                                mm = nc.tensor.matmul(bank[7 * g2][:, o:o + 16], qR[rows, t, 4 * p + h], kcp[rows, p], start=True, stop=True)
                        mm.then_inc(*pe_done.one())
                        pe.wait_ge(*mark["weights"])
                        for t in range(2):
                            for g in range(4):
                                mm = nc.tensor.transpose(bank[1 + t][:, 128 * g:128 * g + 128], p32[:, t, g].rearrange("p h c -> p (h c)"), ident)
                            mm.then_inc(*pe_done.one())
                        pe.wait_ge(*mark["turned"])
                        for t in range(2):
                            for g in range(4):
                                mm = nc.tensor.matmul(bank[3 + 2 * t + g // 2][:, 256 * (g % 2):256 * (g % 2) + 256], p32T[:, t, g],
                                                      vblk[:, g].rearrange("p h d -> p (h d)"), start=True, stop=True)
                                if g % 2:
                                    mm.then_inc(*pe_done.one())

            with ExitStack() as st2:
                s = sb("s", [128, 2, 4, LP], ctx=st2)
                pt = sb("pt", [128, 2, 4, 2, 128], ctx=st2)
                stt = sb("stt", [128, 3, 3, 4], ctx=st2)
                ot = sb("ot", [128, 4, 64], ctx=st2)
                units = [(br, t, g) for br in range(2) for t in range(2) for g in range(4)]
                n = len(units)
                s_filled, s_ready, p_ready = count("s_filled"), count("s_ready"), count("p_ready")
                pt_filled, pt_copied, o_filled, o_added = count("pt_filled"), count("pt_copied"), count("o_filled"), count("o_added")
                with core.block() as block:
                    @block.sync
                    def _(sp):
                        sp.dma_start(O["win_old"], I["win_rows"][:, 1:512]).then_inc(*out_sent.one())

                    @block.tensor
                    def _(pe):
                        for u in range(n + 2):
                            if u < n:
                                br, t, g = units[u]
                                p, rows = g // 2, slice(64 * (g % 2), 64 * (g % 2) + 64)
                                if u >= 2:
                                    pe.wait_ge(*s_ready.at(u - 1))
                                for h in range(4):
                                    mm = nc.tensor.matmul(bank[2 * (u % 2) + h // 2][:, 256 * (h % 2):256 * (h % 2) + 128 * (t + 1)],
                                                          qR[rows, t, 4 * p + h], kvT[rows, 4 + 4 * br + p, 0:128 * (t + 1)], start=True, stop=True)
                                mm.then_inc(*s_filled.one())
                            if 1 <= u <= n:
                                br, t, g = units[u - 1]
                                pe.wait_ge(*p_ready.at(u))
                                if u >= 2:
                                    pe.wait_ge(*pt_copied.at(u - 1))
                                for h in range(4):
                                    for k in range(t + 1):
                                        o = 256 * (h % 2) + 128 * k
                                        mm = nc.tensor.transpose(bank[4 + h // 2][:, o:o + 128], s[:, (u - 1) % 2, h, 128 * k:128 * k + 128], ident)
                                mm.then_inc(*pt_filled.one())
                            if u >= 2:
                                w = u - 2
                                br, t, g = units[w]
                                pe.wait_ge(*pt_copied.at(w + 1))
                                if w >= 2:
                                    pe.wait_ge(*o_added.at(w - 1))
                                for h in range(4):
                                    for k in range(t + 1):
                                        mm = nc.tensor.matmul(bank[6 + w % 2][:, 64 * h:64 * h + 64], pt[:, w % 2, h, k], vn[:, br, k, 64 * g:64 * g + 64],
                                                              start=(k == 0), stop=(k == t))
                                mm.then_inc(*o_filled.one())

                    @block.scalar
                    def _(act):
                        for u in range(n + 1):
                            if u >= 1:
                                br, t, g = units[u - 1]
                                act.wait_ge(*pt_filled.at(u))
                                if u >= 3:
                                    act.wait_ge(*o_filled.at(u - 2))
                                for i in range(2):
                                    src = bank[4 + i][:].rearrange("p (h k q) -> p h k q", h=2, k=2)[:, :, 0:t + 1]
                                    ins = nc.scalar.copy(pt[:, (u - 1) % 2, 2 * i:2 * i + 2, 0:t + 1], src)
                                ins.then_inc(*pt_copied.one())
                            if u < n:
                                act.wait_ge(*s_ready.at(u + 1))
                                seen = 128 * (units[u][1] + 1)
                                for h in range(4):
                                    sh = s[:, u % 2, h, 0:seen]
                                    ins = nc.scalar.activation(sh, sh, ACT.Exp, bias=stt[:, u % 3, 0, h:h + 1], accum_out=stt[:, u % 3, 1, h:h + 1])
                                ins.then_inc(*p_ready.one())

                    @block.vector
                    def _(dve):
                        link = linker(dve, dve_done)
                        for u in range(n + 2):
                            if u < n:
                                br, t, g = units[u]
                                seen = 128 * (t + 1)
                                hd0 = 8 * (g // 2) + g % 2
                                dve.wait_ge(*s_filled.at(u + 1))
                                if u >= 2:
                                    dve.wait_ge(*pt_filled.at(u - 1))
                                for i in range(2):
                                    add = V.tensor_tensor(s[:, u % 2, 2 * i:2 * i + 2, 0:seen], bank[2 * (u % 2) + i][:].rearrange("p (h k) -> p h k", h=2)[:, :, 0:seen],
                                                          bias[:, t, hd0 + 4 * i:hd0 + 4 * i + 3:2, 0:seen], ALU.add)
                                link(add)
                                link(V.tensor_reduce(stt[:, u % 3, 0], s[:, u % 2, :, 0:seen], AX.X, ALU.max))
                                V.tensor_scalar(stt[:, u % 3, 0], stt[:, u % 3, 0], -1.0, None, ALU.mult).then_inc(*s_ready.one())
                            if u >= 2:
                                w = u - 2
                                br, t, g = units[w]
                                b = w % 3
                                hd0 = 8 * (g // 2) + g % 2
                                dve.wait_ge(*p_ready.at(w + 1))
                                link(V.reciprocal(stt[:, b, 2], stt[:, b, 1]))
                                link(V.tensor_tensor(stt[:, b, 2], stt[:, b, 2], gate[:, t, 16 + 16 * br + hd0:16 + 16 * br + hd0 + 7:2], ALU.mult))
                                dve.wait_ge(*o_filled.at(w + 1))
                                link(V.tensor_tensor(ot[:], bank[6 + w % 2][:, 0:256].rearrange("p (h d) -> p h d", h=4),
                                                     stt[:, b, 2].rearrange("p (h o) -> p h o", o=1).to_broadcast([128, 4, 64]), ALU.mult))
                                o = oacc[:, t].rearrange("p (a h b d) -> p a b h d", a=2, h=4, b=2)[:, g // 2, g % 2]
                                V.tensor_tensor(o, o, ot[:], ALU.add).then_inc(*o_added.one())
                                dve.wait_ge(*o_added.now())
            with core.block() as block:
                @block.sync
                def _(sp):
                    sp.wait_ge(*out_sent.now())

                @block.tensor
                def _(pe):
                    for t in range(2):
                        for c in range(8):
                            mm = nc.tensor.transpose(bank[2 * t + c // 4][:, 128 * (c % 4):128 * (c % 4) + 128], oacc[:, t, 128 * c:128 * c + 128], ident)
                            if c % 4 == 3:
                                mm.then_inc(*pe_done.one())

                @block.vector
                def _(dve):
                    for k in range(4):
                        dve.wait_ge(*pe_done.at(k + 1))
                        V.tensor_copy(uT[:, 4 * (k % 2):4 * (k % 2) + 4, 128 * (k // 2):128 * (k // 2) + 128],
                                      bank[k][:].rearrange("p (c q) -> p c q", c=4)[:, :, 127::-1]).then_inc(*dve_done.one())
        env["project"](uT, KT, D, env["nothing"], env["add_residual"])


def hgrn_layer(env):
    (nc, core, I, O, W, cst, par, xT, uT, eps, scratch, linker, ident, ones, lb) = (
        env[k] for k in ("nc", "core", "I", "O", "W", "cst", "par", "xT", "uT", "eps", "scratch", "linker", "ident", "ones", "lb"))
    count, bank = core.count, core.bank
    pe_done, act_done, dve_done = (count(n) for n in ("pe_done", "act_done", "dve_done"))
    misc, out_sent, pool_sent = count("misc_dma", 16), count("out_sent", 16), count("pool_sent", 16)
    state_in, state_out = [count(f"state_in{b}", 16) for b in range(HBS)], [count(f"state_out{b}", 16) for b in range(HBS)]
    V = nc.vector
    with ExitStack() as layer:
        def sb(name, shape, dt=F32, ctx=layer):
            return core.sb("h_" + name, shape, dt, ctx)

        qT, fT, vT, gT = (sb(n, [128, HH, T]) for n in ("qT", "fT", "vT", "gT"))
        oT = uT

        def act_step(act, t, ps):
            dst, f = ((qT, ACT.Silu), (fT, ACT.Sigmoid), (vT, ACT.Copy), (gT, ACT.Silu))[t // 8]
            return nc.scalar.activation(dst[:, t % 8], ps[:, 0:T], f)

        env["project"](uT, KT, 4096, act_step, lambda eng, t, ps: None)
        with core.block() as block:
            @block.vector
            def _(dve):
                for h in range(HH):
                    V.tensor_scalar(fT[:, h], fT[:, h], lb[:, 8 + h:9 + h], lb[:, h:h + 1], ALU.mult, ALU.add).then_inc(*dve_done.one())

        with ExitStack() as st:
            ke, kd = sb("ke", [128, HH, LP], ctx=st), sb("kd", [128, HH, LP], ctx=st)
            dec = sb("dec", [128, HH, NHC], ctx=st)
            vn, kdn = sb("vn", [128, 2, D], ctx=st), sb("kdn", [128, 2, D], ctx=st)
            with ExitStack() as st2:
                ac, ex = sb("ac", [128, HH, LP], ctx=st2), sb("ex", [128, HH, LP], ctx=st2)
                mark = {}

                def chunks(t):
                    return t[:].rearrange("p h (c t) -> p (h c) t", t=HC)
                with core.block() as block:
                    @block.vector
                    def _(dve):
                        link = linker(dve, dve_done)
                        dve.wait_ge(*act_done.at(1))
                        for h in range(HH):
                            V.tensor_tensor_scan(ac[:, h], cst("scan_keep"), ex[:, h], 0.0, ALU.mult, ALU.add).then_inc(*dve_done.one())
                        dve.wait_ge(*dve_done.now())
                        mark["ac"] = dve_done.now()
                        dve.wait_ge(*act_done.at(2))
                        q = qT[:, :, 0:LP]
                        link(V.tensor_tensor(q, q, ex[:], ALU.mult))
                        mark["qe"] = dve_done.now()
                        link(V.tensor_scalar(kd[:], fT[:, :, 0:LP], -1.0, 1.0, ALU.mult, ALU.add))
                        dve.wait_ge(*act_done.at(3))
                        link(V.tensor_tensor(ke[:], kd[:], ex[:], ALU.mult))
                        dve.wait_ge(*act_done.at(4))
                        a = chunks(ac)
                        link(V.tensor_tensor(a, a[:, :, HC - 1:HC].to_broadcast([128, HH * NHC, HC]), a, ALU.subtract))
                        mark["to end"] = dve_done.now()
                        dve.wait_ge(*act_done.at(5))
                        link(V.tensor_tensor(kd[:], kd[:], ex[:], ALU.mult))

                    @block.scalar
                    def _(act):
                        nc.scalar.activation(ex[:], fT[:, :, 0:LP], ACT.Ln).then_inc(*act_done.one())
                        act.wait_ge(*mark["ac"])
                        nc.scalar.activation(ex[:], ac[:], ACT.Exp).then_inc(*act_done.one())
                        act.wait_ge(*mark["qe"])
                        nc.scalar.activation(ex[:], ac[:], ACT.Exp, scale=-1.0).then_inc(*act_done.one())
                        nc.scalar.activation(dec[:], ac[:].rearrange("p h (c t) -> p h c t", t=HC)[:, :, :, HC - 1], ACT.Exp).then_inc(*act_done.one())
                        act.wait_ge(*mark["to end"])
                        nc.scalar.activation(ex[:], ac[:], ACT.Exp).then_inc(*act_done.one())
            att = sb("att", [128, 2, HH, 128], ctx=st)
            states = sb("states", [128, NHC + 1, HH, 128], ctx=st)
            mark = {}
            with core.block() as block:
                @block.tensor
                def _(pe):
                    for k, src in ((0, vT), (1, kd)):
                        for t in range(2):
                            for q in range(2):
                                for i in range(4):
                                    mm = nc.tensor.transpose(bank[4 * k + 2 * t + q][:, 128 * i:128 * i + 128], src[:, 4 * q + i, 128 * t:128 * t + 128], ident)
                                mm.then_inc(*pe_done.one())
                    for t in range(2):
                        for q in range(2):
                            pe.wait_ge(*act_done.at(2 * t + q + 1))
                            for i in range(4):
                                h = 4 * q + i
                                mm = nc.tensor.matmul(bank[2 * t + q][:, 128 * i:128 * i + 128], ke[:, h, 128 * t:128 * t + 128],
                                                      qT[:, h, 128 * t:128 * t + 128], start=True, stop=True)
                            mm.then_inc(*pe_done.one())

                @block.scalar
                def _(act):
                    for k in range(4):
                        act.wait_ge(*pe_done.at(k + 1))
                        nc.scalar.copy(vn[:, k // 2, 512 * (k % 2):512 * (k % 2) + 512], bank[k][:]).then_inc(*act_done.one())

                @block.vector
                def _(dve):
                    V.memset(att[:], 0.0).then_inc(*dve_done.one())
                    V.memset(states[:, 0], 0.0).then_inc(*dve_done.one())
                    for k in range(4):
                        dve.wait_ge(*pe_done.at(k + 5))
                        V.tensor_copy(kdn[:, k // 2, 512 * (k % 2):512 * (k % 2) + 512], bank[4 + k][:]).then_inc(*dve_done.one())
                    dve.wait_ge(*dve_done.now())
                    m = cst("att_mask").bitcast(U32).rearrange("p (o t) -> p o t", o=1).to_broadcast([128, 4, 128])
                    for k in range(4):
                        dve.wait_ge(*pe_done.at(k + 9))
                        V.copy_predicated(att[:, k // 2, 4 * (k % 2):4 * (k % 2) + 4], m, bank[k][:].rearrange("p (h t) -> p h t", h=4)) \
                            .then_inc(*dve_done.one())

            with core.block() as block:
                @block.tensor
                def _(pe):
                    for c in range(NHC):
                        rows, t, r = slice(32 * (c % 4), 32 * (c % 4) + 32), c // 4, c % 4
                        if c >= 4:
                            pe.wait_ge(*dve_done.at(3 * (c - 4) + 3))
                        for h in range(HH):
                            o = 128 * (h % 4)
                            mm = nc.tensor.matmul(bank[2 * r + h // 4][:, o:o + 128], kdn[rows, t, 128 * h:128 * h + 128],
                                                  vn[rows, t, 128 * h:128 * h + 128], start=True, stop=True, tile_position=(32 * r, 0))
                        mm.then_inc(*pe_done.one())

                @block.vector
                def _(dve):
                    link = linker(dve, dve_done)
                    for c in range(NHC):
                        new = states[:, c + 1]
                        link(V.tensor_tensor(new, states[:, c], dec[:, :, c:c + 1].to_broadcast([128, HH, 128]), ALU.mult))
                        dve.wait_ge(*pe_done.at(c + 1))
                        for q in range(2):
                            part = new[:, 4 * q:4 * q + 4]
                            V.tensor_tensor(part, part, bank[2 * (c % 4) + q][:].rearrange("p (h v) -> p h v", h=4), ALU.add).then_inc(*dve_done.one())
                        dve.wait_ge(*dve_done.now())
            with core.block() as block:
                @block.sync
                def _(sp):
                    sp.dma_start(O["hgrn_p"], states[:, NHC]).then_inc(*out_sent.one())
                    sp.wait_ge(*out_sent.now())

                @block.tensor
                def _(pe):
                    for h in range(HH):
                        o = LP * (h % 2)
                        for t in range(2):
                            mm = nc.tensor.matmul(bank[h // 2][:, o + 128 * t:o + 128 * t + 128], vn[:, t, 128 * h:128 * h + 128], att[:, t, h],
                                                  start=True, stop=False, skip_group_check=True)
                            for c in range(4 * t, 4 * t + 4):
                                mm = nc.tensor.matmul(bank[h // 2][:, o + HC * c:o + HC * c + HC], states[:, c, h], qT[:, h, HC * c:HC * c + HC],
                                                      start=False, stop=True, skip_group_check=True)
                        if h % 2:
                            mm.then_inc(*pe_done.one())

                @block.scalar
                def _(act):
                    for k in range(4):
                        act.wait_ge(*pe_done.at(k + 1))
                        nc.scalar.copy(oT[:, 2 * k:2 * k + 2, 0:LP], bank[k][:].rearrange("p (h t) -> p h t", h=2)).then_inc(*act_done.one())

        with ExitStack() as st:
            kS = sb("kS", [128, HH, NB], ctx=st)
            vnat = sb("vnat", [NB, D], ctx=st)
            vb = sb("vb", [128, NB, D], ctx=st)
            sbuf = sb("state", [128, HBS, HH, 128], ctx=st)
            tmp = sb("tmp", [128, HH, 128], ctx=st)
            d_v = scratch("scr_v", [NB, D])
            with core.block() as block:
                @block.tensor
                def _(pe):
                    for h in range(HH):
                        mm = nc.tensor.transpose(bank[h // 4][0:NB, 128 * (h % 4):128 * (h % 4) + 128], vT[:, h, LP:T], ident)
                    mm.then_inc(*pe_done.one())

                @block.vector
                def _(dve):
                    V.tensor_scalar(kS[:], fT[:, :, LP:T], -1.0, 1.0, ALU.mult, ALU.add).then_inc(*dve_done.one())
                    dve.wait_ge(*pe_done.at(1))
                    for k in range(2):
                        V.tensor_copy(vnat[:, 512 * k:512 * k + 512], bank[k][0:NB, :]).then_inc(*dve_done.one())

                @block.gpsimd
                def _(pool):
                    pool.wait_ge(*dve_done.at(3))
                    pool.dma_start(d_v, vnat[:]).then_inc(*pool_sent.one())
                    pool.wait_ge(*pool_sent.now())
                    pool.dma_start(vb[:], d_v.rearrange("(o b) c -> o b c", o=1).to_broadcast([128, NB, D])).then_inc(*misc.one())
                    pool.wait_ge(*misc.now())
            with core.block() as block:
                @block.scalar
                def _(act):
                    for b in range(NB):
                        if b >= HBS:
                            act.wait_ge(*state_out[b % HBS].at(b // HBS))
                            act.wait_ge(*pe_done.at(b - HBS + 1))
                        act.dma_start(sbuf[:, b % HBS], I["hgrn0"][:, b]).then_inc(*state_in[b % HBS].one())
                    act.wait_ge(*pe_done.at(NB))
                    nc.scalar.copy(oT[:, :, LP:T], bank[0][:, 0:64].rearrange("p (h b) -> p h b", h=HH)).then_inc(*act_done.one())

                @block.sync
                def _(sp):
                    for b in range(NB):
                        sp.wait_ge(*dve_done.at(3 * (b + 1)))
                        sp.dma_start(O["hgrn_s"][:, b], sbuf[:, b % HBS]).then_inc(*state_out[b % HBS].one())
                    for k in range(HBS):
                        sp.wait_ge(*state_out[k].now())

                @block.vector
                def _(dve):
                    link = linker(dve, dve_done)
                    for b in range(NB):
                        s = sbuf[:, b % HBS]
                        dve.wait_ge(*state_in[b % HBS].at(b // HBS + 1))
                        link(V.tensor_tensor(s, s, fT[:, :, LP + b:LP + b + 1].to_broadcast([128, HH, 128]), ALU.mult))
                        link(V.tensor_tensor(tmp[:], vb[:, b].rearrange("p (h v) -> p h v", h=HH), kS[:, :, b:b + 1].to_broadcast([128, HH, 128]), ALU.mult))
                        link(V.tensor_tensor(s, s, tmp[:], ALU.add))

                @block.tensor
                def _(pe):
                    for b in range(NB):
                        pe.wait_ge(*dve_done.at(3 * (b + 1)))
                        for h in range(HH):
                            mm = nc.tensor.matmul(bank[0][:, NB * h + b:NB * h + b + 1], sbuf[:, b % HBS, h], qT[:, h, LP + b:LP + b + 1], start=True, stop=True)
                        mm.then_inc(*pe_done.one())
        env["norm_each"]([(oT[:, h], oT[:, h], par("h_norm_g"), 1 / 128, eps[:, 0:1]) for h in range(HH)], ones, "hn")
        with core.block() as block:
            @block.vector
            def _(dve):
                V.tensor_tensor(oT[:], oT[:], gT[:], ALU.mult).then_inc(*dve_done.one())
        env["project"](oT, KT, D, env["nothing"], env["add_residual"])


def pack_params(x):
    def cols(a):
        return a.reshape(-1, 128).T
    rep = lambda a: np.tile(a, 128 // a.shape[0])[:, None]
    pad = lambda a: np.concatenate([a, np.zeros((128 - a.shape[0],), a.dtype)])[:, None]
    cw = x["m_conv_w"].reshape(2, 4, NCH, 128).transpose(0, 2, 1, 3).reshape(-1, 128).T
    pe = x["n_cmp_pe"][0].reshape(2, 2, 8, 128).transpose(3, 0, 1, 2).reshape(128, 32)
    moe_b = np.concatenate([x["moe_b_rg"], x["moe_b_re"]], axis=1).reshape(1, 80)
    parts = [cols(x["norm_g"]), cw, cols(x["m_conv_b"]), cols(x["m_norm_g"]), cols(np.repeat(x["m_d"], 64, axis=1)),
             pad(x["m_a_log"][0]), pad(x["m_a_log"][1]), pad(x["m_dt_bias"][0]), pad(x["m_dt_bias"][1]), rep(x["n_q_g"][0]),
             rep(x["n_k_g"][0, 0]), rep(x["n_k_g"][0, 1]), rep(x["n_k_g"][0, 2]), cols(x["h_lb"]), x["h_norm_g"][0][:, None],
             pe, np.broadcast_to(moe_b, (128, 80))]
    return np.concatenate(parts, axis=1)


def lay_out(x):
    f = {}
    f["consts"] = constants()[0]
    f["onehots"] = bucket_onehots()
    f["params"] = pack_params(x)
    xx = np.concatenate([x["x_prompt"][0], x["x_sample"][:, 0]], axis=0)
    f["xT"] = xx.T.reshape(KT, 128, T).transpose(1, 0, 2)
    chunk = lambda w: w.reshape(w.shape[:-2] + (-1, 128, w.shape[-1]))
    f["m_w_in"] = x["m_w_in"]
    f["w_dt"] = chunk(x["m_w_in"][:, :, 5120:]).transpose(2, 0, 1, 3)
    f["m_w_out"] = x["m_w_out"]
    f["conv0"] = x["state_conv"].reshape(2, NB, 3, NCH, 128).transpose(0, 4, 3, 2, 1)
    f["ssm0"] = x["state_ssm"].reshape(2, NB, CI, 128, 128).transpose(0, 3, 2, 1, 4)
    def heads(w):
        return w.reshape(w.shape[:-1] + (2, 2, 4, 64)).swapaxes(-3, -2).reshape(w.shape)
    w = x["n_w_in"][0]
    f["n_w_in"] = np.concatenate([heads(w[:, :1024]), w[:, 1024:2560]], axis=1)
    gl = w[:, 2560:].reshape(D, 2, 2, 4, 3).transpose(0, 4, 1, 3, 2).reshape(D, 48)
    f["w_gl"] = chunk(gl).transpose(1, 0, 2)
    f["n_w_out"] = heads(x["n_w_out"][0].T).T
    f["rel"] = x["rel_table"].reshape(32, 2, 2, 4).swapaxes(-2, -1).reshape(32, 16)
    f["cmp_w1"] = x["n_cmp_w1"][0].reshape(2, 2, 8, 128, 64).transpose(3, 0, 2, 1, 4)
    f["cmp_w1d"] = np.tile(x["n_cmp_w1"][0].reshape(2, 32, 64, 64).transpose(2, 0, 1, 3), (2, 1, 1, 1))
    f["cmp_w2"] = x["n_cmp_w2"][0].transpose(1, 0, 2)
    n_pool = x["cache_kv_cmp"].shape[1]
    c = x["cache_kv_cmp"][0].reshape(n_pool, 8, 8, 2, 2, 4, 64)
    f["cache_cmp"] = c.transpose(0, 3, 6, 4, 2, 5, 1).reshape(n_pool, 128, 512)

    def kv_page(c):
        k = c[..., 0, :, :].reshape(c.shape[:-4] + (128, 2, 128))
        k = np.swapaxes(k, -3, -1)
        k = k.reshape(c.shape[:-4] + (128, 256))
        return np.concatenate([k, c[..., 1, :, :].reshape(c.shape[:-4] + (128, 256))], axis=-1)
    f["cache_sel"] = kv_page(x["cache_kv_sel"][0])
    win = x["cache_kv_win"][0]
    f["cache_win"] = kv_page(win.reshape(NB, 4, 128, 2, 4, 64)).transpose(0, 2, 1, 3)
    f["win_rows"] = win.reshape(NB, 512, 512)
    f["pages"] = x["page_table"].reshape(1, 64)
    f["h_w_in"], f["h_w_out"] = x["h_w_in"][0], x["h_w_out"][0]
    f["hgrn0"] = x["state_hgrn"][0].transpose(2, 0, 1, 3)
    f["w_rt"] = chunk(np.concatenate([x["moe_w_rg"], x["moe_w_re"]], axis=2)).transpose(2, 0, 1, 3)
    for k in ("moe_w1", "moe_w3", "moe_w2"):
        f[k] = x[k]
    return {k: np.ascontiguousarray(v) for k, v in f.items()}


OUTS = {"yT": (128, KT, T), "conv_tail": (2, 128, NCH, 11), "conv_keep": (2, 128, NCH, 2, NB), "ssm_p": (2, 128, DI),
        "ssm_s": (2, 128, CI, NB, 128), "kvT": (128, 12, T), "win_old": (NB, 511, 512), "hgrn_p": (128, HH, 128),
        "hgrn_s": (128, NB, HH, 128)}


def give_back(r):
    y = r["yT"].transpose(2, 1, 0).reshape(T, D)
    tail = r["conv_tail"].transpose(0, 3, 2, 1).reshape(2, 11, NCH * 128)
    conv_p = tail[:, None, 0:3]
    keep = r["conv_keep"].transpose(0, 4, 3, 2, 1).reshape(2, NB, 2, NCH * 128)
    conv_s = np.concatenate([keep, tail[:, 3:, None]], axis=2)
    ssm_p = r["ssm_p"].reshape(2, 1, 128, MH, 64).transpose(0, 1, 3, 4, 2)
    ssm_s = r["ssm_s"].transpose(0, 3, 2, 1, 4).reshape(2, NB, MH, 64, 128)
    kv = r["kvT"].transpose(2, 1, 0).reshape(T, 3, 2, 4, 64)
    new = [kv[:LP, b][None, None] for b in range(3)]
    dec = [kv[LP:, b][None, :, None] for b in range(3)]
    win_s = np.concatenate([r["win_old"].reshape(1, NB, 511, 2, 4, 64), dec[2]], axis=2)
    hg_p = r["hgrn_p"].transpose(1, 0, 2)[None, None]
    hg_s = r["hgrn_s"].transpose(1, 2, 0, 3)[None]
    outs = (y[None, :LP], y[LP:, None], ssm_p, conv_p, new[0], new[1], new[2], hg_p, ssm_s, conv_s, dec[0], dec[1], win_s, hg_s)
    return tuple(np.ascontiguousarray(o) for o in outs)


def kernel(**inputs):
    import concourse.bacc as bacc
    from concourse.bass_utils import run_bass_kernel_spmd

    nc = bacc.Bacc("TRN2", target_bir_lowering=False, num_devices=1)
    arrays = lay_out({k: np.asarray(v) for k, v in inputs.items()})
    I = {k: nc.dram_tensor("in_" + k, a.shape, mybir.dt.from_np(a.dtype), kind="ExternalInput").ap() for k, a in arrays.items()}
    O = {k: nc.dram_tensor("out_" + k, s, F32, kind="ExternalOutput").ap() for k, s in OUTS.items()}
    build(nc, I, O)
    r = run_bass_kernel_spmd(nc, [{"in_" + k: a for k, a in arrays.items()}], core_ids=[0])
    return give_back({k: r.results[0]["out_" + k] for k in OUTS})
```
